# Optimizing a Trainium2 kernel written in Bass

```python
import math
import jax, jax.numpy as jnp
from jax import lax
import numpy as np

D_MODEL = 1024
BATCH = 1
SEQ = 512
DEPTH = 1

N_META = 16
GDN_HEADS = D_MODEL // 256
GDN_DK = 128
GDN_DV = 128
FOX_HEADS = D_MODEL // 128
FOX_DH = 64
D_MIX = GDN_HEADS * GDN_DV + FOX_HEADS * FOX_DH
CONV_K = 4
CHUNK = 64
BLOCK_Q = 128
D_FF = -(-8 * D_MODEL // (3 * 256)) * 256
EPS = 1e-6
MASK_VALUE = -1e30
GDN_QKV = 2 * GDN_HEADS * GDN_DK + GDN_HEADS * GDN_DV
IN_SIZES = (GDN_HEADS * GDN_DK, GDN_HEADS * GDN_DK, GDN_HEADS * GDN_DV, GDN_HEADS * GDN_DV,
            GDN_HEADS, GDN_HEADS,
            FOX_HEADS * FOX_DH, FOX_HEADS * FOX_DH, FOX_HEADS * FOX_DH, FOX_HEADS)
D_IN = sum(IN_SIZES)
IN_SPLITS = tuple(int(s) for s in np.cumsum(IN_SIZES)[:-1])


def rmsnorm(x, w):
    x32 = x.astype(jnp.float32)
    y = x32 * lax.rsqrt(jnp.mean(x32 * x32, axis=-1, keepdims=True) + EPS)
    return (y * w.astype(jnp.float32)).astype(x.dtype)

def l2norm(x):
    return x * lax.rsqrt(jnp.sum(x * x, axis=-1, keepdims=True) + EPS)

def causal_dwconv(x, w):
    k = w.shape[0]
    return lax.conv_general_dilated(x, w[:, None, :], window_strides=(1,), padding=[(k - 1, 0)],
                                    dimension_numbers=("NWC", "WIO", "NWC"),
                                    feature_group_count=x.shape[-1])

def chunk_gated_delta_rule(q, k, v, beta, g, s0, chunk):
    b, h, t, _ = q.shape
    dv = v.shape[-1]
    n = t // chunk
    q, k, v = (a.reshape(b, h, n, chunk, a.shape[-1]) for a in (q, k, v))
    beta = beta.reshape(b, h, n, chunk)
    gc = jnp.cumsum(g.reshape(b, h, n, chunk), axis=-1)
    incl = jnp.tril(jnp.ones((chunk, chunk), dtype=bool))
    strict = jnp.tril(jnp.ones((chunk, chunk), dtype=bool), -1)
    diff = gc[..., :, None] - gc[..., None, :]
    decay = jnp.where(incl, jnp.exp(jnp.where(incl, diff, 0.0)), 0.0)
    a_mat = jnp.where(strict, jnp.einsum("bhncd,bhnsd->bhncs", k, k) * decay * beta[..., :, None], 0.0)
    rhs = jnp.concatenate([v * beta[..., None], k * (beta * jnp.exp(gc))[..., None]], axis=-1)
    sol = lax.linalg.triangular_solve(a_mat + jnp.eye(chunk, dtype=a_mat.dtype), rhs,
                                      left_side=True, lower=True, unit_diagonal=True)
    u, w = sol[..., :dv], sol[..., dv:]
    qk = jnp.einsum("bhncd,bhnsd->bhncs", q, k) * decay
    xs = tuple(jnp.moveaxis(a, 2, 0) for a in (q, k, u, w, gc, qk))

    def step(state, inp):
        q_c, k_c, u_c, w_c, g_c, qk_c = inp
        v_new = u_c - jnp.einsum("bhcd,bhde->bhce", w_c, state)
        o_c = (jnp.einsum("bhcd,bhde->bhce", q_c * jnp.exp(g_c)[..., None], state)
               + jnp.einsum("bhcs,bhse->bhce", qk_c, v_new))
        g_last = g_c[..., -1:]
        state = (state * jnp.exp(g_last)[..., None]
                 + jnp.einsum("bhcd,bhce->bhde", k_c * jnp.exp(g_last - g_c)[..., None], v_new))
        return state, o_c

    s_final, o = lax.scan(step, s0, xs)
    o = jnp.moveaxis(o, 0, 2).reshape(b, h, t, dv)
    return o, s_final

def gated_deltanet_group(qkv, z, b_raw, a_raw, conv_w, a_log, dt_bias, norm_w):
    bsz, t, _ = qkv.shape
    f32 = jnp.float32
    qkv = jax.nn.silu(causal_dwconv(qkv, conv_w)).astype(f32)
    q, k, v = jnp.split(qkv, [GDN_HEADS * GDN_DK, 2 * GDN_HEADS * GDN_DK], axis=-1)
    q = l2norm(q.reshape(bsz, t, GDN_HEADS, GDN_DK)).transpose(0, 2, 1, 3) * (GDN_DK ** -0.5)
    k = l2norm(k.reshape(bsz, t, GDN_HEADS, GDN_DK)).transpose(0, 2, 1, 3)
    v = v.reshape(bsz, t, GDN_HEADS, GDN_DV).transpose(0, 2, 1, 3)
    beta = jax.nn.sigmoid(b_raw.astype(f32)).transpose(0, 2, 1)
    g = (-jnp.exp(a_log.astype(f32))
         * jax.nn.softplus(a_raw.astype(f32) + dt_bias.astype(f32))).transpose(0, 2, 1)
    s0 = jnp.zeros((bsz, GDN_HEADS, GDN_DK, GDN_DV), f32)
    o_meta, s_meta = chunk_gated_delta_rule(q[:, :, :N_META], k[:, :, :N_META], v[:, :, :N_META],
                                            beta[:, :, :N_META], g[:, :, :N_META], s0, N_META)
    o_real, _ = chunk_gated_delta_rule(q[:, :, N_META:], k[:, :, N_META:], v[:, :, N_META:],
                                       beta[:, :, N_META:], g[:, :, N_META:], s_meta, CHUNK)
    o = jnp.concatenate([o_meta, o_real], axis=2).transpose(0, 2, 1, 3)
    zg = jax.nn.silu(z.astype(f32).reshape(bsz, t, GDN_HEADS, GDN_DV))
    o = o * lax.rsqrt(jnp.mean(o * o, axis=-1, keepdims=True) + EPS) * norm_w.astype(f32) * zg
    return o.reshape(bsz, t, GDN_HEADS * GDN_DV).astype(qkv.dtype)

def forgetting_attention_group(q, k, v, f_raw, f_bias):
    bsz, t, _ = q.shape
    f32 = jnp.float32
    q, k, v = (a.astype(f32).reshape(bsz, t, FOX_HEADS, FOX_DH) for a in (q, k, v))
    logf = jax.nn.log_sigmoid(f_raw.astype(f32) + f_bias.astype(f32))
    c = jnp.cumsum(logf, axis=1).transpose(0, 2, 1)
    scale = FOX_DH ** -0.5
    n_blocks = (t - N_META) // BLOCK_Q
    bounds = [0, N_META] + [N_META + (i + 1) * BLOCK_Q for i in range(n_blocks)]
    outs = []
    for s, e in zip(bounds[:-1], bounds[1:]):
        sc = (jnp.einsum("bqhd,bkhd->bhqk", q[:, s:e], k[:, :e]) * scale
              + c[:, :, s:e, None] - c[:, :, None, :e])
        causal = jnp.arange(s, e)[:, None] >= jnp.arange(e)[None, :]
        p = jax.nn.softmax(jnp.where(causal, sc, MASK_VALUE), axis=-1)
        outs.append(jnp.einsum("bhqk,bkhd->bqhd", p, v[:, :e]))
    return jnp.concatenate(outs, axis=1).reshape(bsz, t, FOX_HEADS * FOX_DH)

def swiglu(x, w_gate, w_up, w_down):
    return (jax.nn.silu(x @ w_gate) * (x @ w_up)) @ w_down

def first_inputs(seed: int = 0) -> dict:
    key = jax.random.key(seed)
    ks = jax.random.split(key, 15)
    nrm = jax.random.normal
    dt = jnp.exp(jax.random.uniform(ks[6], (DEPTH, GDN_HEADS), minval=math.log(1e-3), maxval=math.log(1e-1)))
    return {
        "x": nrm(ks[0], (BATCH, SEQ, D_MODEL), jnp.float32),
        "meta_tokens": nrm(ks[1], (N_META, D_MODEL), jnp.float32),
        "attn_norm_w": 1.0 + 0.02 * nrm(ks[2], (DEPTH, D_MODEL), jnp.float32),
        "w_in": nrm(ks[3], (DEPTH, D_MODEL, D_IN), jnp.float32) * D_MODEL ** -0.5,
        "conv_w": nrm(ks[4], (DEPTH, CONV_K, GDN_QKV), jnp.float32) * CONV_K ** -0.5,
        "a_log": jnp.log(jax.random.uniform(ks[5], (DEPTH, GDN_HEADS), minval=1.0, maxval=16.0)),
        "dt_bias": dt + jnp.log(-jnp.expm1(-dt)),
        "gdn_norm_w": 1.0 + 0.02 * nrm(ks[7], (DEPTH, GDN_DV), jnp.float32),
        "fgate_b": 2.0 + 0.5 * nrm(ks[8], (DEPTH, FOX_HEADS), jnp.float32),
        "w_out": nrm(ks[9], (DEPTH, D_MIX, D_MODEL), jnp.float32) * D_MIX ** -0.5,
        "ffn_norm_w": 1.0 + 0.02 * nrm(ks[10], (DEPTH, D_MODEL), jnp.float32),
        "w_gate": nrm(ks[11], (DEPTH, D_MODEL, D_FF), jnp.float32) * D_MODEL ** -0.5,
        "w_up": nrm(ks[12], (DEPTH, D_MODEL, D_FF), jnp.float32) * D_MODEL ** -0.5,
        "w_down": nrm(ks[13], (DEPTH, D_FF, D_MODEL), jnp.float32) * D_FF ** -0.5,
        "final_norm_w": 1.0 + 0.02 * nrm(ks[14], (D_MODEL,), jnp.float32),
    }

def first_block(x, meta_tokens, attn_norm_w, w_in, conv_w, a_log, dt_bias, gdn_norm_w, fgate_b,
              w_out, ffn_norm_w, w_gate, w_up, w_down, final_norm_w):
    bsz = x.shape[0]
    meta = jnp.broadcast_to(meta_tokens[None].astype(x.dtype), (bsz, N_META, D_MODEL))
    h = jnp.concatenate([meta, x], axis=1)
    for l in range(DEPTH):
        u = rmsnorm(h, attn_norm_w[l])
        proj = u @ w_in[l]
        gq, gk, gv, gz, gb, ga, fq, fk, fv, ff = jnp.split(proj, IN_SPLITS, axis=-1)
        o_gdn = gated_deltanet_group(jnp.concatenate([gq, gk, gv], axis=-1), gz, gb, ga,
                                     conv_w[l], a_log[l], dt_bias[l], gdn_norm_w[l])
        o_fox = forgetting_attention_group(fq, fk, fv, ff, fgate_b[l]).astype(h.dtype)
        h = h + jnp.concatenate([o_gdn, o_fox], axis=-1) @ w_out[l]
        h = h + swiglu(rmsnorm(h, ffn_norm_w[l]), w_gate[l], w_up[l], w_down[l])
    h = rmsnorm(h, final_norm_w)
    return h[:, N_META:]


HEAD_DIM = 64
N_Q_HEADS = 8
N_KV_HEADS = 2
Q_PER_KV = N_Q_HEADS // N_KV_HEADS
ATTN_WIDTH = N_Q_HEADS * HEAD_DIM
KV_WIDTH = N_KV_HEADS * HEAD_DIM
WINDOW = 128
ATTN_BLOCK = WINDOW
ROPE_THETA = 10000.0
CONV_WIDTH = D_MODEL - ATTN_WIDTH
CONV_K_2 = 3
IN_PROJ_WIDTH = ATTN_WIDTH + 2 * KV_WIDTH + 3 * CONV_WIDTH
SPLITS = (ATTN_WIDTH, ATTN_WIDTH + KV_WIDTH, ATTN_WIDTH + 2 * KV_WIDTH,
          ATTN_WIDTH + 2 * KV_WIDTH + CONV_WIDTH, ATTN_WIDTH + 2 * KV_WIDTH + 2 * CONV_WIDTH)
PEER_HEADS = 8
PEER_KEYS = 128
PEER_EXPERTS = PEER_KEYS * PEER_KEYS
PEER_TOPK = 16
PEER_QDIM = 256
PEER_HALF = PEER_QDIM // 2
PEER_CHUNK = 128
N_MOD = 6
NEG = -1e30


def rmsnorm_2(x, g):
    x32 = x.astype(jnp.float32)
    y = x32 * lax.rsqrt(jnp.mean(x32 * x32, axis=-1, keepdims=True) + EPS)
    return (y * g.astype(jnp.float32)).astype(x.dtype)

def modulate(h, shift, scale):
    return h * (1.0 + scale[:, None, :]) + shift[:, None, :]

def rope(t, cos, sin):
    t1, t2 = jnp.split(t.astype(jnp.float32), 2, axis=-1)
    out = jnp.concatenate([t1 * cos - t2 * sin, t2 * cos + t1 * sin], axis=-1)
    return out.astype(t.dtype)

def sliding_window_attention(q, k, v, sinks):
    B, S = q.shape[0], q.shape[1]
    nb = S // ATTN_BLOCK
    qb = q.reshape(B, nb, ATTN_BLOCK, N_KV_HEADS, Q_PER_KV, HEAD_DIM)

    def band(t):
        tb = t.reshape(B, nb, ATTN_BLOCK, N_KV_HEADS, HEAD_DIM)
        prev = jnp.pad(tb, ((0, 0), (1, 0), (0, 0), (0, 0), (0, 0)))[:, :-1]
        return jnp.concatenate([prev, tb], axis=2)

    kb, vb = band(k), band(v)
    s = jnp.einsum('bnqhgd,bnkhd->bnhgqk', qb, kb).astype(jnp.float32) * (HEAD_DIM ** -0.5)
    qi = jnp.arange(ATTN_BLOCK)[:, None]
    kj = jnp.arange(2 * ATTN_BLOCK)[None, :]
    dist = qi + ATTN_BLOCK - kj
    blk = jnp.arange(nb)[:, None, None]
    valid = (dist >= 0) & (dist < WINDOW) & (blk * ATTN_BLOCK - ATTN_BLOCK + kj >= 0)
    s = jnp.where(valid[None, :, None, None], s, NEG)
    sink = sinks.astype(jnp.float32).reshape(1, 1, N_KV_HEADS, Q_PER_KV, 1, 1)
    m = jnp.maximum(jnp.max(s, axis=-1, keepdims=True), sink)
    e = jnp.exp(s - m)
    p = e / (jnp.sum(e, axis=-1, keepdims=True) + jnp.exp(sink - m))
    o = jnp.einsum('bnhgqk,bnkhd->bnqhgd', p.astype(v.dtype), vb)
    return o.reshape(B, S, ATTN_WIDTH)

def short_conv(h, w):
    S = h.shape[1]
    hp = jnp.pad(h, ((0, 0), (CONV_K_2 - 1, 0), (0, 0)))
    y = w[0] * hp[:, 0:S]
    for k in range(1, CONV_K_2):
        y = y + w[k] * hp[:, k:k + S]
    return y

def peer(h, wq, subkeys, u_tab, v_tab):
    B, S, D = h.shape
    T = B * S
    xt = h.reshape(T, D)
    q = (xt @ wq).reshape(T, PEER_HEADS, 2, PEER_HALF)
    sc = jnp.einsum('thpd,hpkd->thpk', q, subkeys).astype(jnp.float32)
    vals, ids = lax.top_k(sc, PEER_TOPK)
    cand = (vals[:, :, 0, :, None] + vals[:, :, 1, None, :]).reshape(T, PEER_HEADS, PEER_TOPK * PEER_TOPK)
    cid = (ids[:, :, 0, :, None] * PEER_KEYS + ids[:, :, 1, None, :]).reshape(T, PEER_HEADS, PEER_TOPK * PEER_TOPK)
    top, pos = lax.top_k(cand, PEER_TOPK)
    idx = jnp.take_along_axis(cid, pos, axis=-1)
    g = jax.nn.softmax(top, axis=-1).astype(h.dtype)
    nc = T // PEER_CHUNK

    def expert_chunk(args):
        xc, ic, gc = args
        u = jnp.take(u_tab, ic, axis=0)
        a = jnp.einsum('chkd,cd->chk', u, xc)
        wgt = gc * jax.nn.gelu(a)
        vv = jnp.take(v_tab, ic, axis=0)
        return jnp.einsum('chk,chkd->cd', wgt, vv)

    out = lax.map(expert_chunk, (xt.reshape(nc, PEER_CHUNK, D),
                                 idx.reshape(nc, PEER_CHUNK, PEER_HEADS, PEER_TOPK),
                                 g.reshape(nc, PEER_CHUNK, PEER_HEADS, PEER_TOPK)))
    return out.reshape(B, S, D)

def second_inputs(seed: int = 0) -> dict:
    key = jax.random.key(seed)
    ks = jax.random.split(key, 20)
    f32 = jnp.float32
    D = D_MODEL

    def nrm(k, shape, scale):
        return jax.random.normal(k, shape, f32) * scale

    return {
        "x": nrm(ks[0], (BATCH, SEQ, D), 1.0),
        "c": nrm(ks[1], (BATCH, D), 1.0),
        "positions": jnp.broadcast_to(jnp.arange(SEQ, dtype=jnp.int32)[None, :], (BATCH, SEQ)),
        "ada_w": nrm(ks[2], (DEPTH, D, N_MOD * D), 0.5 * D ** -0.5),
        "ada_b": nrm(ks[3], (DEPTH, N_MOD * D), 0.02),
        "norm1_g": 1.0 + nrm(ks[4], (DEPTH, D), 0.02),
        "w_in": nrm(ks[5], (DEPTH, D, IN_PROJ_WIDTH), D ** -0.5),
        "q_norm_g": 1.0 + nrm(ks[6], (DEPTH, HEAD_DIM), 0.02),
        "k_norm_g": 1.0 + nrm(ks[7], (DEPTH, HEAD_DIM), 0.02),
        "sinks": nrm(ks[8], (DEPTH, N_Q_HEADS), 0.5),
        "conv_w": nrm(ks[9], (DEPTH, CONV_K_2, CONV_WIDTH), CONV_K_2 ** -0.5),
        "attn_out_g": 1.0 + nrm(ks[10], (DEPTH, ATTN_WIDTH), 0.02),
        "conv_out_g": 1.0 + nrm(ks[11], (DEPTH, CONV_WIDTH), 0.02),
        "w_out": nrm(ks[12], (DEPTH, D, D), D ** -0.5),
        "norm2_g": 1.0 + nrm(ks[13], (DEPTH, D), 0.02),
        "peer_wq": nrm(ks[14], (DEPTH, D, PEER_HEADS * PEER_QDIM), D ** -0.5),
        "peer_subkeys": nrm(ks[15], (DEPTH, PEER_HEADS, 2, PEER_KEYS, PEER_HALF), PEER_HALF ** -0.5),
        "peer_u": nrm(ks[16], (DEPTH, PEER_EXPERTS, D), D ** -0.5),
        "peer_v": nrm(ks[17], (DEPTH, PEER_EXPERTS, D), (PEER_HEADS * PEER_TOPK) ** -0.5),
    }

def second_block(x, c, positions, ada_w, ada_b, norm1_g, w_in, q_norm_g, k_norm_g, sinks, conv_w,
              attn_out_g, conv_out_g, w_out, norm2_g, peer_wq, peer_subkeys, peer_u, peer_v):
    B, S, _ = x.shape
    inv_freq = ROPE_THETA ** (-jnp.arange(0, HEAD_DIM, 2, dtype=jnp.float32) / HEAD_DIM)
    ang = positions.astype(jnp.float32)[..., None] * inv_freq
    cos = jnp.cos(ang)[:, :, None, :]
    sin = jnp.sin(ang)[:, :, None, :]
    c_act = jax.nn.silu(c)

    for l in range(DEPTH):
        mod = c_act @ ada_w[l] + ada_b[l]
        shift1, scale1, gate1, shift2, scale2, gate2 = jnp.split(mod, N_MOD, axis=-1)

        h = modulate(rmsnorm_2(x, norm1_g[l]), shift1, scale1)
        proj = h @ w_in[l]
        q, k, v, cb, cc, cu = jnp.split(proj, SPLITS, axis=-1)

        q = rope(rmsnorm_2(q.reshape(B, S, N_Q_HEADS, HEAD_DIM), q_norm_g[l]), cos, sin)
        k = rope(rmsnorm_2(k.reshape(B, S, N_KV_HEADS, HEAD_DIM), k_norm_g[l]), cos, sin)
        v = v.reshape(B, S, N_KV_HEADS, HEAD_DIM)
        attn = sliding_window_attention(q, k, v, sinks[l])

        conv = cb * short_conv(cc * cu, conv_w[l])

        merged = jnp.concatenate([rmsnorm_2(attn, attn_out_g[l]), rmsnorm_2(conv, conv_out_g[l])], axis=-1)
        x = x + gate1[:, None, :] * (merged @ w_out[l])

        h2 = modulate(rmsnorm_2(x, norm2_g[l]), shift2, scale2)
        x = x + gate2[:, None, :] * peer(h2, peer_wq[l], peer_subkeys[l], peer_u[l], peer_v[l])
    return x


def setup_inputs(seed=0):
    out = dict(first_inputs(seed))
    for name, value in second_inputs(seed + 1).items():
        if name != "x":
            out[name + "_2"] = value
    return out


def reference(
    x, meta_tokens, attn_norm_w, w_in, conv_w, a_log, dt_bias, gdn_norm_w, fgate_b, w_out,
    ffn_norm_w, w_gate, w_up, w_down, final_norm_w, c_2, positions_2, ada_w_2, ada_b_2,
    norm1_g_2, w_in_2, q_norm_g_2, k_norm_g_2, sinks_2, conv_w_2, attn_out_g_2, conv_out_g_2,
    w_out_2, norm2_g_2, peer_wq_2, peer_subkeys_2, peer_u_2, peer_v_2,
):
    x = first_block(
        x, meta_tokens, attn_norm_w, w_in, conv_w, a_log, dt_bias, gdn_norm_w, fgate_b, w_out,
        ffn_norm_w, w_gate, w_up, w_down, final_norm_w,
    )
    return second_block(
        x, c_2, positions_2, ada_w_2, ada_b_2, norm1_g_2, w_in_2, q_norm_g_2, k_norm_g_2,
        sinks_2, conv_w_2, attn_out_g_2, conv_out_g_2, w_out_2, norm2_g_2, peer_wq_2,
        peer_subkeys_2, peer_u_2, peer_v_2,
    )


_drawn_inputs = setup_inputs


def setup_inputs(seed=0):
    import zlib

    import numpy as np

    out = dict(_drawn_inputs(seed))
    spreads = {}
    factors = {'attn_norm_w': 3.241,
     'gdn_norm_w': 6.523,
     'ffn_norm_w': 4.155,
     'final_norm_w': 2.77,
     'norm1_g_2': 7.353,
     'q_norm_g_2': 8.0,
     'k_norm_g_2': 8.0,
     'sinks_2': 8.0,
     'attn_out_g_2': 8.0,
     'conv_out_g_2': 8.0,
     'norm2_g_2': 8.0,
     'peer_wq_2': 3.951,
     'peer_subkeys_2': 3.942,
     'peer_u_2': 4.378,
     'peer_v_2': 3.939}
    for name, (base, spread) in spreads.items():
        noise = np.random.default_rng([zlib.crc32(name.encode()), seed]).standard_normal(out[name].shape)
        drawn = base * np.exp(spread * noise) if base else spread * noise
        out[name] = __import__('jax').numpy.asarray(drawn.astype(out[name].dtype))
    for name, factor in factors.items():
        out[name] = (out[name] * factor).astype(out[name].dtype)
    return out
```

```python
from contextlib import ExitStack

import numpy as np
import concourse.bass as bass
from concourse import mybir

F32 = mybir.dt.float32
BF16 = mybir.dt.bfloat16
I32 = mybir.dt.int32
U32 = mybir.dt.uint32
ALU = mybir.AluOpType
ACT = mybir.ActivationFunctionType
AX = mybir.AxisListType.X

P = 128
D = 1024
DC = D // P
META = 16
SEQ = 512
T = META + SEQ
HALF = T // 2
NT = -(-T // P)
TP = NT * P
LAST = T - (NT - 1) * P
GH, GD = 4, 128
FH, FD = 8, 64
CONV_K = 4
FF = 2816
FC = FF // P
EPS = 1e-6
NEG = -1e30
LEVELS = 7
SLOT = 4096
ROW_B, ROW_A = 32, 64
NG = ROW_A + GH
SEC = 512
MODS = 6 * DC
AH, AD, KV = 8, 64, 2
PER = AH // KV
SC = SEC // P
CW = 512
CK2 = 3
PH, PK, TOP = 8, 128, 16
EB = 4
GROUPS = PK // EB
TWO_PI = 2 * np.pi
RING = 4
LOW = -3.0e38
SMALL = 14 + 13
F_MOD, F_OUT, F_GU, F_DOWN = 7, 19, 21, 32
F_Q2, F_KV2, F_CU2, F_CB2, F_OUT2, F_WQ = 40, 41, 42, 44, 45, 47


def constants():
    i = np.arange(P)
    parts = {}
    parts["ident"] = np.eye(P)
    parts["upto"] = (i[:, None] <= i[None, :])
    parts["after"] = (i[:, None] > i[None, :])
    parts["ones"] = np.ones((P, P))
    parts["mean_d"] = np.full((P, P), 1.0 / D)
    parts["mean_head"] = np.full((P, P), 1.0 / GD)
    parts["causal"] = np.where(i[:, None] >= i[None, :], 0.0, NEG)
    for lev in range(LEVELS):
        b = 1 << lev
        m = (i[:, None] // (2 * b) == i[None, :] // (2 * b)) & (i[:, None] % (2 * b) >= b) & (i[None, :] % (2 * b) < b)
        parts[f"merge{lev}"] = -m.astype(np.float64)
    pick = np.zeros((P, FH, P))
    for h in range(FH):
        pick[h, h, :] = 1.0
    same = i[:, None] // AD == i[None, :] // AD
    parts["mean_ah"] = same / AD
    parts["mean_mix"] = np.full((P, P), 1.0 / CW)
    lo = i % AD < AD // 2
    turn = np.zeros((P, P))
    for d in range(P):
        turn[d + AD // 2 if lo[d] else d - AD // 2, d] = -1.0 if lo[d] else 1.0
    parts["turn"] = turn
    j = np.arange(2 * P)
    seen = (j[None, :] > i[:, None]) & (j[None, :] <= i[:, None] + P)
    parts["window"] = np.where(seen, 0.0, NEG)
    parts["iota"] = np.tile(i[None, :], (P, 1))
    freq = (10000.0 ** (-np.arange(0, AD, 2, dtype=np.float32) / np.float32(AD))).astype(np.float32)
    parts["freq"] = np.tile(freq, P // freq.size)[:, None]
    parts["pick"] = pick.reshape(P, FH * P)
    return parts


def const_places():
    at, places = 0, {}
    for name, a in constants().items():
        places[name] = (at, a.shape[1])
        at += a.shape[1]
    return places, at


def program(nc, io):
    places, n_const = const_places()
    ctx = ExitStack()
    with ctx:
        def sem(name):
            return ctx.enter_context(nc.semaphore(name))

        cst = ctx.enter_context(nc.sbuf_tensor("cst", [P, n_const], F32))

        def const(name, rows=P):
            a, n = places[name]
            return cst[0:rows, a:a + n]

        arena_floats = 53200 - n_const - 64
        arena = ctx.enter_context(nc.sbuf_tensor("arena", [P, arena_floats], F32))
        top = [0]

        def carve(*dims):
            n = int(np.prod(dims))
            a = arena[:, top[0]:top[0] + n]
            top[0] += n
            assert top[0] <= arena_floats, (top[0], arena_floats)
            if len(dims) == 2:
                a = a.rearrange("p (a b) -> p a b", a=dims[0])
            if len(dims) == 3:
                a = a.rearrange("p (a b c) -> p a b c", a=dims[0], b=dims[1])
            return a

        psum = ctx.enter_context(nc.psum_tensor("psum", [P, 8, 512], F32))

        hT = carve(DC, T)
        cact = carve(DC)
        mod_b, mod = carve(MODS), carve(MODS)
        col_n1, col_n2 = carve(DC), carve(DC)
        col_mix = carve(DC)
        col_qk = carve(2)
        col_cv2 = carve(CW // P, CK2)
        sink = carve(AH)
        gate_dve = carve(8)
        amp = carve(2, DC)
        eps = carve(1)
        col_an, col_fn, col_ln = carve(DC), carve(DC), carve(DC)
        col_conv = carve(12, CONV_K)
        col_gn = carve(1)
        col_gb = carve(1)
        col_al = carve(1)
        base0 = top[0]
        slot = [carve(SLOT), carve(SLOT)]
        base1 = top[0]
        uT = carve(DC, T)
        qkvT = carve(3 * GH, TP)
        zT = carve(GH, T)
        fqk = carve(8, T)
        fv = carve(NT, FH * FD)
        mT = carve(DC, T)
        over_rstd = top[0]
        rstd = carve(2, TP)
        gates = carve(TP)
        gtok = carve(NT, NG)
        csum = carve(T)[0:FH, :]
        base2 = top[0]
        smallw = carve(DC, NG)
        cin = carve(2, CONV_K - 1 + T)
        ctmp = carve(2, T)
        graw = carve(T)
        gabs = carve(T)
        gln = carve(T)
        end_a = top[0]

        top[0] = base1
        kc, qc, vc, rhsD, rhsU, expD, expT, egrow = (carve(GH, P) for _ in range(8))
        assert top[0] <= base1 + DC * T
        top[0] = base2
        ktok, vtok, amat, qkT, qs, kdec, E, Dm, Pm, state = (carve(GH, P) for _ in range(10))
        nm = carve(LEVELS, GH * P)
        ecol = carve(12)
        end_g = top[0]
        top[0] = over_rstd
        vnew, res = carve(GH, P), carve(GH, P)
        top[0] = base2
        cb = carve(2, T)
        sc = carve(2, T)
        pT = carve(2, NT * P)
        mx = carve(2)
        rs = carve(2)
        assert top[0] <= max(end_a, end_g)
        top[0] = base1 + DC * T
        hid = carve(FC, T)
        sil = carve(2, T)

        xT2 = hT[:, :, META:T]
        top[0] = base1
        u2 = carve(DC, SEC)
        r2 = carve(2, SEC)
        keep = top[0]
        qkr = carve(5, SEC)
        vt2 = carve(SC, P)
        cosT, sinT, angT, kf = (carve(SEC) for _ in range(4))
        ki = kf.bitcast(I32)
        posi = carve(SEC)
        prod = carve(2, SEC + CK2 - 1)
        cc = carve(2, SEC)
        y2 = carve(CW // P, SEC)
        mix = carve(DC, SEC)
        sq2 = carve(2, SEC)
        tm2 = carve(2, SEC)
        ex = carve(PER, 2 * P)
        pT2 = carve(2, PER * P)
        mxs, nms, rss, ess = (carve(PER) for _ in range(4))
        top[0] = keep
        subk = carve(2 * PH, P)
        qf = carve(2, SEC)
        scb, scr = carve(2, SC, P), carve(2, SC, P)
        val = carve(2, SC, TOP)
        idu = carve(2, SC, TOP)
        idf = carve(2, SC, TOP)
        cand = carve(SC, TOP * TOP)
        cand2 = carve(SC, TOP * TOP)
        best = carve(SC, TOP)
        posu = carve(SC, TOP)
        posh, posl = carve(SC, TOP), carve(SC, TOP)
        eq = carve(2, SC * TOP, TOP)
        ebest = carve(SC, TOP)
        esum = carve(SC)
        tok = carve(3, SC, P)
        choice_end = top[0]
        top[0] = arena_floats - (DC * SEC + 3 * SEC)
        assert choice_end <= top[0], (choice_end, top[0])
        gij = carve(3, SEC)
        h2hi = carve(DC * SEC // 2).bitcast(BF16).rearrange("p (c t) -> p c t", c=DC)
        h2lo = carve(DC * SEC // 2).bitcast(BF16).rearrange("p (c t) -> p c t", c=DC)
        top[0] = base0
        dense = [carve(PK, P), carve(PK, P)]
        hotA, hotB = carve(RING, 4 * P), carve(RING, 4 * P)
        assert top[0] <= arena_floats - (DC * SEC + 3 * SEC), top[0]
        top[0] = base0
        acc = carve(DC, SEC)
        ust = [carve(DC, 2 * P) for _ in range(2)]
        uhl = [[carve(DC * P).bitcast(BF16).rearrange("p (c e) -> p c e", c=DC) for _ in range(2)] for _ in range(2)]
        vst = [carve(D) for _ in range(4)]
        vhl = [[carve(EB * D // 2).bitcast(BF16).rearrange("p (b f) -> p b f", b=EB) for _ in range(2)] for _ in range(2)]
        gst = [carve(SEC) for _ in range(4)]
        gel = [carve(SEC) for _ in range(2)]
        wf = [carve(SEC) for _ in range(2)]
        whl = [[carve(EB * SEC // 2).bitcast(BF16).rearrange("p (b t) -> p b t", b=EB) for _ in range(2)] for _ in range(2)]
        assert top[0] <= arena_floats - (DC * SEC + 3 * SEC), top[0]

        S = {n: sem(n) for n in (
            "const_in", "h_in", "small_in", "landed0", "landed1",
            "sq_ready", "ms_ready", "std_ready", "u_ready", "dve_step", "pool_step",
            "proj_ready", "proj_taken", "conv_done", "qkv_ready",
            "l2_sq", "l2_ms", "l2_std", "l2_done",
            "gate_y", "gate_act", "gate_done", "gate_T", "gate_tok",
            "g_staged", "g_rhs", "g_pre", "g_diff", "g_tok", "g_exp", "g_amat", "g_nm", "g_init", "g_prep",
            "g_p", "g_pc", "g_y", "g_lv", "g_ks", "g_res", "g_r", "g_v", "g_vc", "g_o", "g_oc", "g_state", "g_fin",
            "x_cb", "x_cbc", "x_s", "x_sc", "x_exp", "x_nrm", "x_t", "x_tc", "x_o", "x_oc", "x_csum",
            "out_done", "res_done", "ffn_ps", "ffn_sil", "ffn_hid", "final_done",
            "cact_ready", "mod_done", "mod_ready", "shifted", "x2_ready",
            "p2_ready", "p2_taken", "tab", "tab_sin", "qk_sq", "qk_ms", "qk_std", "qk_n", "qk_rot", "qk_done",
            "cv_prod", "cv_y", "mix_cv", "a_s", "a_sc", "a_exp", "a_p", "a_t", "a_tc", "a_o", "a_oc",
            "m_sq", "m_ms", "m_std", "m_done", "out2_done", "res2_done", "h2_split", "posi_in", "sub_in",
            "wq_done", "wq_taken", "sc_done", "sc_taken", "tk", "tk_free", "tk_scores", "tk_cand", "tk_exp", "tk_pos", "tk_top", "tk_gate", "h2_hi", "cv_cc", "a_e",
            "tk_eq", "tk_sel", "acc_zero", "gij_T", "gij_in", "hot_i", "hot_j", "hot_a", "dense_mm", "dense_in", "dense_out0", "dense_out1",
            "u_in0", "u_in1", "u_hi", "u_lo", "v_in0", "v_in1", "v_in2", "v_in3", "v_hi", "v_lo", "g_in0", "g_in1", "g_in2", "g_in3", "e_a", "e_gel", "e_w", "e_o", "e_acc", "stored",
        )}

        def W(name):
            return S[name]

        def fill_done(n):
            return S[f"landed{n % 2}"], 32 * (n // 2 + 1)

        def pair(f):
            return [psum[:, 2 * (f % 2), 0:HALF], psum[:, 2 * (f % 2) + 1, 0:HALF]]

        def slot_cols(n, width=512):
            return slot[n % 2][:, 0:DC * width].rearrange("p (c n) -> p c n", c=DC)

        NPROJ = 30

        block = ctx.enter_context(nc.Block())

        @block.sync
        def _(sp):
            sp.dma_start(cst[:, :], io["consts"]).then_inc(S["const_in"], 16)
            for c in range(DC):
                sp.dma_start(hT[:, c, 0:META], io["metaT"][c * P:(c + 1) * P, :]).then_inc(S["h_in"], 16)
                sp.dma_start(hT[:, c, META:T], io["xT"][c * P:(c + 1) * P, :]).then_inc(S["h_in"], 16)
            cols = lambda name: io[name].rearrange("(c p) -> p c", p=P)
            with nc.allow_non_contiguous_dma(reason="small vectors"):
                sp.dma_start(col_an[:, :], cols("attn_norm_w")).then_inc(S["small_in"], 16)
                sp.dma_start(col_fn[:, :], cols("ffn_norm_w")).then_inc(S["small_in"], 16)
                sp.dma_start(col_ln[:, :], cols("final_norm_w")).then_inc(S["small_in"], 16)
                for k in range(CONV_K):
                    sp.dma_start(col_conv[:, :, k], io["conv_w"][k, :].rearrange("(c p) -> p c", p=P)
                                 ).then_inc(S["small_in"], 16)
                sp.dma_start(col_gn[:, :], cols("gdn_norm_w")).then_inc(S["small_in"], 16)
                sp.dma_start(cact[:, :], cols("c")).then_inc(S["small_in"], 16)
                sp.dma_start(mod_b[:, :], cols("ada_b")).then_inc(S["small_in"], 16)
                sp.dma_start(col_n1[:, :], cols("norm1_g")).then_inc(S["small_in"], 16)
                sp.dma_start(col_n2[:, :], cols("norm2_g")).then_inc(S["small_in"], 16)
                sp.dma_start(col_mix[:, :], cols("mix_g")).then_inc(S["small_in"], 16)
                for k in range(2):
                    rows = slice(k * AD, (k + 1) * AD)
                    sp.dma_start(col_qk[rows, 0:1], io["q_norm_g"].rearrange("(p o) -> p o", o=1)).then_inc(S["small_in"], 16)
                    sp.dma_start(col_qk[rows, 1:2], io["k_norm_g"].rearrange("(p o) -> p o", o=1)).then_inc(S["small_in"], 16)
                for k in range(CK2):
                    sp.dma_start(col_cv2[:, :, k], io["conv_w2"][k, :].rearrange("(c p) -> p c", p=P)).then_inc(S["small_in"], 16)
                sp.dma_start(sink[:, :], io["sinks"].rearrange("(o h) -> o h", o=1).to_broadcast([P, AH])).then_inc(S["small_in"], 16)
                sp.wait_ge(S["pool_step"], 3)
                sp.dma_start(col_gb[0:FH, :], io["fgate_b"].rearrange("(p o) -> p o", o=1)).then_inc(S["small_in"], 16)
                sp.dma_start(col_gb[ROW_A:ROW_A + GH, :], io["dt_bias"].rearrange("(p o) -> p o", o=1)).then_inc(S["small_in"], 16)
                sp.dma_start(col_al[ROW_A:ROW_A + GH, :], io["a_log"].rearrange("(p o) -> p o", o=1)).then_inc(S["small_in"], 16)
                w = io["w_in"].rearrange("(c p) n -> p c n", p=P)
                c_b = 4 * GH * GD
                c_f = w.shape[2] - FH
                sp.dma_start(smallw[:, :, 0:FH], w[:, :, c_f:c_f + FH]).then_inc(S["small_in"], 16)
                sp.dma_start(smallw[:, :, ROW_B:ROW_B + GH], w[:, :, c_b:c_b + GH]).then_inc(S["small_in"], 16)
                sp.dma_start(smallw[:, :, ROW_A:ROW_A + GH], w[:, :, c_b + GH:c_b + 2 * GH]).then_inc(S["small_in"], 16)

            def fill(n, parts, reader, count):
                if reader:
                    sp.wait_ge(S[reader], count)
                for dst, src in parts:
                    sp.dma_start(dst, src).then_inc(S[f"landed{n % 2}"], 16)

            def halves(n, src, width=512):
                dst = slot_cols(n, width)
                return [(dst[:, 0:4, :], src[:, 0:4, :]), (dst[:, 4:8, :], src[:, 4:8, :])]

            wf = 4 * GH * GD + 2 * GH
            for n in range(7):
                c0 = n * 512 if n < 4 else wf + (n - 4) * 512
                fill(n, halves(n, w[:, :, c0:c0 + 512]), "proj_ready" if n >= 2 else None, 4 * (n - 1))
            wo = io["w_out"].rearrange("(c p) n -> p c n", p=P)
            aw = io["ada_w"].rearrange("(c p) n -> p c n", p=P)
            for k in range(12):
                reader, count = ("proj_ready", 24 + k * NT) if k < 2 else ("mod_done", 4 * (k - 1))
                fill(F_MOD + k, halves(F_MOD + k, aw[:, :, k * 512:(k + 1) * 512]), reader, count)
            for k in range(2):
                fill(F_OUT + k, halves(F_OUT + k, wo[:, :, k * 512:(k + 1) * 512]), "mod_done", 44 + 4 * k)
            wg = io["w_gate"].rearrange("(c p) n -> p c n", p=P)
            wu = io["w_up"].rearrange("(c p) n -> p c n", p=P)

            def gate_up(n, cols):
                dst = slot[n % 2].rearrange("p (g c n) -> p g c n", g=2, c=DC)
                return [(dst[:, 0], wg[:, :, cols]), (dst[:, 1], wu[:, :, cols])]

            for k in range(2):
                fill(F_GU + k, gate_up(F_GU + k, slice(k * 256, k * 256 + 256)), "out_done", 4 * k + 4)
            with sp.Fori(0, 4) as i:
                for k in range(2):
                    fill(F_GU + 2 + k, gate_up(F_GU + 2 + k, bass.ds(i * 512 + (2 + k) * 256, 256)), "ffn_ps", i * 4 + 2 * k + 2)
            fill(F_GU + 10, gate_up(F_GU + 10, slice(2560, 2816)), "ffn_ps", 18)
            wd = io["w_down"].rearrange("(c p) n -> p c n", p=P)

            def down(n, cols):
                dst = slot[n % 2][:, 0:FC * P].rearrange("p (c n) -> p c n", c=FC)
                return [(dst[:, 0:11], wd[:, 0:11, cols]), (dst[:, 11:22], wd[:, 11:22, cols])]

            for k in range(2):
                fill(F_DOWN + k, down(F_DOWN + k, slice(k * P, k * P + P)), "ffn_ps", 20 + 2 * k)
            with sp.Fori(0, 3) as i:
                for k in range(2):
                    fill(F_DOWN + 2 + k, down(F_DOWN + 2 + k, bass.ds(i * 256 + (2 + k) * P, P)), "out_done", i * 2 + DC + k + 1)


            sp.wait_ge(S["x2_ready"], DC)
            sp.dma_start(posi.bitcast(I32), io["positions"].rearrange("(o t) -> o t", o=1).to_broadcast([P, SEC])).then_inc(S["posi_in"], 16)
            w2 = io["w_in2"].rearrange("(c p) n -> p c n", p=P)
            fill(F_Q2, halves(F_Q2, w2[:, :, 0:512]), "out_done", 2 * DC - 1)
            fill(F_KV2, halves(F_KV2, w2[:, :, 512:768], 256), "out_done", 2 * DC)
            c_cb, c_cc, c_cu = 768, 768 + CW, 768 + 2 * CW
            for k in range(2):
                dst = slot[(F_CU2 + k) % 2].rearrange("p (g c n) -> p g c n", g=2, c=DC)
                o = k * 256
                fill(F_CU2 + k, [(dst[:, 0], w2[:, :, c_cc + o:c_cc + o + 256]), (dst[:, 1], w2[:, :, c_cu + o:c_cu + o + 256])],
                     "p2_ready", 4 if k == 0 else 5 + SC)
            fill(F_CB2, halves(F_CB2, w2[:, :, c_cb:c_cb + 512]), "p2_ready", 5 + SC + 2)
            wo2 = io["w_out2"].rearrange("(c p) n -> p c n", p=P)
            for k in range(2):
                fill(F_OUT2 + k, halves(F_OUT2 + k, wo2[:, :, k * 512:(k + 1) * 512]), "p2_ready", 5 + SC + 4 * (k + 1))
            wq = io["wq"].rearrange("(c p) n -> p c n", p=P)
            for k in range(4):
                reader, count = ("out2_done", 4 * (k + 1)) if k < 2 else ("wq_done", 4 * (k - 1))
                fill(F_WQ + k, halves(F_WQ + k, wq[:, :, k * 512:(k + 1) * 512]), reader, count)
                if k == 0:
                    sp.wait_ge(S["m_done"], DC)
                    sp.dma_start(subk[:, :, :], io["subk"].rearrange("u p k -> p u k")).then_inc(S["sub_in"], 16)

            for t in range(SC):
                sp.wait_ge(S["dense_in"], 32 * (t + 1) + RING)
                for q in range(4):
                    sp.dma_start(io["dense"][q * 32:(q + 1) * 32, :, t * P:(t + 1) * P].rearrange("i j t -> j i t"),
                                 dense[t % 2][:, q * 32:(q + 1) * 32, :]).then_inc(S[f"dense_out{t % 2}"], 16)

            ut = io["uT"].rearrange("(c p) e -> p c e", p=P)
            vt = io["v"].rearrange("(b p) f -> b p f", p=P)
            sp.wait_ge(S["dense_out0"], 64 * SC // 2)
            sp.wait_ge(S["dense_out1"], 64 * SC // 2)

            def load_group(g, first):
                for k in range(2):
                    if not first:
                        sp.wait_ge(S["u_lo"], g * 2 + k - 1)
                    sp.dma_start(ust[k][:, :, :], ut[:, :, bass.ds(g * (EB * P) + k * 2 * P, 2 * P)]).then_inc(S[f"u_in{k}"], 16)
                for b in range(EB):
                    if not first:
                        sp.wait_ge(S["e_w"], g * (3 * EB) + (3 * (b - EB) + 1 + 6))
                    sp.dma_start(gst[b], io["dense"][bass.ds(g * EB + b, 1), :, :].rearrange("o j t -> (o j) t")).then_inc(S[f"g_in{b}"], 16)
                    if not first:
                        sp.wait_ge(S["v_lo"], g * EB + (b - EB + 1))
                    sp.dma_start(vst[b], vt[bass.ds(g * EB + b, 1), :, :].rearrange("o p f -> (o p) f")).then_inc(S[f"v_in{b}"], 16)

            load_group(0, True)
            with sp.Fori(1, GROUPS) as g:
                load_group(g, False)
            for c in range(DC):
                sp.wait_ge(S["stored"], c + 1)
                sp.dma_start(io["out"][c * P:(c + 1) * P, :], acc[:, c, :]).then_inc(S["final_done"], 16)
            sp.wait_ge(S["final_done"], 16 * DC)

        @block.gpsimd
        def _(pool):
            n_step = 0

            def step(ins):
                nonlocal n_step
                n_step += 1
                ins.then_inc(S["pool_step"], 1)

            step(pool.memset(col_gb[:, :], 0.0))
            step(pool.memset(col_al[:, :], 0.0))
            step(pool.memset(smallw[:, :, :], 0.0))
            step(pool.memset(eps[:, :], EPS))
            step(pool.memset(cin[:, :, 0:CONV_K - 1], 0.0))
            step(pool.memset(qkvT[:, :, T:TP], 0.0))
            step(pool.memset(gates[:, :], 0.0))
            assert n_step == 7

            pool.wait_ge(S["gate_tok"], NT)
            pool.wait_ge(S["l2_done"], 2 * GH)
            pool.wait_ge(S["x_csum"], 1)
            pool.memset(state[:, :, :], 0.0).then_inc(S["g_state"], GH)
            pool.engine_nop().then_inc(S["g_fin"], 1)
            pool.engine_nop().then_inc(S["g_oc"], 1)
            with pool.Fori(0, NT) as m:
                pool.wait_ge(S["g_fin"], m + 1)
                tile = bass.ds(m * P, P)
                pool.tensor_copy(kc[:, :, :], qkvT[:, GH:2 * GH, tile]).then_inc(S["g_staged"], 1)
                pool.tensor_copy(qc[:, :, :], qkvT[:, 0:GH, tile]).then_inc(S["g_staged"], 1)
                pool.tensor_copy(vc[:, :, :], qkvT[:, 2 * GH:3 * GH, tile]).then_inc(S["g_staged"], 1)
                g = gtok[:, bass.ds(m, 1), ROW_A:ROW_A + GH].rearrange("p o h -> p (o h)")
                gb = g.unsqueeze(2).to_broadcast([P, GH, P])
                pool.tensor_tensor(rhsD[:, :, :], const("after").unsqueeze(1).to_broadcast([P, GH, P]), gb,
                                   ALU.mult).then_inc(S["g_rhs"], 1)
                pool.tensor_tensor(rhsU[:, :, :], const("upto").unsqueeze(1).to_broadcast([P, GH, P]), gb,
                                   ALU.mult).then_inc(S["g_rhs"], 1)
                pool.wait_ge(S["g_amat"], m * GH + GH)
                for lev in range(LEVELS):
                    pool.tensor_tensor(nm[:, lev, :].rearrange("p (h t) -> p h t", h=GH), amat[:, :, :],
                                       const(f"merge{lev}").unsqueeze(1).to_broadcast([P, GH, P]),
                                       ALU.mult).then_inc(S["g_nm"], 1)

            pool.wait_ge(S["x_csum"], 1)
            pool.engine_nop().then_inc(S["dense_mm"], RING)
            pool.engine_nop().then_inc(S["dense_in"], RING)
            pool.engine_nop().then_inc(S["e_w"], 6)
            pool.engine_nop().then_inc(S["e_o"], DC + 1)
            pool.engine_nop().then_inc(S["e_acc"], 2)

            pool.wait_ge(S["tab"], 1)
            with pool.Fori(0, PH) as h:
                for p in range(2):
                    pool.wait_ge(S["tk_pos"], h * 2 + p + 1)
                    e4 = eq[:, p].rearrange("p (a b) k -> p a b k", a=SC)
                    pool.tensor_tensor(e4, e4, idf[:, p].unsqueeze(2).to_broadcast([P, SC, TOP, TOP]),
                                       ALU.mult).then_inc(S["tk_eq"], 1)

            pool.wait_ge(S["gij_in"], 3)
            for t in range(SC):
                with pool.Fori(0, 32 // RING) as i:
                    for k in range(RING):
                        pool.wait_ge(S["hot_i"], i * RING + (32 * t + k + 1))
                        at = i * (4 * RING) + (P * t + 4 * k)
                        a4 = hotA[:, k].rearrange("p (q i) -> p q i", q=4)
                        pool.tensor_tensor(a4, a4, gij[:, 0, bass.ds(at, 4)].unsqueeze(2).to_broadcast([P, 4, P]),
                                           ALU.mult).then_inc(S["hot_a"], 1)

            pool.wait_ge(S["dense_out0"], 64 * SC // 2)
            pool.wait_ge(S["dense_out1"], 64 * SC // 2)
            pool.memset(acc[:, :, :], 0.0).then_inc(S["acc_zero"], 1)
            with pool.Fori(0, GROUPS // 2) as i:
                for par in range(2):
                    for b in range(EB):
                        n = i * (2 * EB) + (par * EB + b)
                        pool.wait_ge(S["v_hi"], n + 1)
                        pool.tensor_tensor(vhl[par][1][:, b, :], vst[b], vhl[par][0][:, b, :], ALU.subtract).then_inc(S["v_lo"], 1)

        @block.tensor
        def _(pe):
            mm = pe.matmul
            pe.wait_ge(S["const_in"], 16)

            def mean_square(k, width, banks):
                for c in range(DC):
                    pe.wait_ge(S["sq_ready"], DC * k + c + 1)
                    for j, out in enumerate(banks):
                        last = mm(out, const("mean_d"), uT[:, c, j * width:(j + 1) * width],
                                  start=c == 0, stop=c == DC - 1)
                last.then_inc(S["ms_ready"], 1)

            mean_square(0, HALF, [psum[:, 6, 0:HALF], psum[:, 7, 0:HALF]])

            pe.wait_ge(S["u_ready"], DC)
            for f in range(24):
                n, k = divmod(f, 4)
                if k == 0:
                    pe.wait_ge(*fill_done(n))
                if f >= 2:
                    pe.wait_ge(S["proj_taken"], f - 1)
                w = slot_cols(n)
                for c in range(DC):
                    for j, out in enumerate(pair(f)):
                        last = mm(out, w[:, c, k * P:(k + 1) * P], uT[:, c, j * HALF:(j + 1) * HALF],
                                  start=c == 0, stop=c == DC - 1)
                last.then_inc(S["proj_ready"], 1)
            pe.wait_ge(*fill_done(6))
            w = slot_cols(6)
            for m in range(NT):
                f = 24 + m
                rows = P if m < NT - 1 else LAST
                pe.wait_ge(S["proj_taken"], f - 1)
                for c in range(DC):
                    last = mm(psum[0:rows, 2 * (f % 2), :], uT[:, c, m * P:m * P + rows], w[:, c, :],
                              start=c == 0, stop=c == DC - 1)
                last.then_inc(S["proj_ready"], 1)
            f = 29
            pe.wait_ge(S["proj_taken"], f - 1)
            pe.wait_ge(S["small_in"], 16 * SMALL)
            for c in range(DC):
                for j, out in enumerate(pair(f)):
                    last = mm(out[0:NG, :], smallw[:, c, :], uT[:, c, j * HALF:(j + 1) * HALF],
                              start=c == 0, stop=c == DC - 1)
            last.then_inc(S["proj_ready"], 1)

            for f in range(2 * GH):
                pe.wait_ge(S["l2_sq"], f + 1)
                if f >= 2:
                    pe.wait_ge(S["l2_std"], f - 1)
                for j in range(2):
                    last = mm(psum[:, 4 + 2 * (f % 2) + j, 0:HALF], const("ones"),
                              rstd[:, f % 2, j * HALF:(j + 1) * HALF], start=True, stop=True)
                last.then_inc(S["l2_ms"], 1)

            pe.wait_ge(S["gate_done"], 2)
            pe.wait_ge(S["proj_taken"], 30)
            for m in range(NT):
                if m >= 2:
                    pe.wait_ge(S["gate_tok"], m - 1)
                pe.transpose(psum[:, m % 2, 0:NG], gates[0:NG, m * P:(m + 1) * P],
                             const("ident")[0:NG, 0:NG]).then_inc(S["gate_T"], 1)

            pe.wait_ge(S["gate_tok"], NT)
            pe.wait_ge(S["l2_std"], 2 * GH)
            bank = lambda b: psum[:, b, :].rearrange("p (h t) -> p h t", h=GH)
            KK, KQ, KT, VT, DF, DFT, GR, SM = (bank(b) for b in range(8))
            with pe.Fori(0, NT) as m:
                pe.wait_ge(S["g_staged"], m * 3 + 3)
                pe.wait_ge(S["g_oc"], m + 1)
                pe.wait_ge(S["g_state"], m * GH + GH)
                for h in range(GH):
                    mm(KK[:, h], kc[:, h], kc[:, h], start=True, stop=True)
                    mm(KQ[:, h], kc[:, h], qc[:, h], start=True, stop=True)
                    pe.transpose(KT[:, h], kc[:, h], const("ident"))
                    last = pe.transpose(VT[:, h], vc[:, h], const("ident"))
                last.then_inc(S["g_pre"], 1)
                pe.wait_ge(S["g_rhs"], m * 2 + 2)
                flat = lambda a: a.rearrange("p h t -> p (h t)")
                mm(psum[:, 4, :], const("upto"), flat(rhsD), start=True, stop=True)
                mm(psum[:, 5, :], const("after"), flat(rhsU), start=True, stop=True)
                mm(psum[:, 6, :], const("ones"), flat(rhsU), start=True, stop=True)
                g = gtok[:, bass.ds(m, 1), ROW_A:ROW_A + GH].rearrange("p o h -> p (o h)")
                mm(psum[:, 7, 0:4], const("upto"), g, start=True, stop=True)
                mm(psum[:, 7, 4:8], const("after"), g, start=True, stop=True)
                mm(psum[:, 7, 8:12], const("ones"), g, start=True, stop=True).then_inc(S["g_diff"], 1)
                pe.wait_ge(S["g_init"], m * 2 + 2)
                pe.wait_ge(S["g_tok"], m * 2 + 2)
                pe.wait_ge(S["g_exp"], m * 4 + 4)
                for lev in range(LEVELS):
                    pe.wait_ge(S["g_nm"], m * LEVELS + lev + 1)
                    if lev:
                        pe.wait_ge(S["g_lv"], m * 2 * LEVELS + 2 * lev)
                    for h in range(GH):
                        last = mm(KT[:, h], nm[:, lev, h * P:(h + 1) * P], E[:, h], start=True, stop=True)
                    last.then_inc(S["g_p"], 1)
                    pe.wait_ge(S["g_pc"], m * LEVELS + lev + 1)
                    for h in range(GH):
                        mm(VT[:, h], Dm[:, h], Pm[:, h], start=True, stop=True)
                        last = mm(DF[:, h], Pm[:, h], Dm[:, h], start=True, stop=True)
                    last.then_inc(S["g_y"], 1)
                for h in range(GH):
                    last = mm(DFT[:, h], kc[:, h], state[:, h], start=True, stop=True)
                last.then_inc(S["g_ks"], 1)
                pe.wait_ge(S["g_r"], m + 1)
                pe.wait_ge(S["g_lv"], m * 2 * LEVELS + 2 * LEVELS)
                for h in range(GH):
                    last = mm(GR[:, h], E[:, h], res[:, h], start=True, stop=True)
                last.then_inc(S["g_v"], 1)
                pe.wait_ge(S["g_vc"], m + 1)
                pe.wait_ge(S["g_prep"], m * 4 + 4)
                for h in range(GH):
                    mm(SM[:, h], state[:, h], qs[:, h], start=True, stop=False)
                    last = mm(SM[:, h], vnew[:, h], qkT[:, h], start=False, stop=True)
                last.then_inc(S["g_o"], 1)
                for h in range(GH):
                    last = mm(KK[:, h], kdec[:, h], vnew[:, h], start=True, stop=True)
                last.then_inc(S["g_fin"], 1)

            for f in range(GH):
                pe.wait_ge(S["l2_sq"], 2 * GH + f + 1)
                if f >= 2:
                    pe.wait_ge(S["l2_std"], 2 * GH + f - 1)
                for j in range(2):
                    last = mm(psum[:, 4 + 2 * (f % 2) + j, 0:HALF], const("mean_head"),
                              rstd[:, f % 2, j * HALF:(j + 1) * HALF], start=True, stop=True)
                last.then_inc(S["l2_ms"], 1)

            def mod_tile(f):
                n, k = divmod(f, 4)
                if k == 0:
                    pe.wait_ge(*fill_done(F_MOD + n))
                if f == 0:
                    pe.wait_ge(S["cact_ready"], 1)
                w = slot_cols(F_MOD + n)
                for c in range(DC):
                    last = mm(psum[:, 7, f:f + 1], w[:, c, k * P:(k + 1) * P], cact[:, c:c + 1],
                              start=c == 0, stop=c == DC - 1)
                last.then_inc(S["mod_done"], 1)

            pe.wait_ge(S["x_csum"], 1)
            pe.wait_ge(S["g_state"], GH * (NT + 1))
            pe.wait_ge(S["l2_std"], 3 * GH)
            step = 0
            for h in range(FH):
                lo, hi = (h % 2) * FD, (h % 2) * FD + FD
                if h:
                    pe.wait_ge(S["x_cbc"], h)
                for j in range(2):
                    last = mm(psum[:, 2 + j, 0:HALF], const("pick", FH)[:, h * P:(h + 1) * P],
                              csum[:, j * HALF:(j + 1) * HALF], start=True, stop=True)
                last.then_inc(S["x_cb"], 1)
                for m in range(NT):
                    rows = P if m < NT - 1 else LAST
                    keys = m * P + rows
                    if step:
                        pe.wait_ge(S["x_sc"], step)
                    for j in range(-(-keys // 512)):
                        kk = min(512, keys - j * 512)
                        last = mm(psum[0:rows, j, 0:kk], fqk[lo:hi, h // 2, m * P:m * P + rows],
                                  fqk[lo:hi, 4 + h // 2, j * 512:j * 512 + kk], start=True, stop=True)
                    last.then_inc(S["x_s"], 1)
                    single = 2 * FH * NT - MODS
                    if step < single:
                        mod_tile(step)
                    else:
                        mod_tile(2 * step - single)
                        mod_tile(2 * step - single + 1)
                    pe.wait_ge(S["x_nrm"], step + 1)
                    if step:
                        pe.wait_ge(S["x_tc"], step)
                    for j in range(m + 1):
                        kr = P if j < NT - 1 else LAST
                        last = pe.transpose(psum[0:kr, 4 + j // 4, (j % 4) * P:(j % 4) * P + rows],
                                            sc[0:rows, step % 2, j * P:j * P + kr], const("ident")[0:rows, 0:rows])
                    last.then_inc(S["x_t"], 1)
                    pe.wait_ge(S["x_tc"], step + 1)
                    if step:
                        pe.wait_ge(S["x_oc"], step)
                    for j in range(m + 1):
                        kr = P if j < NT - 1 else LAST
                        last = mm(psum[lo:hi, 6, 0:rows], fv[0:kr, j, h * FD:(h + 1) * FD],
                                  pT[0:kr, step % 2, j * P:j * P + rows], start=j == 0, stop=j == m)
                    last.then_inc(S["x_o"], 1)
                    step += 1

            pe.wait_ge(S["x_oc"], step)
            pe.wait_ge(S["l2_done"], 3 * GH)
            pe.wait_ge(S["mod_ready"], 1)
            for f in range(8):
                n, k = F_OUT + f // 4, f % 4
                if k == 0:
                    pe.wait_ge(*fill_done(n))
                if f >= 2:
                    pe.wait_ge(S["res_done"], f - 1)
                w = slot_cols(n)
                for c in range(DC):
                    for j, out in enumerate(pair(f)):
                        last = mm(out, w[:, c, k * P:(k + 1) * P], mT[:, c, j * HALF:(j + 1) * HALF],
                                  start=c == 0, stop=c == DC - 1)
                last.then_inc(S["out_done"], 1)

            mean_square(1, HALF, [psum[:, 6, 0:HALF], psum[:, 7, 0:HALF]])
            pe.wait_ge(S["u_ready"], 2 * DC)
            pe.wait_ge(S["std_ready"], 4)

            def gate_up_tile(w, k, before):
                if before is not None:
                    pe.wait_ge(S["ffn_hid"], before)
                for g in range(2):
                    for c in range(DC):
                        for j in range(2):
                            last = mm(psum[:, 4 * g + 2 * (k % 2) + j, 0:HALF], w[:, g, c, k % 2 * P:(k % 2 + 1) * P],
                                      uT[:, c, j * HALF:(j + 1) * HALF], start=c == 0, stop=c == DC - 1)
                last.then_inc(S["ffn_ps"], 1)

            def gate_up_fill(n, landed, first_tile):
                w = slot[n % 2].rearrange("p (g c n) -> p g c n", g=2, c=DC)
                pe.wait_ge(S[f"landed{n % 2}"], landed)
                for k in range(2):
                    last = gate_up_tile(w, k, first_tile + k - 1)
    
            with pe.Fori(0, 5) as i:
                for k in range(2):
                    gate_up_fill(F_GU + k, i * 32 + fill_done(F_GU + k)[1], i * 4 + 2 + 2 * k)
            gate_up_fill(F_GU + 10, fill_done(F_GU + 10)[1], FC)
            pe.wait_ge(S["ffn_hid"], FC + 2)

            with pe.Fori(0, 4) as i:
                for k in range(2):
                    n = F_DOWN + k
                    w = slot[n % 2][:, 0:FC * P].rearrange("p (c n) -> p c n", c=FC)
                    pe.wait_ge(S[f"landed{n % 2}"], i * 32 + fill_done(n)[1])
                    pe.wait_ge(S["res_done"], i * 2 + DC + k - 1)
                    for c in range(FC):
                        for j in range(2):
                            last = mm(psum[:, 2 * k + j, 0:HALF], w[:, c, :], hid[:, c, j * HALF:(j + 1) * HALF],
                                      start=c == 0, stop=c == FC - 1)
                    last.then_inc(S["out_done"], 1)
        
            def mean_square2(k):
                for c in range(DC):
                    pe.wait_ge(S["sq_ready"], DC * k + c + 1)
                    last = mm(psum[:, 6, :], const("mean_d"), u2[:, c, :], start=c == 0, stop=c == DC - 1)
                last.then_inc(S["ms_ready"], 1)

            mean_square2(2)
            mean_square2(3)

            def product(bank, w, cols, src, sig):
                for c in range(DC):
                    last = mm(psum[:, bank, :], w[:, c, cols], src[:, c, :], start=c == 0, stop=c == DC - 1)
                if sig:
                    last.then_inc(S[sig], 1)

            pe.wait_ge(S["shifted"], DC)
            for f in range(5):
                n, k = (F_Q2, f) if f < 4 else (F_KV2, 0)
                if k == 0:
                    pe.wait_ge(*fill_done(n))
                if f >= 2:
                    pe.wait_ge(S["p2_taken"], f - 1)
                product(f % 2, slot_cols(n, 512 if f < 4 else 256), slice(k * P, (k + 1) * P), u2, "p2_ready")
            w = slot_cols(F_KV2, 256)
            for t in range(SC):
                f = 5 + t
                pe.wait_ge(S["p2_taken"], f - 1)
                for c in range(DC):
                    last = mm(psum[:, f % 2, 0:P], u2[:, c, t * P:(t + 1) * P], w[:, c, P:2 * P],
                              start=c == 0, stop=c == DC - 1)
                last.then_inc(S["p2_ready"], 1)
            for j in range(8):
                f = 5 + SC + j
                if j < 5:
                    pe.wait_ge(S["qk_sq"], j + 1)
                    mm(psum[:, 4 + j % 2, :], const("mean_ah"), sq2[:, j % 2, :], start=True, stop=True).then_inc(S["qk_ms"], 1)
                if 2 <= j < 7:
                    pe.wait_ge(S["qk_n"], j - 1)
                    if j >= 4:
                        pe.wait_ge(S["qk_done"], j - 3)
                    mm(psum[:, 6 + j % 2, :], const("turn"), qkr[:, j - 2, :], start=True, stop=True).then_inc(S["qk_rot"], 1)
                pe.wait_ge(S["p2_taken"], f - 1)
                if j < 4:
                    n = F_CU2 + j // 2
                    if j % 2 == 0:
                        pe.wait_ge(*fill_done(n))
                    w = slot[n % 2].rearrange("p (g c n) -> p g c n", g=2, c=DC)
                    cols = slice(j % 2 * P, (j % 2 + 1) * P)
                    product(f % 2, w[:, 0], cols, u2, None)
                    product(2 + f % 2, w[:, 1], cols, u2, "p2_ready")
                else:
                    if j == 4:
                        pe.wait_ge(*fill_done(F_CB2))
                    product(f % 2, slot_cols(F_CB2), slice((j - 4) * P, (j - 3) * P), u2, "p2_ready")

            pe.wait_ge(S["qk_done"], 5)
            pe.wait_ge(S["p2_taken"], 5 + SC + 8)
            for s in range(SC * KV):
                n, kv = divmod(s, KV)
                lo, hi = kv * AD, (kv + 1) * AD
                k0 = P if n == 0 else 0
                if s:
                    pe.wait_ge(S["a_sc"], s)
                for i in range(PER):
                    last = mm(psum[:, i // 2, (i % 2) * 256 + k0:(i % 2) * 256 + 256], qkr[lo:hi, i, n * P:(n + 1) * P],
                              qkr[lo:hi, 4, (n - 1) * P + k0:(n + 1) * P], start=True, stop=True)
                last.then_inc(S["a_s"], 1)
                pe.wait_ge(S["a_p"], s + 1)
                if s:
                    pe.wait_ge(S["a_tc"], s)
                for i in range(PER):
                    for kb in range(k0 // P, 2):
                        last = pe.transpose(psum[:, 2 + kb, i * P:(i + 1) * P], ex[:, i, kb * P:(kb + 1) * P], const("ident"))
                last.then_inc(S["a_t"], 1)
                pe.wait_ge(S["a_tc"], s + 1)
                if s >= 2:
                    pe.wait_ge(S["a_oc"], s - 1)
                for kb in range(k0 // P, 2):
                    tile = n - 1 + kb
                    last = mm(psum[lo:hi, 4 + kv, :], vt2[:, tile, lo:hi], pT2[:, kb, :], start=kb == k0 // P, stop=kb == 1)
                last.then_inc(S["a_o"], 1)

            pe.wait_ge(S["a_oc"], SC * KV)
            for c in range(DC):
                pe.wait_ge(S["m_sq"], c + 1)
                last = mm(psum[:, 6 + c // 4, :], const("mean_mix"), u2[:, c, :], start=c % 4 == 0, stop=c % 4 == 3)
                if c % 4 == 3:
                    last.then_inc(S["m_ms"], 1)
            pe.wait_ge(S["m_done"], DC)
            for f in range(DC):
                n = F_OUT2 + f // 4
                if f % 4 == 0:
                    pe.wait_ge(*fill_done(n))
                if f >= 2:
                    pe.wait_ge(S["res2_done"], f - 1)
                product(f % 2, slot_cols(n), slice(f % 4 * P, (f % 4 + 1) * P), mix, "out2_done")
            mean_square2(4)

            pe.wait_ge(S["shifted"], 2 * DC)
            pe.wait_ge(S["res2_done"], DC)
            pe.wait_ge(S["sub_in"], 16)

            def scores(u):
                pe.wait_ge(S["wq_taken"], u + 1)
                if u >= 4:
                    pe.wait_ge(S["sc_taken"], u - 3)
                for t in range(SC):
                    last = mm(psum[:, 2 + u % 4, t * P:(t + 1) * P], qf[:, u % 2, t * P:(t + 1) * P], subk[:, u, :],
                              start=True, stop=True)
                last.then_inc(S["sc_done"], 1)

            for u in range(2 * PH):
                n = F_WQ + u // 4
                if u % 4 == 0:
                    pe.wait_ge(*fill_done(n))
                if u >= 2:
                    pe.wait_ge(S["wq_taken"], u - 1)
                product(u % 2, slot_cols(n), slice(u % 4 * P, (u % 4 + 1) * P), u2, "wq_done")
                if u:
                    scores(u - 1)
            scores(2 * PH - 1)

            pe.wait_ge(S["tk_sel"], 2 * PH)
            pe.wait_ge(S["tk_gate"], PH)
            pe.wait_ge(S["sc_taken"], 2 * PH)
            for a in range(3):
                for t in range(SC):
                    last = pe.transpose(psum[:, 4 + a, t * P:(t + 1) * P], tok[:, a, t, :], const("ident"))
                last.then_inc(S["gij_T"], 1)

            for t in range(SC):
                with pe.Fori(0, 32 // RING) as i:
                    for k in range(RING):
                        batch = i * RING + (32 * t + k)
                        pe.wait_ge(S["hot_j"], batch + 1)
                        pe.wait_ge(S["hot_a"], batch + 1)
                        pe.wait_ge(S["dense_in"], batch + 1)
                        for q in range(4):
                            last = mm(psum[:, k, q * P:(q + 1) * P], hotB[:, k, q * P:(q + 1) * P], hotA[:, k, q * P:(q + 1) * P],
                                      start=True, stop=True)
                        last.then_inc(S["dense_mm"], 1)

            pe.wait_ge(S["h2_split"], DC)
            pe.wait_ge(S["dense_in"], 32 * SC + RING)

            def up(g, par, first=False):
                for b in range(EB):
                    hi, lo = uhl[b // 2]
                    e = slice(b % 2 * P, (b % 2 + 1) * P)
                    if b % 2 == 0:
                        pe.wait_ge(S["u_lo"], g * 2 + (b // 2 + 1))
                    if not (first and b < 2):
                        pe.wait_ge(S["e_gel"], g * EB + (b - 1))
                    for c in range(DC):
                        mm(psum[:, b % 2, :], hi[:, c, e], h2hi[:, c, :], start=c == 0, stop=False)
                        mm(psum[:, b % 2, :], hi[:, c, e], h2lo[:, c, :], start=False, stop=False)
                        last = mm(psum[:, b % 2, :], lo[:, c, e], h2hi[:, c, :], start=False, stop=c == DC - 1)
                    last.then_inc(S["e_a"], 1)

            def down2(g, par):
                pe.wait_ge(S["e_w"], g * (3 * EB) + (3 * EB + 6))
                pe.wait_ge(S["v_lo"], g * EB + EB)
                vh, vl = vhl[par]
                wh, wl = whl[par]
                for f in range(DC):
                    pe.wait_ge(S["e_acc"], g * DC + (f + 1))
                    cols = slice(f * P, (f + 1) * P)
                    for b in range(EB):
                        mm(psum[:, 2 + f % 2, :], vh[:, b, cols], wh[:, b, :], start=b == 0, stop=False)
                        mm(psum[:, 2 + f % 2, :], vh[:, b, cols], wl[:, b, :], start=False, stop=False)
                        last = mm(psum[:, 2 + f % 2, :], vl[:, b, cols], wh[:, b, :], start=False, stop=b == EB - 1)
                    last.then_inc(S["e_o"], 1)

            up(0, 0, first=True)
            with pe.Fori(0, GROUPS // 2 - 1) as i:
                up(i * 2 + 1, 1)
                down2(i * 2, 0)
                up(i * 2 + 2, 0)
                down2(i * 2 + 1, 1)
            up(GROUPS - 1, 1)
            down2(GROUPS - 2, 0)
            down2(GROUPS - 1, 1)

        @block.scalar
        def _(act):
            f_ = act.activation

            def squares(k, src, width, before):
                for c in range(DC):
                    before(c)
                    f_(uT[:, c, 0:width], src[:, c, :], ACT.Square).then_inc(S["sq_ready"], 1)

            def std(k, banks, width):
                act.wait_ge(S["ms_ready"], k + 1)
                for j, src in enumerate(banks):
                    f_(rstd[:, 0, j * width:(j + 1) * width], src, ACT.Sqrt, bias=eps[:, 0:1]
                       ).then_inc(S["std_ready"], 1)

            squares(0, hT, T, lambda c: act.wait_ge(S["h_in"], 32 * DC))
            act.wait_ge(S["pool_step"], 7)
            act.wait_ge(S["small_in"], 16 * SMALL)
            std(0, [psum[:, 6, 0:HALF], psum[:, 7, 0:HALF]], HALF)

            f_(cact[:, :], cact[:, :], ACT.Silu).then_inc(S["cact_ready"], 1)

            def silu_conv(f):
                act.wait_ge(S["conv_done"], f + 1)
                f_(qkvT[:, f, 0:T], ctmp[:, f % 2, :], ACT.Silu).then_inc(S["qkv_ready"], 1)

            def take(f):
                act.wait_ge(S["proj_ready"], f + 1)

            for f in range(12):
                if f >= 2:
                    act.wait_ge(S["conv_done"], f - 1)
                take(f)
                o = cin[:, f % 2, CONV_K - 1:]
                f_(o[:, 0:HALF], pair(f)[0], ACT.Copy)
                f_(o[:, HALF:T], pair(f)[1], ACT.Copy).then_inc(S["proj_taken"], 1)
                if f:
                    silu_conv(f - 1)
            silu_conv(11)
            for f in range(12, 30):
                take(f)
                if f < 24:
                    dst, fn = (zT[:, f - 12, :], ACT.Silu) if f < 16 else (fqk[:, f - 16, :], ACT.Copy)
                    f_(dst[:, 0:HALF], pair(f)[0], fn)
                    f_(dst[:, HALF:T], pair(f)[1], fn).then_inc(S["proj_taken"], 1)
                elif f < 29:
                    rows = P if f < 28 else LAST
                    f_(fv[0:rows, f - 24, 0:256], psum[0:rows, 2 * (f % 2), 0:256], ACT.Copy)
                    f_(fv[0:rows, f - 24, 256:512], psum[0:rows, 2 * (f % 2), 256:512], ACT.Copy).then_inc(S["proj_taken"], 1)
                else:
                    f_(graw[0:NG, 0:HALF], pair(f)[0][0:NG, :], ACT.Copy)
                    f_(graw[0:NG, HALF:T], pair(f)[1][0:NG, :], ACT.Copy).then_inc(S["proj_taken"], 1)

            def head_square(f, src, first):
                n = first + f
                if f >= 2:
                    act.wait_ge(S["l2_done"], n - 1)
                f_(rstd[:, f % 2, 0:T], src[:, f, 0:T], ACT.Square).then_inc(S["l2_sq"], 1)

            def head_std(f, first):
                n = first + f
                act.wait_ge(S["l2_ms"], n + 1)
                for j in range(2):
                    ins = f_(rstd[:, f % 2, j * HALF:(j + 1) * HALF], psum[:, 4 + 2 * (f % 2) + j, 0:HALF], ACT.Sqrt,
                             bias=eps[:, 0:1])
                ins.then_inc(S["l2_std"], 1)

            def head_norms(count, src, first):
                head_square(0, src, first)
                for f in range(count):
                    if f + 1 < count:
                        head_square(f + 1, src, first)
                    head_std(f, first)

            act.wait_ge(S["qkv_ready"], 12)
            act.wait_ge(S["u_ready"], DC)
            head_norms(2 * GH, qkvT, 0)

            act.wait_ge(S["gate_y"], 2)
            f_(gabs[0:NG, :], gabs[0:NG, :], ACT.Exp, scale=-1.0).then_inc(S["gate_act"], 1)
            act.wait_ge(S["gate_act"], 1)
            f_(gln[0:NG, :], gabs[0:NG, :], ACT.Ln, bias=1.0).then_inc(S["gate_act"], 1)
            act.wait_ge(S["small_in"], 16 * SMALL)
            f_(col_al[0:NG, :], col_al[0:NG, :], ACT.Exp).then_inc(S["gate_act"], 1)
            act.wait_ge(S["gate_y"], 3)
            f_(gates[ROW_B:ROW_B + GH, 0:T], gabs[ROW_B:ROW_B + GH, :], ACT.Exp).then_inc(S["gate_done"], 1)

            for m in range(NT):
                act.wait_ge(S["gate_T"], m + 1)
                f_(gtok[:, m, :], psum[:, m % 2, 0:NG], ACT.Copy).then_inc(S["gate_tok"], 1)

            flat = lambda a: a.rearrange("p h t -> p (h t)")
            with act.Fori(0, NT) as m:
                act.wait_ge(S["g_pre"], m + 1)
                f_(flat(ktok), psum[:, 2, :], ACT.Copy).then_inc(S["g_tok"], 1)
                f_(flat(vtok), psum[:, 3, :], ACT.Copy).then_inc(S["g_tok"], 1)
                act.wait_ge(S["g_diff"], m + 1)
                f_(flat(expD), psum[:, 4, :], ACT.Exp).then_inc(S["g_exp"], 1)
                f_(flat(expT), psum[:, 5, :], ACT.Exp).then_inc(S["g_exp"], 1)
                f_(flat(egrow), psum[:, 6, :], ACT.Exp).then_inc(S["g_exp"], 1)
                f_(ecol[:, 0:12], psum[:, 7, 0:12], ACT.Exp).then_inc(S["g_exp"], 1)
                for lev in range(LEVELS):
                    act.wait_ge(S["g_p"], m * LEVELS + lev + 1)
                    f_(flat(Pm), psum[:, 2, :], ACT.Copy).then_inc(S["g_pc"], 1)
                act.wait_ge(S["g_v"], m + 1)
                f_(flat(vnew), psum[:, 6, :], ACT.Copy).then_inc(S["g_vc"], 1)
                act.wait_ge(S["g_o"], m + 1)
                f_(qkvT[:, 2 * GH:3 * GH, bass.ds(m * P, P)], psum[:, 7, :].rearrange("p (h t) -> p h t", h=GH),
                   ACT.Copy).then_inc(S["g_oc"], 1)

            act.wait_ge(S["g_oc"], NT + 1)
            act.wait_ge(S["g_fin"], NT + 1)
            head_norms(GH, qkvT[:, 2 * GH:3 * GH, :], 2 * GH)

            act.wait_ge(S["l2_done"], 3 * GH)
            step = 0
            for h in range(FH):
                act.wait_ge(S["x_cb"], h + 1)
                if h >= 2:
                    act.wait_ge(S["x_sc"], (h - 1) * NT)
                for j in range(2):
                    ins = f_(cb[:, h % 2, j * HALF:(j + 1) * HALF], psum[:, 2 + j, 0:HALF], ACT.Copy)
                ins.then_inc(S["x_cbc"], 1)
                for m in range(NT):
                    rows = P if m < NT - 1 else LAST
                    keys = m * P + rows
                    act.wait_ge(S["x_exp"], 2 * step + 1)
                    f_(sc[0:rows, step % 2, 0:keys], sc[0:rows, step % 2, 0:keys], ACT.Exp,
                       bias=mx[0:rows, step % 2:step % 2 + 1], accum_out=rs[0:rows, step % 2:step % 2 + 1]
                       ).then_inc(S["x_exp"], 1)
                    act.wait_ge(S["x_t"], step + 1)
                    if step >= 2:
                        act.wait_ge(S["x_o"], step - 1)
                    for b in range(-(-(m + 1) // 4)):
                        n = min(4, m + 1 - 4 * b)
                        kr = P if b == 0 else LAST
                        src = psum[0:kr, 4 + b, 0:n * P].rearrange("p (a t) -> p a t", t=P)[:, :, 0:rows]
                        dst = pT[0:kr, step % 2, 4 * b * P:(4 * b + n) * P].rearrange("p (a t) -> p a t", t=P)[:, :, 0:rows]
                        ins = f_(dst, src, ACT.Copy)
                    ins.then_inc(S["x_tc"], 1)
                    step += 1

            squares(1, hT, T, lambda c: act.wait_ge(S["res_done"], DC))
            std(1, [psum[:, 6, 0:HALF], psum[:, 7, 0:HALF]], HALF)

            def silu_tile(k, ready, free):
                act.wait_ge(S["ffn_ps"], ready)
                act.wait_ge(S["ffn_hid"], free)
                for j in range(2):
                    ins = f_(sil[:, k, j * HALF:(j + 1) * HALF], psum[:, 2 * k + j, 0:HALF], ACT.Silu)
                ins.then_inc(S["ffn_sil"], 1)

            with act.Fori(0, FC // 2) as i:
                for k in range(2):
                    silu_tile(k, i * 2 + k + 1, i * 2 + k + 1)

            def squares2(k, ready, count):
                for c in range(DC):
                    act.wait_ge(S[ready], count(c))
                    f_(u2[:, c, :], xT2[:, c, :], ACT.Square).then_inc(S["sq_ready"], 1)

            def std2(k):
                act.wait_ge(S["ms_ready"], k + 1)
                f_(r2[:, 0, :], psum[:, 6, :], ACT.Sqrt, bias=eps[:, 0:1]).then_inc(S["std_ready"], 1)

            def shift(k, col):
                for c in range(DC):
                    act.wait_ge(S["u_ready"], (2 + k) * DC + c + 1)
                    f_(u2[:, c, :], u2[:, c, :], ACT.Identity, bias=mod[:, col + c:col + c + 1]).then_inc(S["shifted"], 1)

            squares2(2, "res_done", lambda c: 2 * DC)
            std2(2)
            squares2(3, "x2_ready", lambda c: c + 1)
            std2(3)
            shift(0, 0)
            for f in range(5 + SC):
                act.wait_ge(S["p2_ready"], f + 1)
                if f < 5:
                    f_(qkr[:, f, :], psum[:, f % 2, :], ACT.Copy).then_inc(S["p2_taken"], 1)
                else:
                    f_(vt2[:, f - 5, :], psum[:, f % 2, 0:P], ACT.Copy).then_inc(S["p2_taken"], 1)
            act.wait_ge(S["tab"], 1)
            f_(sinT, sinT, ACT.Sin).then_inc(S["tab_sin"], 1)
            f_(cosT, cosT, ACT.Sin).then_inc(S["tab_sin"], 1)
            act.wait_ge(S["p2_taken"], 5)
            for j in range(5):
                if j >= 2:
                    act.wait_ge(S["qk_n"], j - 1)
                f_(sq2[:, j % 2, :], qkr[:, j, :], ACT.Square).then_inc(S["qk_sq"], 1)
                act.wait_ge(S["qk_ms"], j + 1)
                f_(sq2[:, j % 2, :], psum[:, 4 + j % 2, :], ACT.Sqrt, bias=eps[:, 0:1]).then_inc(S["qk_std"], 1)
                if j < 4:
                    f = 5 + SC + j
                    act.wait_ge(S["p2_ready"], f + 1)
                    if j >= 2:
                        act.wait_ge(S["p2_taken"], f - 1)
                    f_(cc[:, j % 2, :], psum[:, f % 2, :], ACT.Copy).then_inc(S["cv_cc"], 1)

            for s in range(SC * KV):
                n, kv = divmod(s, KV)
                lo, hi = kv * AD, (kv + 1) * AD
                k0 = P if n == 0 else 0
                act.wait_ge(S["a_exp"], 2 * s + 2)
                for i in range(PER):
                    f_(ex[:, i, k0:], ex[:, i, k0:], ACT.Exp, bias=nms[:, i:i + 1], scale=AD ** -0.5,
                       accum_out=rss[:, i:i + 1])
                f_(ess[:, :], ess[:, :], ACT.Exp).then_inc(S["a_e"], 1)
                act.wait_ge(S["a_t"], s + 1)
                if s:
                    act.wait_ge(S["a_o"], s)
                for kb in range(k0 // P, 2):
                    ins = f_(pT2[:, kb, :], psum[:, 2 + kb, :], ACT.Copy)
                ins.then_inc(S["a_tc"], 1)

            for c in range(DC):
                act.wait_ge(S["a_oc"], SC * KV)
                act.wait_ge(S["mix_cv"], 4)
                f_(u2[:, c, :], mix[:, c, :], ACT.Square).then_inc(S["m_sq"], 1)
            for g in range(2):
                act.wait_ge(S["m_ms"], g + 1)
                f_(r2[:, g, :], psum[:, 6 + g, :], ACT.Sqrt, bias=eps[:, 0:1]).then_inc(S["m_std"], 1)

            act.wait_ge(S["m_done"], DC)
            squares2(4, "res2_done", lambda c: c + 1)
            std2(4)
            shift(1, 3 * DC)
            for c in range(DC):
                act.wait_ge(S["shifted"], DC + c + 1)
                f_(h2hi[:, c, :], u2[:, c, :], ACT.Copy).then_inc(S["h2_hi"], 1)

            def take_scores(u):
                act.wait_ge(S["sc_done"], u + 1)
                if u >= 2:
                    act.wait_ge(S["tk_free"], u // 2)
                f_(scb[:, u % 2].rearrange("p t k -> p (t k)"), psum[:, 2 + u % 4, :], ACT.Copy).then_inc(S["sc_taken"], 1)

            def gate_exp(h):
                act.wait_ge(S["tk_top"], h + 1)
                f_(ebest[:, :, :], ebest[:, :, :], ACT.Exp).then_inc(S["tk_exp"], 1)

            for u in range(2 * PH):
                act.wait_ge(S["wq_done"], u + 1)
                if u >= 2:
                    act.wait_ge(S["sc_done"], u - 1)
                f_(qf[:, u % 2, :], psum[:, u % 2, :], ACT.Copy).then_inc(S["wq_taken"], 1)
                if u:
                    take_scores(u - 1)
                if u >= 3 and u % 2:
                    gate_exp(u // 2 - 1)
            take_scores(2 * PH - 1)
            gate_exp(PH - 1)
            for a in range(3):
                act.wait_ge(S["gij_T"], a + 1)
                f_(gij[:, a, :], psum[:, 4 + a, :], ACT.Copy).then_inc(S["gij_in"], 1)

            for t in range(SC):
                if t >= 2:
                    act.wait_ge(S[f"dense_out{t % 2}"], 64 * (t // 2))
                with act.Fori(0, 32 // RING) as i:
                    for k in range(RING):
                        act.wait_ge(S["dense_mm"], i * RING + (32 * t + k + 1 + RING))
                        f_(dense[t % 2][:, :, bass.ds(i * (4 * RING) + 4 * k, 4)].rearrange("p i q -> p q i"),
                           psum[:, k, :].rearrange("p (q i) -> p q i", q=4), ACT.Copy).then_inc(S["dense_in"], 1)

            act.wait_ge(S["dense_out0"], 64 * SC // 2)
            act.wait_ge(S["dense_out1"], 64 * SC // 2)

            def u_high(k, landed, used=None):
                act.wait_ge(S[f"u_in{k}"], landed)
                if used is not None:
                    act.wait_ge(S["e_a"], used)
                f_(uhl[k][0][:, :, :], ust[k][:, :, :], ACT.Copy).then_inc(S["u_hi"], 1)

            def gelu_group(g, par, more=True):
                for b in range(EB):
                    act.wait_ge(S["e_a"], g * EB + (b + 1))
                    act.wait_ge(S["e_w"], g * (3 * EB) + (3 * b + 1))
                    f_(gel[b % 2], psum[:, b % 2, :], ACT.Gelu_apprx_tanh).then_inc(S["e_gel"], 1)
                    act.wait_ge(S[f"v_in{b}"], g * 16 + 16)
                    act.wait_ge(S["e_o"], g * DC + 1)
                    f_(vhl[par][0][:, b, :], vst[b], ACT.Copy).then_inc(S["v_hi"], 1)
                    if more and b % 2:
                        u_high(b // 2, g * 16 + 32, g * EB + (b + 1))

            u_high(0, 16)
            u_high(1, 16)
            with act.Fori(0, GROUPS // 2 - 1) as i:
                gelu_group(i * 2, 0)
                gelu_group(i * 2 + 1, 1)
            gelu_group(GROUPS - 2, 0)
            gelu_group(GROUPS - 1, 1, more=False)

        @block.vector
        def _(dve):
            n_step = 0

            def settle(ins):
                nonlocal n_step
                n_step += 1
                ins.then_inc(S["dve_step"], 1)
                dve.wait_ge(S["dve_step"], n_step)

            stt = dve.scalar_tensor_tensor

            def normed(k, width, src, weight, dst=None):
                dve.wait_ge(S["std_ready"], 2 * k + 2)
                settle(dve.reciprocal(rstd[:, 0, 0:width], rstd[:, 0, 0:width]))
                for c in range(DC):
                    stt((dst or uT)[:, c, 0:width], src[:, c, :], weight[:, c:c + 1], rstd[:, 0, 0:width],
                        ALU.mult, ALU.mult).then_inc(S["u_ready"], 1)

            dve.wait_ge(S["small_in"], 16 * SMALL)
            normed(0, T, hT, col_an)

            for f in range(12):
                dve.wait_ge(S["proj_taken"], f + 1)
                if f >= 2:
                    dve.wait_ge(S["qkv_ready"], f - 1)
                x, o = cin[:, f % 2, :], ctmp[:, f % 2, :]
                settle(dve.tensor_scalar(o, x[:, 0:T], col_conv[:, f, 0:1], None, ALU.mult))
                for k in range(1, CONV_K):
                    ins = stt(o, x[:, k:k + T], col_conv[:, f, k:k + 1], o, ALU.mult, ALU.add)
                    if k < CONV_K - 1:
                        settle(ins)
                ins.then_inc(S["conv_done"], 1)

            def head_scale(f, src, first, scale):
                dve.wait_ge(S["l2_std"], first + f + 1)
                settle(dve.reciprocal(rstd[:, f % 2, 0:T], rstd[:, f % 2, 0:T]))
                return stt(src[:, f, 0:T], src[:, f, 0:T], scale, rstd[:, f % 2, 0:T], ALU.mult, ALU.mult)

            for f in range(2 * GH):
                head_scale(f, qkvT, 0, GD ** -0.5 if f < GH else 1.0).then_inc(S["l2_done"], 1)

            dve.wait_ge(S["proj_taken"], 30)
            settle(dve.tensor_scalar(graw[0:NG, :], graw[0:NG, :], col_gb[0:NG, 0:1], None, ALU.add))
            stt(gabs[0:NG, :], graw[0:NG, :], -1.0, graw[0:NG, :], ALU.mult, ALU.max).then_inc(S["gate_y"], 2)
            dve.wait_ge(S["gate_act"], 3)
            stt(gabs[0:ROW_A, :], graw[0:ROW_A, :], 0.0, gln[0:ROW_A, :], ALU.min, ALU.subtract).then_inc(S["gate_y"], 1)
            settle(stt(gln[ROW_A:NG, :], graw[ROW_A:NG, :], 0.0, gln[ROW_A:NG, :], ALU.max, ALU.add))
            dve.tensor_scalar(gates[ROW_A:NG, 0:T], gln[ROW_A:NG, :], col_al[ROW_A:NG, 0:1], -1.0,
                              ALU.mult, ALU.mult).then_inc(S["gate_done"], 1)
            settle(dve.tensor_scalar(gln[0:FH, :], gabs[0:FH, :], 0.0, 1.0, ALU.mult, ALU.add))
            dve.wait_ge(S["gate_y"], 3)
            dve.tensor_tensor_scan(csum, gln[0:FH, :], gabs[0:FH, :], 0.0, ALU.mult, ALU.subtract).then_inc(S["x_csum"], 1)

            flat = lambda a: a.rearrange("p h t -> p (h t)")
            wide = lambda a: a.unsqueeze(1).to_broadcast([P, GH, P])
            per_head = lambda a: a.unsqueeze(2).to_broadcast([P, GH, P])
            dve.wait_ge(S["x_csum"], 1)
            dve.wait_ge(S["gate_tok"], NT)
            with dve.Fori(0, NT) as m:
                beta = gtok[:, bass.ds(m, 1), ROW_B:ROW_B + GH].rearrange("p o h -> p (o h)")
                dve.wait_ge(S["g_pre"], m + 1)
                dve.tensor_copy(E[:, :, :], wide(const("ident"))).then_inc(S["g_init"], 1)
                dve.tensor_copy(Dm[:, :, :], wide(const("ident"))).then_inc(S["g_init"], 1)
                dve.wait_ge(S["g_exp"], m * 4 + 4)
                for h in range(GH):
                    stt(amat[:, h], psum[:, 0, h * P:(h + 1) * P], beta[:, h:h + 1], expD[:, h], ALU.mult,
                        ALU.mult).then_inc(S["g_amat"], 1)
                dve.tensor_tensor(flat(qkT), psum[:, 1, :], flat(expT), ALU.mult).then_inc(S["g_prep"], 1)
                dve.tensor_tensor(flat(qs), flat(qc), flat(egrow), ALU.mult).then_inc(S["g_prep"], 1)
                dve.wait_ge(S["g_tok"], m * 2 + 2)
                dve.tensor_tensor(kdec[:, :, :], ktok[:, :, :], per_head(ecol[:, 4:8]), ALU.mult).then_inc(S["g_prep"], 1)
                dve.wait_ge(S["g_prep"], m * 4 + 1)
                dve.tensor_tensor(qkT[:, :, :], qkT[:, :, :], wide(const("upto")), ALU.mult).then_inc(S["g_prep"], 1)
                dve.wait_ge(S["g_init"], m * 2 + 2)
                for lev in range(LEVELS):
                    dve.wait_ge(S["g_y"], m * LEVELS + lev + 1)
                    if lev:
                        dve.wait_ge(S["g_lv"], m * 2 * LEVELS + 2 * lev)
                    dve.tensor_tensor(flat(E), flat(E), psum[:, 3, :], ALU.add).then_inc(S["g_lv"], 1)
                    dve.tensor_tensor(flat(Dm), flat(Dm), psum[:, 4, :], ALU.add).then_inc(S["g_lv"], 1)
                dve.wait_ge(S["g_ks"], m + 1)
                dve.tensor_tensor(res[:, :, :], psum[:, 5, :].rearrange("p (h t) -> p h t", h=GH),
                                  per_head(ecol[:, 0:4]), ALU.mult).then_inc(S["g_res"], 1)
                dve.wait_ge(S["g_res"], m * 2 + 1)
                dve.tensor_tensor(flat(res), flat(vtok), flat(res), ALU.subtract).then_inc(S["g_res"], 1)
                dve.wait_ge(S["g_res"], m * 2 + 2)
                dve.tensor_tensor(res[:, :, :], res[:, :, :], per_head(beta), ALU.mult).then_inc(S["g_r"], 1)
                dve.wait_ge(S["g_fin"], m + 2)
                for h in range(GH):
                    stt(state[:, h], state[:, h], ecol[:, 8 + h:9 + h], psum[:, 0, h * P:(h + 1) * P], ALU.mult,
                        ALU.add).then_inc(S["g_state"], 1)

            o_all = qkvT[:, 2 * GH:3 * GH, :]
            for f in range(GH):
                settle(head_scale(f, o_all, 2 * GH, col_gn[:, 0:1]))
                dve.tensor_tensor(mT[:, f, :], o_all[:, f, 0:T], zT[:, f, :], ALU.mult).then_inc(S["l2_done"], 1)

            dve.wait_ge(S["g_state"], GH * (NT + 1))
            step = 0
            done = []

            def output(s):
                h, m, rows = done[s]
                lo, hi = (h % 2) * FD, (h % 2) * FD + FD
                dve.wait_ge(S["x_o"], s + 1)
                dve.tensor_copy(mT[lo:hi, GH + h // 2, m * P:m * P + rows], psum[lo:hi, 6, 0:rows]
                                ).then_inc(S["x_oc"], 1)

            for h in range(FH):
                dve.wait_ge(S["x_cbc"], h + 1)
                for m in range(NT):
                    rows = P if m < NT - 1 else LAST
                    keys = m * P + rows
                    s = sc[0:rows, step % 2, 0:keys]
                    dve.wait_ge(S["x_s"], step + 1)
                    if step >= 2:
                        dve.wait_ge(S["x_t"], step - 1)
                    for j in range(-(-keys // 512)):
                        kk = min(512, keys - j * 512)
                        settle(stt(s[:, j * 512:j * 512 + kk], psum[0:rows, j, 0:kk], FD ** -0.5,
                                   cb[0:rows, h % 2, j * 512:j * 512 + kk], ALU.mult, ALU.add))
                    diag = s[:, m * P:keys]
                    ins = dve.tensor_tensor(diag, diag, const("causal")[0:rows, 0:rows], ALU.add)
                    settle(ins)
                    settle(dve.tensor_reduce(mx[0:rows, step % 2:step % 2 + 1], s, AX, ALU.max))
                    dve.tensor_scalar(mx[0:rows, step % 2:step % 2 + 1], mx[0:rows, step % 2:step % 2 + 1], -1.0, None,
                                      ALU.mult).then_inc(S["x_exp"], 1)
                    dve.engine_nop().then_inc(S["x_sc"], 1)
                    dve.wait_ge(S["x_exp"], 2 * step + 2)
                    settle(dve.reciprocal(rs[0:rows, step % 2:step % 2 + 1], rs[0:rows, step % 2:step % 2 + 1]))
                    dve.tensor_scalar(s, s, rs[0:rows, step % 2:step % 2 + 1], None, ALU.mult).then_inc(S["x_nrm"], 1)
                    done.append((h, m, rows))
                    output(step)
                    step += 1

            def residual(f, lane, ready, dst):
                dve.wait_ge(S["out_done"], ready)
                for j in range(2):
                    a = dst[:, j * HALF:(j + 1) * HALF]
                    ins = dve.tensor_tensor(a, a, psum[:, 2 * lane + j, 0:HALF], ALU.add)
                ins.then_inc(S["res_done"], 1)

            dve.wait_ge(S["mod_done"], MODS)
            settle(dve.tensor_tensor(mod[:, :], psum[:, 7, 0:MODS], mod_b[:, :], ALU.add))
            dve.engine_nop().then_inc(S["mod_ready"], 1)
            for f in range(DC):
                residual(f, f % 2, f + 1, hT[:, f, :])
            normed(1, T, hT, col_fn)

            dve.engine_nop().then_inc(S["ffn_hid"], 2)
            with dve.Fori(0, FC // 2) as i:
                for k in range(2):
                    dve.wait_ge(S["ffn_sil"], i * 2 + k + 1)
                    for j in range(2):
                        ins = dve.tensor_tensor(hid[:, bass.ds(i * 2 + k, 1), j * HALF:(j + 1) * HALF].rearrange("p o t -> p (o t)"),
                                                sil[:, k, j * HALF:(j + 1) * HALF],
                                                psum[:, 4 + 2 * k + j, 0:HALF], ALU.mult)
                    ins.then_inc(S["ffn_hid"], 1)
            with dve.Fori(0, 4) as i:
                for k in range(2):
                    residual(0, k, i * 2 + DC + k + 1,
                             hT[:, bass.ds(i * 2 + k, 1), :].rearrange("p o t -> p (o t)"))

            dve.wait_ge(S["res_done"], 2 * DC)
            dve.wait_ge(S["std_ready"], 5)
            settle(dve.reciprocal(r2[:, 0, :], r2[:, 0, :]))
            for c in range(DC):
                stt(xT2[:, c, :], xT2[:, c, :], col_ln[:, c:c + 1], r2[:, 0, :], ALU.mult, ALU.mult).then_inc(S["x2_ready"], 1)

            def modulated(k, weight, scale):
                settle(stt(amp[:, k, :], mod[:, scale:scale + DC], 1.0, weight[:, :], ALU.add, ALU.mult))
                dve.wait_ge(S["std_ready"], 6 + k)
                settle(dve.reciprocal(r2[:, 0, :], r2[:, 0, :]))
                for c in range(DC):
                    stt(u2[:, c, :], xT2[:, c, :], amp[:, k, c:c + 1], r2[:, 0, :], ALU.mult, ALU.mult).then_inc(S["u_ready"], 1)

            dve.wait_ge(S["x2_ready"], DC)
            modulated(0, col_n1, DC)

            dve.wait_ge(S["posi_in"], 16)
            settle(dve.tensor_copy(angT, posi.bitcast(I32)))
            settle(dve.tensor_scalar(angT, angT, const("freq"), None, ALU.mult))
            parts, rest = [], TWO_PI
            for _ in range(2):
                m, e = np.frexp(rest)
                parts.append(float(np.round(m * 2048) / 2048 * 2.0 ** e))
                rest -= parts[-1]
            parts.append(rest)
            for dst, lead in ((sinT, 0.0), (cosT, 0.25)):
                settle(dve.tensor_scalar(kf, angT, 1.0 / TWO_PI, lead, ALU.mult, ALU.add))
                settle(dve.tensor_scalar(kf, kf, 1.5 * 2.0 ** 23, None, ALU.add))
                settle(dve.tensor_scalar(kf, kf, -1.5 * 2.0 ** 23, None, ALU.add))
                settle(stt(dst, kf, -parts[0], angT, ALU.mult, ALU.add))
                settle(stt(dst, kf, -parts[1], dst, ALU.mult, ALU.add))
                settle(stt(dst, kf, -parts[2], dst, ALU.mult, ALU.add))
                settle(dve.tensor_scalar(dst, dst, lead * TWO_PI, 3.1415925, ALU.add, ALU.min))
                settle(dve.tensor_scalar(dst, dst, -3.1415925, None, ALU.max))
            settle(dve.memset(prod[:, :, 0:CK2 - 1], 0.0))
            dve.engine_nop().then_inc(S["tab"], 1)

            for j in range(8):
                f = 5 + SC + j
                if j < 5:
                    dve.wait_ge(S["qk_std"], j + 1)
                    settle(dve.reciprocal(sq2[:, j % 2, :], sq2[:, j % 2, :]))
                    g = col_qk[:, 0:1] if j < 4 else col_qk[:, 1:2]
                    stt(qkr[:, j, :], qkr[:, j, :], g, sq2[:, j % 2, :], ALU.mult, ALU.mult).then_inc(S["qk_n"], 1)
                if 2 <= j < 7:
                    r = j - 2
                    dve.wait_ge(S["qk_rot"], r + 1)
                    dve.wait_ge(S["tab_sin"], 2)
                    dve.tensor_tensor(tm2[:, j % 2, :], psum[:, 6 + j % 2, :], sinT, ALU.mult)
                    settle(dve.tensor_tensor(qkr[:, r, :], qkr[:, r, :], cosT, ALU.mult))
                    dve.tensor_tensor(qkr[:, r, :], qkr[:, r, :], tm2[:, j % 2, :], ALU.add).then_inc(S["qk_done"], 1)
                if j < 4:
                    dve.wait_ge(S["cv_cc"], j + 1)
                    x = prod[:, j % 2, :]
                    ins = dve.tensor_tensor(x[:, CK2 - 1:], cc[:, j % 2, :], psum[:, 2 + f % 2, :], ALU.mult)
                    ins.then_inc(S["p2_taken"], 1)
                    dve.wait_ge(S["p2_taken"], f + 1)
                    y = y2[:, j, :]
                    settle(dve.tensor_scalar(y, x[:, 0:SEC], col_cv2[:, j, 0:1], None, ALU.mult))
                    settle(stt(y, x[:, 1:1 + SEC], col_cv2[:, j, 1:2], y, ALU.mult, ALU.add))
                    settle(stt(y, x[:, 2:2 + SEC], col_cv2[:, j, 2:3], y, ALU.mult, ALU.add))
                else:
                    dve.wait_ge(S["p2_ready"], f + 1)
                    dve.tensor_tensor(mix[:, j, :], psum[:, f % 2, :], y2[:, j - 4, :], ALU.mult).then_inc(S["p2_taken"], 1)
            dve.wait_ge(S["p2_taken"], 5 + SC + 8)
            dve.engine_nop().then_inc(S["mix_cv"], 4)

            for s in range(SC * KV):
                n, kv = divmod(s, KV)
                lo, hi = kv * AD, (kv + 1) * AD
                k0 = P if n == 0 else 0
                w = 2 * P - k0
                mine = sink[:, kv * PER:(kv + 1) * PER]
                if s:
                    dve.wait_ge(S["a_t"], s)
                dve.wait_ge(S["a_s"], s + 1)
                two = psum[:, 0:2, :].rearrange("p b (i k) -> p (b i) k", i=2)[:, :, k0:]
                mask = const("window")[:, k0:].unsqueeze(1).to_broadcast([P, PER, w])
                dve.tensor_tensor(ex[:, :, k0:], two, mask, ALU.add).then_inc(S["a_sc"], 1)
                dve.wait_ge(S["a_sc"], s + 1)
                settle(dve.tensor_reduce(mxs[:, :], ex[:, :, k0:], AX, ALU.max))
                settle(stt(mxs[:, :], mxs[:, :], AD ** -0.5, mine, ALU.mult, ALU.max))
                dve.tensor_scalar(nms[:, :], mxs[:, :], -1.0, None, ALU.mult).then_inc(S["a_exp"], 1)
                dve.tensor_tensor(ess[:, :], mine, mxs[:, :], ALU.subtract).then_inc(S["a_exp"], 1)
                dve.wait_ge(S["a_e"], s + 1)
                settle(dve.tensor_tensor(rss[:, :], rss[:, :], ess[:, :], ALU.add))
                settle(dve.reciprocal(rss[:, :], rss[:, :]))
                dve.tensor_tensor(ex[:, :, k0:], ex[:, :, k0:], rss[:, :].unsqueeze(2).to_broadcast([P, PER, w]),
                                  ALU.mult).then_inc(S["a_p"], 1)
                dve.wait_ge(S["a_o"], s + 1)
                dve.tensor_copy(mix[lo:hi, 0:PER, n * P:(n + 1) * P],
                                psum[lo:hi, 4 + kv, :].rearrange("p (i q) -> p i q", i=PER)).then_inc(S["a_oc"], 1)

            for g in range(2):
                dve.wait_ge(S["m_std"], g + 1)
                settle(dve.reciprocal(r2[:, g, :], r2[:, g, :]))
                for c in range(4 * g, 4 * g + 4):
                    stt(mix[:, c, :], mix[:, c, :], col_mix[:, c:c + 1], r2[:, g, :], ALU.mult, ALU.mult).then_inc(S["m_done"], 1)
            for f in range(DC):
                dve.wait_ge(S["out2_done"], f + 1)
                stt(xT2[:, f, :], psum[:, f % 2, :], mod[:, 2 * DC + f:2 * DC + f + 1], xT2[:, f, :], ALU.mult,
                    ALU.add).then_inc(S["res2_done"], 1)
            modulated(1, col_n2, 4 * DC)
            for c in range(DC):
                dve.wait_ge(S["h2_hi"], c + 1)
                dve.tensor_tensor(h2lo[:, c, :], u2[:, c, :], h2hi[:, c, :], ALU.subtract).then_inc(S["h2_split"], 1)

            STAGES = 10
            with dve.Fori(0, PH) as h:
                units = [(p, t) for p in range(2) for t in range(SC)]

                def hold(name, value, k):
                    dve.wait_ge(S[name], value)
                    dve.memset(gate_dve[:, k:k + 1], 0.0)

                done = lambda n: hold("tk", h * STAGES + n, n) if n < 7 else dve.wait_ge(S["tk"], h * STAGES + n)
                hold("sc_taken", h * 2 + 2, 0)
                for p, t in units:
                    ins = dve.max(val[:, p, t, 0:8], scb[:, p, t, :])
                ins.then_inc(S["tk"], 1)
                done(1)
                for p, t in units:
                    dve.max_index(idu[:, p, t, 0:8].bitcast(U32), val[:, p, t, 0:8], scb[:, p, t, :])
                for p, t in units:
                    ins = dve.match_replace(scr[:, p, t, :], val[:, p, t, 0:8], scb[:, p, t, :], LOW)
                ins.then_inc(S["tk_free"], 1)
                hold("tk_free", h + 1, 7)
                for p, t in units:
                    ins = dve.max(val[:, p, t, 8:16], scr[:, p, t, :])
                ins.then_inc(S["tk"], 1)
                done(2)
                for p, t in units:
                    dve.max_index(idu[:, p, t, 8:16].bitcast(U32), val[:, p, t, 8:16], scr[:, p, t, :])
                ins = dve.tensor_tensor(cand[:, :, :].rearrange("p t (a b) -> p t a b", a=TOP),
                                        val[:, 0].unsqueeze(3).to_broadcast([P, SC, TOP, TOP]),
                                        val[:, 1].unsqueeze(2).to_broadcast([P, SC, TOP, TOP]), ALU.add)
                ins.then_inc(S["tk"], 1)
                done(3)
                for t in range(SC):
                    ins = dve.max(best[:, t, 0:8], cand[:, t, :])
                ins.then_inc(S["tk"], 1)
                done(4)
                for t in range(SC):
                    dve.max_index(posu[:, t, 0:8].bitcast(U32), best[:, t, 0:8], cand[:, t, :])
                for t in range(SC):
                    ins = dve.match_replace(cand2[:, t, :], best[:, t, 0:8], cand[:, t, :], LOW)
                ins.then_inc(S["tk"], 1)
                done(5)
                for t in range(SC):
                    ins = dve.max(best[:, t, 8:16], cand2[:, t, :])
                ins.then_inc(S["tk"], 1)
                done(6)
                for t in range(SC):
                    dve.max_index(posu[:, t, 8:16].bitcast(U32), best[:, t, 8:16], cand2[:, t, :])
                dve.tensor_tensor(ebest[:, :, :], best[:, :, :], best[:, :, 0:1].to_broadcast([P, SC, TOP]),
                                  ALU.subtract).then_inc(S["tk_top"], 1)
                dve.wait_ge(S["tk_top"], h + 1)
                pu = posu[:, :, :].rearrange("p a b -> p (a b)").bitcast(U32)
                ph, pl = (a[:, :, :].rearrange("p a b -> p (a b)") for a in (posh, posl))
                dve.tensor_single_scalar(ph.bitcast(U32), pu, 4, ALU.logical_shift_right)
                dve.tensor_single_scalar(pl.bitcast(U32), pu, 15, ALU.bitwise_and).then_inc(S["tk"], 1)
                done(7)
                dve.tensor_copy(ph, ph.bitcast(U32))
                dve.tensor_copy(pl, pl.bitcast(U32))
                dve.tensor_copy(idf[:, :, :, :].rearrange("p a b c -> p (a b c)"),
                                idu[:, :, :, :].rearrange("p a b c -> p (a b c)").bitcast(U32)).then_inc(S["tk"], 1)
                done(8)
                io16 = const("iota")[:, 0:TOP].unsqueeze(1).to_broadcast([P, SC * TOP, TOP])
                for p, pos in enumerate((ph, pl)):
                    dve.tensor_tensor(eq[:, p], io16, pos.unsqueeze(2).to_broadcast([P, SC * TOP, TOP]),
                                      ALU.is_equal).then_inc(S["tk_pos"], 1)
                dve.wait_ge(S["tk_exp"], h + 1)
                dve.tensor_reduce(esum[:, :], ebest[:, :, :], AX, ALU.add).then_inc(S["tk"], 1)
                done(9)
                dve.reciprocal(esum[:, :], esum[:, :]).then_inc(S["tk"], 1)
                done(10)
                dve.tensor_tensor(tok[:, 0, :, bass.ds(h * TOP, TOP)], ebest[:, :, :],
                                  esum[:, :].unsqueeze(2).to_broadcast([P, SC, TOP]), ALU.mult).then_inc(S["tk_gate"], 1)
                for p in range(2):
                    dve.wait_ge(S["tk_eq"], h * 2 + 1 + p)
                    dve.tensor_reduce(tok[:, 1 + p, :, bass.ds(h * TOP, TOP)],
                                      eq[:, p].rearrange("p (a b) k -> p a b k", a=SC), AX, ALU.add).then_inc(S["tk_sel"], 1)

            dve.wait_ge(S["gij_in"], 3)
            for t in range(SC):
                with dve.Fori(0, 32 // RING) as i:
                    for k in range(RING):
                        dve.wait_ge(S["dense_mm"], i * RING + (32 * t + k + 1))
                        for hot, a, sig in ((hotA, 1, "hot_i"), (hotB, 2, "hot_j")):
                            col = gij[:, a, bass.ds(i * (4 * RING) + (P * t + 4 * k), 4)]
                            dve.tensor_tensor(hot[:, k].rearrange("p (q i) -> p q i", q=4),
                                              const("iota").unsqueeze(1).to_broadcast([P, 4, P]),
                                              col.unsqueeze(2).to_broadcast([P, 4, P]), ALU.is_equal).then_inc(S[sig], 1)

            def u_low(k, hi):
                dve.wait_ge(S["u_hi"], hi)
                dve.tensor_tensor(uhl[k][1][:, :, :], ust[k][:, :, :], uhl[k][0][:, :, :], ALU.subtract).then_inc(S["u_lo"], 1)

            def gated(g, par, more=True):
                for b in range(EB):
                    dve.wait_ge(S["e_gel"], g * EB + (b + 1))
                    dve.wait_ge(S[f"g_in{b}"], g * 16 + 16)
                    dve.tensor_tensor(wf[b % 2], gel[b % 2], gst[b], ALU.mult).then_inc(S["e_w"], 1)
                    dve.wait_ge(S["e_o"], g * DC + 1)
                    dve.wait_ge(S["e_w"], g * (3 * EB) + (3 * b + 7))
                    dve.tensor_copy(whl[par][0][:, b, :], wf[b % 2]).then_inc(S["e_w"], 1)
                    dve.wait_ge(S["e_w"], g * (3 * EB) + (3 * b + 8))
                    dve.tensor_tensor(whl[par][1][:, b, :], wf[b % 2], whl[par][0][:, b, :], ALU.subtract).then_inc(S["e_w"], 1)
                    if more and b % 2:
                        u_low(b // 2, g * 2 + (2 + b // 2 + 1))

            def gather(g):
                for f in range(DC):
                    dve.wait_ge(S["e_o"], g * DC + (DC + f + 2))
                    dve.wait_ge(S["e_acc"], g * DC + 2)
                    dve.tensor_tensor(acc[:, f, :], acc[:, f, :], psum[:, 2 + f % 2, :], ALU.add).then_inc(S["e_acc"], 1)

            dve.wait_ge(S["acc_zero"], 1)
            u_low(0, 1)
            u_low(1, 2)
            gated(0, 0)
            with dve.Fori(0, GROUPS // 2 - 1) as i:
                gated(i * 2 + 1, 1)
                gather(i * 2)
                gated(i * 2 + 2, 0)
                gather(i * 2 + 1)
            gated(GROUPS - 1, 1, more=False)
            gather(GROUPS - 2)
            gather(GROUPS - 1)
            dve.wait_ge(S["e_acc"], GROUPS * DC + 2)
            for c in range(DC):
                stt(acc[:, c, :], acc[:, c, :], mod[:, 5 * DC + c:5 * DC + c + 1], xT2[:, c, :], ALU.mult,
                    ALU.add).then_inc(S["stored"], 1)


def kernel(**inputs):
    import numpy as _np
    import concourse.bacc as _bacc
    from concourse import mybir as _mybir
    from concourse.bass_utils import run_bass_kernel_spmd as _run

    a = {k: _np.asarray(v) for k, v in inputs.items()}
    heads = lambda x, axis: _np.moveaxis(
        _np.moveaxis(x, axis, 0).reshape((KV, PER, AD) + _np.moveaxis(x, axis, 0).shape[1:]).swapaxes(0, 1).reshape(
            _np.moveaxis(x, axis, 0).shape), 0, axis)
    w_in2 = a["w_in_2"][0]
    w_out2 = a["w_out_2"][0]
    aw = AH * AD
    packed = {
        "consts": _np.concatenate(list(constants().values()), axis=1).astype(_np.float32),
        "xT": a["x"][0].T, "metaT": a["meta_tokens"].T,
        "attn_norm_w": a["attn_norm_w"][0], "ffn_norm_w": a["ffn_norm_w"][0], "final_norm_w": a["final_norm_w"],
        "conv_w": a["conv_w"][0], "gdn_norm_w": a["gdn_norm_w"][0], "fgate_b": a["fgate_b"][0],
        "dt_bias": a["dt_bias"][0], "a_log": a["a_log"][0], "w_in": a["w_in"][0], "w_out": a["w_out"][0],
        "w_gate": a["w_gate"][0], "w_up": a["w_up"][0], "w_down": a["w_down"][0],
        "c": a["c_2"][0], "positions": a["positions_2"][0], "ada_w": a["ada_w_2"][0], "ada_b": a["ada_b_2"][0],
        "norm1_g": a["norm1_g_2"][0], "norm2_g": a["norm2_g_2"][0],
        "w_in2": _np.concatenate([heads(w_in2[:, :aw], 1), w_in2[:, aw:]], axis=1),
        "q_norm_g": a["q_norm_g_2"][0], "k_norm_g": a["k_norm_g_2"][0], "sinks": a["sinks_2"][0],
        "conv_w2": a["conv_w_2"][0],
        "mix_g": _np.concatenate([heads(a["attn_out_g_2"][0], 0), a["conv_out_g_2"][0]]),
        "w_out2": _np.concatenate([heads(w_out2[:aw], 0), w_out2[aw:]], axis=0),
        "wq": a["peer_wq_2"][0],
        "subk": a["peer_subkeys_2"][0].reshape(2 * PH, PK, P).transpose(0, 2, 1),
        "uT": a["peer_u_2"][0].T, "v": a["peer_v_2"][0],
    }
    nc = _bacc.Bacc("TRN2", target_bir_lowering=False, num_devices=1)
    arrays, io = {}, {}
    for name, x in packed.items():
        x = _np.ascontiguousarray(x)
        arrays[f"in_{name}"] = x
        io[name] = nc.dram_tensor(f"in_{name}", x.shape, _mybir.dt.from_np(x.dtype), kind="ExternalInput").ap()
    io["dense"] = nc.dram_tensor("dense_gates", (PK, P, SEC), F32, kind="Internal").ap()
    io["out"] = nc.dram_tensor("out_dram", (D, SEC), F32, kind="ExternalOutput").ap()
    program(nc, io)
    r = _run(nc, [arrays], core_ids=[0])
    return _np.ascontiguousarray(r.results[0]["out_dram"].T)[None]
```

```python
from contextlib import ExitStack

import numpy as np
import concourse.bass as bass
from concourse import mybir

F32 = mybir.dt.float32
BF16 = mybir.dt.bfloat16
I32 = mybir.dt.int32
U32 = mybir.dt.uint32
ALU = mybir.AluOpType
ACT = mybir.ActivationFunctionType
AX = mybir.AxisListType.X

P = 128
D = 1024
DC = D // P
META = 16
SEQ = 512
T = META + SEQ
HALF = T // 2
NT = -(-T // P)
TP = NT * P
LAST = T - (NT - 1) * P
GH, GD = 4, 128
FH, FD = 8, 64
CONV_K = 4
FF = 2816
FC = FF // P
EPS = 1e-6
NEG = -1e30
LEVELS = 7
SLOT = 4096
ROW_B, ROW_A = 32, 64
NG = ROW_A + GH
SEC = 512
MODS = 6 * DC
AH, AD, KV = 8, 64, 2
PER = AH // KV
SC = SEC // P
CW = 512
CK2 = 3
PH, PK, TOP = 8, 128, 16
EB = 4
GROUPS = PK // EB
TWO_PI = 2 * np.pi
RING = 4
LOW = -3.0e38
SMALL = 14 + 13
F_MOD, F_OUT, F_GU, F_DOWN = 7, 19, 21, 32
F_Q2, F_KV2, F_CU2, F_CB2, F_OUT2, F_WQ = 40, 41, 42, 44, 45, 47


def constants():
    i = np.arange(P)
    parts = {}
    parts["ident"] = np.eye(P)
    parts["upto"] = (i[:, None] <= i[None, :])
    parts["after"] = (i[:, None] > i[None, :])
    parts["ones"] = np.ones((P, P))
    parts["mean_d"] = np.full((P, P), 1.0 / D)
    parts["mean_head"] = np.full((P, P), 1.0 / GD)
    parts["causal"] = np.where(i[:, None] >= i[None, :], 0.0, NEG)
    for lev in range(LEVELS):
        b = 1 << lev
        m = (i[:, None] // (2 * b) == i[None, :] // (2 * b)) & (i[:, None] % (2 * b) >= b) & (i[None, :] % (2 * b) < b)
        parts[f"merge{lev}"] = -m.astype(np.float64)
    pick = np.zeros((P, FH, P))
    for h in range(FH):
        pick[h, h, :] = 1.0
    same = i[:, None] // AD == i[None, :] // AD
    parts["mean_ah"] = same / AD
    parts["mean_mix"] = np.full((P, P), 1.0 / CW)
    lo = i % AD < AD // 2
    turn = np.zeros((P, P))
    for d in range(P):
        turn[d + AD // 2 if lo[d] else d - AD // 2, d] = -1.0 if lo[d] else 1.0
    parts["turn"] = turn
    j = np.arange(2 * P)
    seen = (j[None, :] > i[:, None]) & (j[None, :] <= i[:, None] + P)
    parts["window"] = np.where(seen, 0.0, NEG)
    parts["iota"] = np.tile(i[None, :], (P, 1))
    freq = (10000.0 ** (-np.arange(0, AD, 2, dtype=np.float32) / np.float32(AD))).astype(np.float32)
    parts["freq"] = np.tile(freq, P // freq.size)[:, None]
    parts["pick"] = pick.reshape(P, FH * P)
    return parts


def const_places():
    at, places = 0, {}
    for name, a in constants().items():
        places[name] = (at, a.shape[1])
        at += a.shape[1]
    return places, at


def program(nc, io):
    places, n_const = const_places()
    ctx = ExitStack()
    with ctx:
        def sem(name):
            return ctx.enter_context(nc.semaphore(name))

        cst = ctx.enter_context(nc.sbuf_tensor("cst", [P, n_const], F32))

        def const(name, rows=P):
            a, n = places[name]
            return cst[0:rows, a:a + n]

        arena_floats = 53200 - n_const - 64
        arena = ctx.enter_context(nc.sbuf_tensor("arena", [P, arena_floats], F32))
        top = [0]

        def carve(*dims):
            n = int(np.prod(dims))
            a = arena[:, top[0]:top[0] + n]
            top[0] += n
            assert top[0] <= arena_floats, (top[0], arena_floats)
            if len(dims) == 2:
                a = a.rearrange("p (a b) -> p a b", a=dims[0])
            if len(dims) == 3:
                a = a.rearrange("p (a b c) -> p a b c", a=dims[0], b=dims[1])
            return a

        psum = ctx.enter_context(nc.psum_tensor("psum", [P, 8, 512], F32))

        hT = carve(DC, T)
        cact = carve(DC)
        mod_b, mod = carve(MODS), carve(MODS)
        col_n1, col_n2 = carve(DC), carve(DC)
        col_mix = carve(DC)
        col_qk = carve(2)
        col_cv2 = carve(CW // P, CK2)
        sink = carve(AH)
        gate_dve = carve(8)
        amp = carve(2, DC)
        eps = carve(1)
        col_an, col_fn, col_ln = carve(DC), carve(DC), carve(DC)
        col_conv = carve(12, CONV_K)
        col_gn = carve(1)
        col_gb = carve(1)
        col_al = carve(1)
        base0 = top[0]
        slot = [carve(SLOT), carve(SLOT)]
        base1 = top[0]
        uT = carve(DC, T)
        qkvT = carve(3 * GH, TP)
        zT = carve(GH, T)
        fqk = carve(8, T)
        fv = carve(NT, FH * FD)
        mT = carve(DC, T)
        over_rstd = top[0]
        rstd = carve(2, TP)
        gates = carve(TP)
        gtok = carve(NT, NG)
        csum = carve(T)[0:FH, :]
        base2 = top[0]
        smallw = carve(DC, NG)
        cin = carve(2, CONV_K - 1 + T)
        ctmp = carve(2, T)
        graw = carve(T)
        gabs = carve(T)
        gln = carve(T)
        end_a = top[0]

        top[0] = base1
        rhsD, rhsU, expD, expT, egrow = (carve(GH, P) for _ in range(5))
        nm = carve(2, GH * P)
        ecol = carve(12)
        assert top[0] <= base1 + DC * T
        top[0] = base2
        ktok, vtok, amat, qkT, qs, kdec, E, Dm, Pm, state = (carve(GH, P) for _ in range(10))
        cb = carve(2, T)
        sc = carve(3, T)
        pT = carve(2, NT * P)
        mx = carve(3)
        rs = carve(3)
        end_g = top[0]
        top[0] = over_rstd
        vnew, res = carve(GH, P), carve(GH, P)
        assert top[0] <= over_rstd + 2 * TP
        top[0] = base1 + DC * T
        hid = carve(FC, T)
        sil = carve(2, T)

        xT2 = hT[:, :, META:T]
        top[0] = base1
        u2 = carve(DC, SEC)
        r2 = carve(2, SEC)
        keep = top[0]
        qkr = carve(5, SEC)
        vt2 = carve(SC, P)
        cosT, sinT, angT, kf = (carve(SEC) for _ in range(4))
        ki = kf.bitcast(I32)
        posi = carve(SEC)
        prod = carve(2, SEC + CK2 - 1)
        cc = carve(2, SEC)
        y2 = carve(CW // P, SEC)
        mix = carve(DC, SEC)
        sq2 = carve(2, SEC)
        tm2 = carve(2, SEC)
        ex = carve(PER, 2 * P)
        pT2 = carve(2, PER * P)
        mxs, nms, rss, ess = (carve(PER) for _ in range(4))
        top[0] = keep
        subk = carve(2 * PH, P)
        qf = carve(2, SEC)
        scb, scr = carve(2, SC, P), carve(2, SC, P)
        val = carve(2, SC, TOP)
        idu = carve(2, SC, TOP)
        idf = carve(2, SC, TOP)
        cand = carve(SC, TOP * TOP)
        cand2 = carve(SC, TOP * TOP)
        best = carve(SC, TOP)
        posu = carve(SC, TOP)
        posh, posl = carve(SC, TOP), carve(SC, TOP)
        eq = carve(2, SC * TOP, TOP)
        ebest = carve(SC, TOP)
        esum = carve(SC)
        tok = carve(3, SC, P)
        choice_end = top[0]
        top[0] = arena_floats - (DC * SEC + 3 * SEC)
        assert choice_end <= top[0], (choice_end, top[0])
        gij = carve(3, SEC)
        h2hi = carve(DC * SEC // 2).bitcast(BF16).rearrange("p (c t) -> p c t", c=DC)
        h2lo = carve(DC * SEC // 2).bitcast(BF16).rearrange("p (c t) -> p c t", c=DC)
        top[0] = base0
        dense = [carve(PK, P), carve(PK, P)]
        hotA, hotB = carve(RING, 4 * P), carve(RING, 4 * P)
        assert top[0] <= arena_floats - (DC * SEC + 3 * SEC), top[0]
        top[0] = base0
        acc = carve(DC, SEC)
        ust = [carve(DC, 2 * P) for _ in range(2)]
        uhl = [[carve(DC * P).bitcast(BF16).rearrange("p (c e) -> p c e", c=DC) for _ in range(2)] for _ in range(2)]
        assert top[0] - base0 <= PK * P
        vst = [carve(D) for _ in range(4)]
        vhl = [[carve(EB * D // 2).bitcast(BF16).rearrange("p (b f) -> p b f", b=EB) for _ in range(2)] for _ in range(2)]
        gst = [carve(SEC) for _ in range(4)]
        gel = [carve(SEC) for _ in range(2)]
        wf = [carve(SEC) for _ in range(2)]
        whl = [[carve(EB * SEC // 2).bitcast(BF16).rearrange("p (b t) -> p b t", b=EB) for _ in range(2)] for _ in range(2)]
        assert top[0] <= arena_floats - (DC * SEC + 3 * SEC), top[0]

        S = {n: sem(n) for n in (
            "const_in", "h_in", "small_in", "landed0", "landed1",
            "sq_ready", "ms_ready", "std_ready", "u_ready", "dve_step", "pool_step",
            "proj_ready", "proj_taken", "conv_done", "qkv_ready",
            "l2_sq", "l2_ms", "l2_std", "l2_done",
            "gate_y", "gate_act", "gate_done", "gate_T", "gate_tok",
            "g_rhs", "g_pre", "g_diff", "g_tok", "g_exp", "g_amat", "g_nm", "g_init", "g_prep",
            "g_p", "g_pc", "g_y", "g_lv", "g_ks", "g_res", "g_r", "g_v", "g_vc", "g_o", "g_oc", "g_state", "g_fin",
            "x_cb", "x_cbc", "x_s", "x_sc", "x_max", "g_d1", "g_d2", "x_exp", "x_nrm", "x_t", "x_tc", "x_o", "x_oc", "x_csum",
            "out_done", "res_done", "ffn_ps", "ffn_sil", "ffn_hid", "final_done",
            "cact_ready", "mod_done", "mod_ready", "shifted", "x2_ready",
            "p2_ready", "p2_taken", "tab", "tab_sin", "qk_sq", "qk_ms", "qk_std", "qk_n", "qk_rot", "qk_done",
            "cv_prod", "cv_y", "mix_cv", "a_s", "a_sc", "a_exp", "a_p", "a_t", "a_tc", "a_o", "a_oc",
            "m_sq", "m_ms", "m_std", "m_done", "out2_done", "res2_done", "h2_split", "posi_in", "sub_in",
            "wq_done", "wq_taken", "sc_done", "sc_taken", "tk", "tk_free", "tk_scores", "tk_cand", "tk_exp", "tk_pos", "tk_top", "tk_gate", "h2_hi", "cv_cc", "a_e",
            "tk_eq", "tk_sel", "acc_zero", "gij_T", "gij_in", "hot_i", "hot_j", "hot_a", "dense_mm", "dense_in", "dense_out0", "dense_out1",
            "u_in0", "u_in1", "u_hi", "u_lo", "v_in0", "v_in1", "v_in2", "v_in3", "v_hi", "v_lo", "g_in0", "g_in1", "g_in2", "g_in3", "e_a", "e_gel", "e_w", "e_o", "e_acc", "stored",
        )}

        def W(name):
            return S[name]

        def fill_done(n):
            return S[f"landed{n % 2}"], 32 * (n // 2 + 1)

        STEPS = FH * NT
        PIECES = [(m, what) for m in range(NT) for what in ["pre", "decay", *range(LEVELS), "recall", "values", "output"]]

        def slots():
            k = 0
            for m, what in PIECES:
                if what == "decay" or isinstance(what, int):
                    yield m, what, k
                    k += 1
                else:
                    yield m, what, None
            for k in range(STEPS, STEPS + 4):
                yield None, None, k

        def fox(s):
            h, m = divmod(s, NT)
            rows = P if m < NT - 1 else LAST
            return h, m, rows, m * P + rows

        def pair(f):
            return [psum[:, 2 * (f % 2), 0:HALF], psum[:, 2 * (f % 2) + 1, 0:HALF]]

        def slot_cols(n, width=512):
            return slot[n % 2][:, 0:DC * width].rearrange("p (c n) -> p c n", c=DC)

        NPROJ = 30

        block = ctx.enter_context(nc.Block())

        @block.sync
        def _(sp):
            sp.dma_start(cst[:, :], io["consts"]).then_inc(S["const_in"], 16)
            for c in range(DC):
                sp.dma_start(hT[:, c, 0:META], io["metaT"][c * P:(c + 1) * P, :]).then_inc(S["h_in"], 16)
                sp.dma_start(hT[:, c, META:T], io["xT"][c * P:(c + 1) * P, :]).then_inc(S["h_in"], 16)
            cols = lambda name: io[name].rearrange("(c p) -> p c", p=P)
            with nc.allow_non_contiguous_dma(reason="small vectors"):
                sp.dma_start(col_an[:, :], cols("attn_norm_w")).then_inc(S["small_in"], 16)
                sp.dma_start(col_fn[:, :], cols("ffn_norm_w")).then_inc(S["small_in"], 16)
                sp.dma_start(col_ln[:, :], cols("final_norm_w")).then_inc(S["small_in"], 16)
                for k in range(CONV_K):
                    sp.dma_start(col_conv[:, :, k], io["conv_w"][k, :].rearrange("(c p) -> p c", p=P)
                                 ).then_inc(S["small_in"], 16)
                sp.dma_start(col_gn[:, :], cols("gdn_norm_w")).then_inc(S["small_in"], 16)
                sp.dma_start(cact[:, :], cols("c")).then_inc(S["small_in"], 16)
                sp.dma_start(mod_b[:, :], cols("ada_b")).then_inc(S["small_in"], 16)
                sp.dma_start(col_n1[:, :], cols("norm1_g")).then_inc(S["small_in"], 16)
                sp.dma_start(col_n2[:, :], cols("norm2_g")).then_inc(S["small_in"], 16)
                sp.dma_start(col_mix[:, :], cols("mix_g")).then_inc(S["small_in"], 16)
                for k in range(2):
                    rows = slice(k * AD, (k + 1) * AD)
                    sp.dma_start(col_qk[rows, 0:1], io["q_norm_g"].rearrange("(p o) -> p o", o=1)).then_inc(S["small_in"], 16)
                    sp.dma_start(col_qk[rows, 1:2], io["k_norm_g"].rearrange("(p o) -> p o", o=1)).then_inc(S["small_in"], 16)
                for k in range(CK2):
                    sp.dma_start(col_cv2[:, :, k], io["conv_w2"][k, :].rearrange("(c p) -> p c", p=P)).then_inc(S["small_in"], 16)
                sp.dma_start(sink[:, :], io["sinks"].rearrange("(o h) -> o h", o=1).to_broadcast([P, AH])).then_inc(S["small_in"], 16)
                sp.wait_ge(S["pool_step"], 3)
                sp.dma_start(col_gb[0:FH, :], io["fgate_b"].rearrange("(p o) -> p o", o=1)).then_inc(S["small_in"], 16)
                sp.dma_start(col_gb[ROW_A:ROW_A + GH, :], io["dt_bias"].rearrange("(p o) -> p o", o=1)).then_inc(S["small_in"], 16)
                sp.dma_start(col_al[ROW_A:ROW_A + GH, :], io["a_log"].rearrange("(p o) -> p o", o=1)).then_inc(S["small_in"], 16)
                w = io["w_in"].rearrange("(c p) n -> p c n", p=P)
                c_b = 4 * GH * GD
                c_f = w.shape[2] - FH
                sp.dma_start(smallw[:, :, 0:FH], w[:, :, c_f:c_f + FH]).then_inc(S["small_in"], 16)
                sp.dma_start(smallw[:, :, ROW_B:ROW_B + GH], w[:, :, c_b:c_b + GH]).then_inc(S["small_in"], 16)
                sp.dma_start(smallw[:, :, ROW_A:ROW_A + GH], w[:, :, c_b + GH:c_b + 2 * GH]).then_inc(S["small_in"], 16)

            def fill(n, parts, reader, count):
                if reader:
                    sp.wait_ge(S[reader], count)
                for dst, src in parts:
                    sp.dma_start(dst, src).then_inc(S[f"landed{n % 2}"], 16)

            def halves(n, src, width=512):
                dst = slot_cols(n, width)
                return [(dst[:, 0:4, :], src[:, 0:4, :]), (dst[:, 4:8, :], src[:, 4:8, :])]

            wf = 4 * GH * GD + 2 * GH
            for n in range(7):
                c0 = n * 512 if n < 4 else wf + (n - 4) * 512
                fill(n, halves(n, w[:, :, c0:c0 + 512]), "proj_ready" if n >= 2 else None, 4 * (n - 1))
            wo = io["w_out"].rearrange("(c p) n -> p c n", p=P)
            aw = io["ada_w"].rearrange("(c p) n -> p c n", p=P)
            for k in range(12):
                reader, count = ("proj_ready", 24 + k * NT) if k < 2 else ("mod_done", 4 * (k - 1))
                fill(F_MOD + k, halves(F_MOD + k, aw[:, :, k * 512:(k + 1) * 512]), reader, count)
            for k in range(2):
                fill(F_OUT + k, halves(F_OUT + k, wo[:, :, k * 512:(k + 1) * 512]), "mod_done", 44 + 4 * k)
            wg = io["w_gate"].rearrange("(c p) n -> p c n", p=P)
            wu = io["w_up"].rearrange("(c p) n -> p c n", p=P)

            def gate_up(n, cols):
                dst = slot[n % 2].rearrange("p (g c n) -> p g c n", g=2, c=DC)
                return [(dst[:, 0], wg[:, :, cols]), (dst[:, 1], wu[:, :, cols])]

            for k in range(2):
                fill(F_GU + k, gate_up(F_GU + k, slice(k * 256, k * 256 + 256)), "out_done", 4 * k + 4)
            with sp.Fori(0, 4) as i:
                for k in range(2):
                    fill(F_GU + 2 + k, gate_up(F_GU + 2 + k, bass.ds(i * 512 + (2 + k) * 256, 256)), "ffn_ps", i * 4 + 2 * k + 2)
            fill(F_GU + 10, gate_up(F_GU + 10, slice(2560, 2816)), "ffn_ps", 18)
            wd = io["w_down"].rearrange("(c p) n -> p c n", p=P)

            def down(n, cols):
                dst = slot[n % 2][:, 0:FC * P].rearrange("p (c n) -> p c n", c=FC)
                return [(dst[:, 0:11], wd[:, 0:11, cols]), (dst[:, 11:22], wd[:, 11:22, cols])]

            for k in range(2):
                fill(F_DOWN + k, down(F_DOWN + k, slice(k * P, k * P + P)), "ffn_ps", 20 + 2 * k)
            with sp.Fori(0, 3) as i:
                for k in range(2):
                    fill(F_DOWN + 2 + k, down(F_DOWN + 2 + k, bass.ds(i * 256 + (2 + k) * P, P)), "out_done", i * 2 + DC + k + 1)


            sp.wait_ge(S["x2_ready"], DC)
            sp.dma_start(posi.bitcast(I32), io["positions"].rearrange("(o t) -> o t", o=1).to_broadcast([P, SEC])).then_inc(S["posi_in"], 16)
            w2 = io["w_in2"].rearrange("(c p) n -> p c n", p=P)
            fill(F_Q2, halves(F_Q2, w2[:, :, 0:512]), "out_done", 2 * DC - 1)
            fill(F_KV2, halves(F_KV2, w2[:, :, 512:768], 256), "out_done", 2 * DC)
            c_cb, c_cc, c_cu = 768, 768 + CW, 768 + 2 * CW
            for k in range(2):
                dst = slot[(F_CU2 + k) % 2].rearrange("p (g c n) -> p g c n", g=2, c=DC)
                o = k * 256
                fill(F_CU2 + k, [(dst[:, 0], w2[:, :, c_cc + o:c_cc + o + 256]), (dst[:, 1], w2[:, :, c_cu + o:c_cu + o + 256])],
                     "p2_ready", 4 if k == 0 else 5 + SC)
            fill(F_CB2, halves(F_CB2, w2[:, :, c_cb:c_cb + 512]), "p2_ready", 5 + SC + 2)
            wo2 = io["w_out2"].rearrange("(c p) n -> p c n", p=P)
            for k in range(2):
                fill(F_OUT2 + k, halves(F_OUT2 + k, wo2[:, :, k * 512:(k + 1) * 512]), "p2_ready", 5 + SC + 4 * (k + 1))
            wq = io["wq"].rearrange("(c p) n -> p c n", p=P)
            for k in range(4):
                reader, count = ("out2_done", 4 * (k + 1)) if k < 2 else ("wq_done", 4 * (k - 1))
                fill(F_WQ + k, halves(F_WQ + k, wq[:, :, k * 512:(k + 1) * 512]), reader, count)
                if k == 0:
                    sp.wait_ge(S["m_done"], DC)
                    sp.dma_start(subk[:, :, :], io["subk"].rearrange("u p k -> p u k")).then_inc(S["sub_in"], 16)

            ut = io["uT"].rearrange("(c p) e -> p c e", p=P)
            for t in range(SC):
                if t == SC - 1:
                    sp.wait_ge(S["dense_out0"], 64 * SC // 2)
                    for k in range(2):
                        sp.dma_start(ust[k][:, :, :], ut[:, :, k * 2 * P:(k + 1) * 2 * P]).then_inc(S[f"u_in{k}"], 16)
                sp.wait_ge(S["dense_in"], 32 * (t + 1) + RING)
                for q in range(4):
                    sp.dma_start(io["dense"][q * 32:(q + 1) * 32, :, t * P:(t + 1) * P].rearrange("i j t -> j i t"),
                                 dense[t % 2][:, q * 32:(q + 1) * 32, :]).then_inc(S[f"dense_out{t % 2}"], 16)

            vt = io["v"].rearrange("(b p) f -> b p f", p=P)
            sp.wait_ge(S["dense_out0"], 64 * SC // 2)
            sp.wait_ge(S["dense_out1"], 64 * SC // 2)

            def load_group(g, first):
                if not first:
                    for k in range(2):
                        sp.wait_ge(S["u_lo"], g * 2 + k - 1)
                        sp.dma_start(ust[k][:, :, :], ut[:, :, bass.ds(g * (EB * P) + k * 2 * P, 2 * P)]).then_inc(S[f"u_in{k}"], 16)
                for b in range(EB):
                    if not first:
                        sp.wait_ge(S["e_w"], g * (3 * EB) + (3 * (b - EB) + 1 + 6))
                    sp.dma_start(gst[b], io["dense"][bass.ds(g * EB + b, 1), :, :].rearrange("o j t -> (o j) t")).then_inc(S[f"g_in{b}"], 16)
                    if not first:
                        sp.wait_ge(S["v_lo"], g * EB + (b - EB + 1))
                    sp.dma_start(vst[b], vt[bass.ds(g * EB + b, 1), :, :].rearrange("o p f -> (o p) f")).then_inc(S[f"v_in{b}"], 16)

            load_group(0, True)
            with sp.Fori(1, GROUPS) as g:
                load_group(g, False)
            for c in range(DC):
                sp.wait_ge(S["stored"], c + 1)
                sp.dma_start(io["out"][c * P:(c + 1) * P, :], acc[:, c, :]).then_inc(S["final_done"], 16)
            sp.wait_ge(S["final_done"], 16 * DC)

        @block.gpsimd
        def _(pool):
            n_step = 0

            def step(ins):
                nonlocal n_step
                n_step += 1
                ins.then_inc(S["pool_step"], 1)

            step(pool.memset(col_gb[:, :], 0.0))
            step(pool.memset(col_al[:, :], 0.0))
            step(pool.memset(smallw[:, :, :], 0.0))
            step(pool.memset(eps[:, :], EPS))
            step(pool.memset(cin[:, :, 0:CONV_K - 1], 0.0))
            step(pool.memset(qkvT[:, :, T:TP], 0.0))
            step(pool.memset(gates[:, :], 0.0))
            assert n_step == 7

            pool.wait_ge(S["gate_tok"], NT)
            pool.wait_ge(S["l2_done"], 2 * GH)
            pool.wait_ge(S["x_csum"], 1)
            pool.memset(state[:, :, :], 0.0).then_inc(S["g_state"], GH)
            heads = lambda a: a.unsqueeze(1).to_broadcast([P, GH, P])

            def decay_sides(m):
                gb = gtok[:, m, ROW_A:ROW_A + GH].unsqueeze(2).to_broadcast([P, GH, P])
                if m:
                    pool.wait_ge(S["g_diff"], m)
                pool.tensor_tensor(rhsD[:, :, :], heads(const("after")), gb, ALU.mult).then_inc(S["g_rhs"], 1)
                pool.tensor_tensor(rhsU[:, :, :], heads(const("upto")), gb, ALU.mult).then_inc(S["g_rhs"], 1)

            decay_sides(0)
            for m in range(NT):
                pool.wait_ge(S["g_amat"], m * GH + GH)
                for lev in range(LEVELS):
                    n = m * LEVELS + lev
                    if n >= 2:
                        pool.wait_ge(S["g_p"], n - 1)
                    pool.tensor_tensor(nm[:, n % 2, :].rearrange("p (h t) -> p h t", h=GH), amat[:, :, :],
                                       heads(const(f"merge{lev}")), ALU.mult).then_inc(S["g_nm"], 1)
                if m + 1 < NT:
                    decay_sides(m + 1)

            pool.wait_ge(S["x_csum"], 1)
            pool.engine_nop().then_inc(S["dense_mm"], RING)
            pool.engine_nop().then_inc(S["dense_in"], RING)
            pool.engine_nop().then_inc(S["e_w"], 6)
            pool.engine_nop().then_inc(S["e_o"], DC + 1)
            pool.engine_nop().then_inc(S["e_acc"], 2)

            pool.wait_ge(S["tab"], 1)
            with pool.Fori(0, PH) as h:
                for p in range(2):
                    pool.wait_ge(S["tk_pos"], h * 2 + p + 1)
                    e4 = eq[:, p].rearrange("p (a b) k -> p a b k", a=SC)
                    pool.tensor_tensor(e4, e4, idf[:, p].unsqueeze(2).to_broadcast([P, SC, TOP, TOP]),
                                       ALU.mult).then_inc(S["tk_eq"], 1)

            pool.wait_ge(S["gij_in"], 3)
            for t in range(SC):
                with pool.Fori(0, 32 // RING) as i:
                    for k in range(RING):
                        pool.wait_ge(S["hot_i"], i * RING + (32 * t + k + 1))
                        at = i * (4 * RING) + (P * t + 4 * k)
                        a4 = hotA[:, k].rearrange("p (q i) -> p q i", q=4)
                        pool.tensor_tensor(a4, a4, gij[:, 0, bass.ds(at, 4)].unsqueeze(2).to_broadcast([P, 4, P]),
                                           ALU.mult).then_inc(S["hot_a"], 1)

            pool.wait_ge(S["dense_out0"], 64 * SC // 2)
            pool.memset(acc[:, :, :], 0.0).then_inc(S["acc_zero"], 1)
            pool.wait_ge(S["dense_out1"], 64 * SC // 2)
            with pool.Fori(0, GROUPS // 2) as i:
                for par in range(2):
                    for b in range(EB):
                        n = i * (2 * EB) + (par * EB + b)
                        pool.wait_ge(S["v_hi"], n + 1)
                        pool.tensor_tensor(vhl[par][1][:, b, :], vst[b], vhl[par][0][:, b, :], ALU.subtract).then_inc(S["v_lo"], 1)

        @block.tensor
        def _(pe):
            mm = pe.matmul
            pe.wait_ge(S["const_in"], 16)

            def mean_square(k, width, banks):
                for c in range(DC):
                    pe.wait_ge(S["sq_ready"], DC * k + c + 1)
                    for j, out in enumerate(banks):
                        last = mm(out, const("mean_d"), uT[:, c, j * width:(j + 1) * width],
                                  start=c == 0, stop=c == DC - 1)
                last.then_inc(S["ms_ready"], 1)

            mean_square(0, HALF, [psum[:, 6, 0:HALF], psum[:, 7, 0:HALF]])

            pe.wait_ge(S["u_ready"], DC)
            for f in range(24):
                n, k = divmod(f, 4)
                if k == 0:
                    pe.wait_ge(*fill_done(n))
                if f >= 2:
                    pe.wait_ge(S["proj_taken"], f - 1)
                w = slot_cols(n)
                for c in range(DC):
                    for j, out in enumerate(pair(f)):
                        last = mm(out, w[:, c, k * P:(k + 1) * P], uT[:, c, j * HALF:(j + 1) * HALF],
                                  start=c == 0, stop=c == DC - 1)
                last.then_inc(S["proj_ready"], 1)
            pe.wait_ge(*fill_done(6))
            w = slot_cols(6)
            for m in range(NT):
                f = 24 + m
                rows = P if m < NT - 1 else LAST
                pe.wait_ge(S["proj_taken"], f - 1)
                for c in range(DC):
                    last = mm(psum[0:rows, 2 * (f % 2), :], uT[:, c, m * P:m * P + rows], w[:, c, :],
                              start=c == 0, stop=c == DC - 1)
                last.then_inc(S["proj_ready"], 1)
            f = 29
            pe.wait_ge(S["proj_taken"], f - 1)
            pe.wait_ge(S["small_in"], 16 * SMALL)
            for c in range(DC):
                for j, out in enumerate(pair(f)):
                    last = mm(out[0:NG, :], smallw[:, c, :], uT[:, c, j * HALF:(j + 1) * HALF],
                              start=c == 0, stop=c == DC - 1)
            last.then_inc(S["proj_ready"], 1)

            for f in range(2 * GH):
                pe.wait_ge(S["l2_sq"], f + 1)
                if f >= 2:
                    pe.wait_ge(S["l2_std"], f - 1)
                for j in range(2):
                    last = mm(psum[:, 4 + 2 * (f % 2) + j, 0:HALF], const("ones"),
                              rstd[:, f % 2, j * HALF:(j + 1) * HALF], start=True, stop=True)
                last.then_inc(S["l2_ms"], 1)

            pe.wait_ge(S["gate_done"], 2)
            pe.wait_ge(S["proj_taken"], 30)
            for m in range(NT):
                if m >= 2:
                    pe.wait_ge(S["gate_tok"], m - 1)
                pe.transpose(psum[:, m % 2, 0:NG], gates[0:NG, m * P:(m + 1) * P],
                             const("ident")[0:NG, 0:NG]).then_inc(S["gate_T"], 1)

            pe.wait_ge(S["gate_tok"], NT)
            pe.wait_ge(S["l2_done"], 2 * GH)
            pe.wait_ge(S["x_csum"], 1)
            bank = lambda b: psum[:, b, :].rearrange("p (h t) -> p h t", h=GH)
            flat = lambda a: a.rearrange("p h t -> p (h t)")

            def delta(m, what, part):
                tile = slice(m * P, (m + 1) * P)
                k, q, v = (lambda h, b=b: qkvT[:, b + h, tile] for b in (GH, 0, 2 * GH))
                if what == "pre" and part == 0:
                    if m:
                        pe.wait_ge(S["g_oc"], m)
                        pe.wait_ge(S["g_vc"], m)
                    pe.wait_ge(S["g_state"], m * GH + GH)
                    for h in range(GH):
                        mm(bank(3)[:, h], k(h), k(h), start=True, stop=True)
                        mm(bank(4)[:, h], k(h), q(h), start=True, stop=True)
                        pe.transpose(bank(5)[:, h], k(h), const("ident"))
                        last = pe.transpose(bank(6)[:, h], v(h), const("ident"))
                    last.then_inc(S["g_pre"], 1)
                    pe.wait_ge(S["g_rhs"], m * 2 + 2)
                    mm(psum[:, 7, :], const("upto"), flat(rhsD), start=True, stop=True).then_inc(S["g_d1"], 1)
                if what == "decay" and part == 0:
                    pe.wait_ge(S["g_tok"], m * 2 + 2)
                    mm(psum[:, 5, :], const("after"), flat(rhsU), start=True, stop=True)
                    mm(psum[:, 6, :], const("ones"), flat(rhsU), start=True, stop=True).then_inc(S["g_d2"], 1)
                    pe.wait_ge(S["g_exp"], m * 4 + 1)
                    g = gtok[:, m, ROW_A:ROW_A + GH]
                    mm(psum[:, 7, 0:4], const("upto"), g, start=True, stop=True)
                    mm(psum[:, 7, 4:8], const("after"), g, start=True, stop=True)
                    mm(psum[:, 7, 8:12], const("ones"), g, start=True, stop=True).then_inc(S["g_diff"], 1)
                if isinstance(what, int):
                    n = m * LEVELS + what
                    if part == 0:
                        if what == 0:
                            pe.wait_ge(S["g_init"], m * 2 + 2)
                            pe.wait_ge(S["g_exp"], m * 4 + 4)
                        else:
                            pe.wait_ge(S["g_lv"], 2 * n)
                        pe.wait_ge(S["g_nm"], n + 1)
                        for h in range(GH):
                            last = mm(bank(5)[:, h], nm[:, n % 2, h * P:(h + 1) * P], E[:, h], start=True, stop=True)
                        last.then_inc(S["g_p"], 1)
                    else:
                        pe.wait_ge(S["g_pc"], n + 1)
                        for h in range(GH):
                            mm(bank(6)[:, h], Dm[:, h], Pm[:, h], start=True, stop=True)
                            last = mm(bank(7)[:, h], Pm[:, h], Dm[:, h], start=True, stop=True)
                        last.then_inc(S["g_y"], 1)
                if what == "recall" and part == 0:
                    for h in range(GH):
                        last = mm(bank(3)[:, h], k(h), state[:, h], start=True, stop=True)
                    last.then_inc(S["g_ks"], 1)
                if what == "values" and part == 0:
                    pe.wait_ge(S["g_r"], m + 1)
                    pe.wait_ge(S["g_lv"], (m + 1) * 2 * LEVELS)
                    pe.wait_ge(S["g_prep"], m * 4 + 4)
                    for h in range(GH):
                        last = mm(bank(4)[:, h], E[:, h], res[:, h], start=True, stop=True)
                    last.then_inc(S["g_v"], 1)
                if what == "output" and part == 0:
                    pe.wait_ge(S["g_vc"], m + 1)
                    for h in range(GH):
                        last = mm(bank(6)[:, h], kdec[:, h], vnew[:, h], start=True, stop=True)
                    last.then_inc(S["g_fin"], 1)
                    for h in range(GH):
                        mm(bank(5)[:, h], state[:, h], qs[:, h], start=True, stop=False)
                        last = mm(bank(5)[:, h], vnew[:, h], qkT[:, h], start=False, stop=True)
                    last.then_inc(S["g_o"], 1)

            def mod_tile(f):
                n, k = divmod(f, 4)
                if k == 0:
                    pe.wait_ge(*fill_done(F_MOD + n))
                if f == 0:
                    pe.wait_ge(S["cact_ready"], 1)
                w = slot_cols(F_MOD + n)
                for c in range(DC):
                    last = mm(psum[:, 2, 256 + f:257 + f], w[:, c, k * P:(k + 1) * P], cact[:, c:c + 1],
                              start=c == 0, stop=c == DC - 1)
                last.then_inc(S["mod_done"], 1)

            def attend_scores(s):
                h, m, rows, keys = fox(s)
                lo, hi = (h % 2) * FD, (h % 2) * FD + FD
                if s:
                    pe.wait_ge(S["x_sc"], s)
                if m in (0, NT - 1) and s >= 3:
                    pe.wait_ge(S["x_tc"], s - 2)
                if m == 0:
                    pick = const("pick", FH)[:, h * P:(h + 1) * P]
                    mm(psum[:, 0, :], pick, csum[:, 0:512], start=True, stop=True)
                    mm(psum[:, 1, 0:T - 512], pick, csum[:, 512:T], start=True, stop=True).then_inc(S["x_cb"], 1)
                    pe.wait_ge(S["x_cbc"], h + 1)
                q = fqk[lo:hi, h // 2, m * P:m * P + rows]
                first = min(512, keys)
                last = mm(psum[0:rows, 0, 0:first], q, fqk[lo:hi, 4 + h // 2, 0:first], start=True, stop=True)
                if keys > 512:
                    last = mm(psum[0:rows, 1, 0:keys - 512], q, fqk[lo:hi, 4 + h // 2, 512:keys], start=True, stop=True)
                last.then_inc(S["x_s"], 1)

            def attend_turn(s):
                h, m, rows, keys = fox(s)
                pe.wait_ge(S["x_nrm"], s + 1)
                pe.wait_ge(S["x_sc"], min(s + 3, STEPS))
                if s:
                    pe.wait_ge(S["x_tc"], s)
                for j in range(m + 1):
                    kr = P if j < NT - 1 else LAST
                    last = pe.transpose(psum[0:kr, 1, j * rows:(j + 1) * rows], sc[0:rows, s % 3, j * P:j * P + kr],
                                        const("ident")[0:rows, 0:rows])
                last.then_inc(S["x_t"], 1)

            def attend_out(s):
                h, m, rows, keys = fox(s)
                lo, hi = (h % 2) * FD, (h % 2) * FD + FD
                pe.wait_ge(S["x_tc"], s + 1)
                for j in range(m + 1):
                    kr = P if j < NT - 1 else LAST
                    last = mm(psum[lo:hi, 2, 0:rows], fv[0:kr, j, h * FD:(h + 1) * FD],
                              pT[0:kr, s % 2, j * rows:(j + 1) * rows], start=j == 0, stop=j == m)
                last.then_inc(S["x_o"], 1)

            single = 2 * STEPS - MODS
            for m, what, s in slots():
                if m is not None:
                    delta(m, what, 0)
                if s is not None and s < STEPS:
                    attend_scores(s)
                if m is not None:
                    delta(m, what, 1)
                if s is not None:
                    if 0 <= s - 2 < STEPS:
                        attend_turn(s - 2)
                    if s >= 4:
                        pe.wait_ge(S["x_oc"], s - 3)
                    if s < STEPS:
                        for f in ([s] if s < single else [2 * s - single, 2 * s - single + 1]):
                            mod_tile(f)
                    if 0 <= s - 3 < STEPS:
                        attend_out(s - 3)

            pe.wait_ge(S["g_oc"], NT)
            pe.wait_ge(S["g_state"], GH * (NT + 1))
            for f in range(GH):
                pe.wait_ge(S["l2_sq"], 2 * GH + f + 1)
                if f >= 2:
                    pe.wait_ge(S["l2_std"], 2 * GH + f - 1)
                for j in range(2):
                    last = mm(psum[:, 4 + 2 * (f % 2) + j, 0:HALF], const("mean_head"),
                              rstd[:, f % 2, j * HALF:(j + 1) * HALF], start=True, stop=True)
                last.then_inc(S["l2_ms"], 1)

            pe.wait_ge(S["x_oc"], STEPS)
            pe.wait_ge(S["l2_done"], 3 * GH)
            pe.wait_ge(S["mod_ready"], 1)
            for f in range(8):
                n, k = F_OUT + f // 4, f % 4
                if k == 0:
                    pe.wait_ge(*fill_done(n))
                if f >= 2:
                    pe.wait_ge(S["res_done"], f - 1)
                w = slot_cols(n)
                for c in range(DC):
                    for j, out in enumerate(pair(f)):
                        last = mm(out, w[:, c, k * P:(k + 1) * P], mT[:, c, j * HALF:(j + 1) * HALF],
                                  start=c == 0, stop=c == DC - 1)
                last.then_inc(S["out_done"], 1)

            mean_square(1, HALF, [psum[:, 6, 0:HALF], psum[:, 7, 0:HALF]])
            pe.wait_ge(S["u_ready"], 2 * DC)
            pe.wait_ge(S["std_ready"], 4)

            def gate_up_tile(w, k, before):
                if before is not None:
                    pe.wait_ge(S["ffn_hid"], before)
                for g in range(2):
                    for c in range(DC):
                        for j in range(2):
                            last = mm(psum[:, 4 * g + 2 * (k % 2) + j, 0:HALF], w[:, g, c, k % 2 * P:(k % 2 + 1) * P],
                                      uT[:, c, j * HALF:(j + 1) * HALF], start=c == 0, stop=c == DC - 1)
                last.then_inc(S["ffn_ps"], 1)

            def gate_up_fill(n, landed, first_tile):
                w = slot[n % 2].rearrange("p (g c n) -> p g c n", g=2, c=DC)
                pe.wait_ge(S[f"landed{n % 2}"], landed)
                for k in range(2):
                    last = gate_up_tile(w, k, first_tile + k - 1)
    
            with pe.Fori(0, 5) as i:
                for k in range(2):
                    gate_up_fill(F_GU + k, i * 32 + fill_done(F_GU + k)[1], i * 4 + 2 + 2 * k)
            gate_up_fill(F_GU + 10, fill_done(F_GU + 10)[1], FC)
            pe.wait_ge(S["ffn_hid"], FC + 2)

            with pe.Fori(0, 4) as i:
                for k in range(2):
                    n = F_DOWN + k
                    w = slot[n % 2][:, 0:FC * P].rearrange("p (c n) -> p c n", c=FC)
                    pe.wait_ge(S[f"landed{n % 2}"], i * 32 + fill_done(n)[1])
                    pe.wait_ge(S["res_done"], i * 2 + DC + k - 1)
                    for c in range(FC):
                        for j in range(2):
                            last = mm(psum[:, 2 * k + j, 0:HALF], w[:, c, :], hid[:, c, j * HALF:(j + 1) * HALF],
                                      start=c == 0, stop=c == FC - 1)
                    last.then_inc(S["out_done"], 1)
        
            def mean_square2(k):
                for c in range(DC):
                    pe.wait_ge(S["sq_ready"], DC * k + c + 1)
                    last = mm(psum[:, 6, :], const("mean_d"), u2[:, c, :], start=c == 0, stop=c == DC - 1)
                last.then_inc(S["ms_ready"], 1)

            mean_square2(2)
            mean_square2(3)

            def product(bank, w, cols, src, sig):
                for c in range(DC):
                    last = mm(psum[:, bank, :], w[:, c, cols], src[:, c, :], start=c == 0, stop=c == DC - 1)
                if sig:
                    last.then_inc(S[sig], 1)

            pe.wait_ge(S["shifted"], DC)
            for f in range(5):
                n, k = (F_Q2, f) if f < 4 else (F_KV2, 0)
                if k == 0:
                    pe.wait_ge(*fill_done(n))
                if f >= 2:
                    pe.wait_ge(S["p2_taken"], f - 1)
                product(f % 2, slot_cols(n, 512 if f < 4 else 256), slice(k * P, (k + 1) * P), u2, "p2_ready")
            w = slot_cols(F_KV2, 256)
            for t in range(SC):
                f = 5 + t
                pe.wait_ge(S["p2_taken"], f - 1)
                for c in range(DC):
                    last = mm(psum[:, f % 2, 0:P], u2[:, c, t * P:(t + 1) * P], w[:, c, P:2 * P],
                              start=c == 0, stop=c == DC - 1)
                last.then_inc(S["p2_ready"], 1)
            def conv_products(q, base):
                j = q // 2 if q < 8 else q - 4
                f = 5 + SC + j
                if q < 8:
                    n = F_CU2 + j // 2
                    if q % 4 == 0:
                        pe.wait_ge(*fill_done(n))
                    w = slot[n % 2].rearrange("p (g c n) -> p g c n", g=2, c=DC)
                    if q % 2 == 0:
                        pe.wait_ge(S["p2_taken"], f if j == 3 else f - 1)
                    product(base[q % 2], w[:, q % 2], slice(j % 2 * P, (j % 2 + 1) * P), u2,
                            "p2_ready" if q % 2 else None)
                else:
                    if j == 4:
                        pe.wait_ge(*fill_done(F_CB2))
                    pe.wait_ge(S["p2_taken"], f if j == 4 else f - 1)
                    product(base[j % 2], slot_cols(F_CB2), slice((j - 4) * P, (j - 3) * P), u2, "p2_ready")

            for j in range(7):
                if j < 5:
                    pe.wait_ge(S["qk_sq"], j + 1)
                    mm(psum[:, 4 + j % 2, :], const("mean_ah"), sq2[:, j % 2, :], start=True, stop=True).then_inc(S["qk_ms"], 1)
                if 2 <= j:
                    pe.wait_ge(S["qk_n"], j - 1)
                    if j >= 4:
                        pe.wait_ge(S["qk_done"], j - 3)
                    mm(psum[:, 6 + j % 2, :], const("turn"), qkr[:, j - 2, :], start=True, stop=True).then_inc(S["qk_rot"], 1)
                if j < 4:
                    f = 5 + SC + j // 2
                    conv_products(j, (f % 2, 2 + f % 2))

            def window_scores(s):
                n, kv = divmod(s, KV)
                lo, hi = kv * AD, (kv + 1) * AD
                k0 = P if n == 0 else 0
                if s:
                    pe.wait_ge(S["a_sc"], s)
                for i in range(PER):
                    last = mm(psum[:, i // 2, (i % 2) * 256 + k0:(i % 2) * 256 + 256], qkr[lo:hi, i, n * P:(n + 1) * P],
                              qkr[lo:hi, 4, (n - 1) * P + k0:(n + 1) * P], start=True, stop=True)
                last.then_inc(S["a_s"], 1)

            pe.wait_ge(S["qk_done"], 5)
            pe.wait_ge(S["p2_taken"], 5 + SC + 2)
            window_scores(0)
            for s in range(SC * KV):
                n, kv = divmod(s, KV)
                lo, hi = kv * AD, (kv + 1) * AD
                k0 = P if n == 0 else 0
                conv_products(4 + s, (6, 7))
                pe.wait_ge(S["a_p"], s + 1)
                if s:
                    pe.wait_ge(S["a_tc"], s)
                for i in range(PER):
                    for kb in range(k0 // P, 2):
                        last = pe.transpose(psum[:, 2 + kb, i * P:(i + 1) * P], ex[:, i, kb * P:(kb + 1) * P], const("ident"))
                last.then_inc(S["a_t"], 1)
                if s + 1 < SC * KV:
                    window_scores(s + 1)
                pe.wait_ge(S["a_tc"], s + 1)
                if s >= 2:
                    pe.wait_ge(S["a_oc"], s - 1)
                for kb in range(k0 // P, 2):
                    tile = n - 1 + kb
                    last = mm(psum[lo:hi, 4 + kv, :], vt2[:, tile, lo:hi], pT2[:, kb, :], start=kb == k0 // P, stop=kb == 1)
                last.then_inc(S["a_o"], 1)

            pe.wait_ge(S["a_oc"], SC * KV)
            pe.wait_ge(S["p2_taken"], 5 + SC + 8)
            for c in range(DC):
                pe.wait_ge(S["m_sq"], c + 1)
                last = mm(psum[:, 6 + c // 4, :], const("mean_mix"), u2[:, c, :], start=c % 4 == 0, stop=c % 4 == 3)
                if c % 4 == 3:
                    last.then_inc(S["m_ms"], 1)
            pe.wait_ge(S["m_done"], DC)
            for f in range(DC):
                n = F_OUT2 + f // 4
                if f % 4 == 0:
                    pe.wait_ge(*fill_done(n))
                if f >= 2:
                    pe.wait_ge(S["res2_done"], f - 1)
                product(f % 2, slot_cols(n), slice(f % 4 * P, (f % 4 + 1) * P), mix, "out2_done")
            mean_square2(4)

            pe.wait_ge(S["shifted"], 2 * DC)
            pe.wait_ge(S["res2_done"], DC)
            pe.wait_ge(S["sub_in"], 16)

            def scores(u):
                pe.wait_ge(S["wq_taken"], u + 1)
                if u >= 4:
                    pe.wait_ge(S["sc_taken"], u - 3)
                for t in range(SC):
                    last = mm(psum[:, 2 + u % 4, t * P:(t + 1) * P], qf[:, u % 2, t * P:(t + 1) * P], subk[:, u, :],
                              start=True, stop=True)
                last.then_inc(S["sc_done"], 1)

            for u in range(2 * PH):
                n = F_WQ + u // 4
                if u % 4 == 0:
                    pe.wait_ge(*fill_done(n))
                if u >= 2:
                    pe.wait_ge(S["wq_taken"], u - 1)
                product(u % 2, slot_cols(n), slice(u % 4 * P, (u % 4 + 1) * P), u2, "wq_done")
                if u:
                    scores(u - 1)
            scores(2 * PH - 1)

            pe.wait_ge(S["tk_sel"], 2 * PH)
            pe.wait_ge(S["tk_gate"], PH)
            pe.wait_ge(S["sc_taken"], 2 * PH)
            for a in range(3):
                for t in range(SC):
                    last = pe.transpose(psum[:, 4 + a, t * P:(t + 1) * P], tok[:, a, t, :], const("ident"))
                last.then_inc(S["gij_T"], 1)

            for t in range(SC):
                with pe.Fori(0, 32 // RING) as i:
                    for k in range(RING):
                        batch = i * RING + (32 * t + k)
                        pe.wait_ge(S["hot_j"], batch + 1)
                        pe.wait_ge(S["hot_a"], batch + 1)
                        pe.wait_ge(S["dense_in"], batch + 1)
                        for q in range(4):
                            last = mm(psum[:, k, q * P:(q + 1) * P], hotB[:, k, q * P:(q + 1) * P], hotA[:, k, q * P:(q + 1) * P],
                                      start=True, stop=True)
                        last.then_inc(S["dense_mm"], 1)

            pe.wait_ge(S["h2_split"], DC)
            pe.wait_ge(S["dense_in"], 32 * SC + RING)

            def up(g, par, first=False):
                for b in range(EB):
                    hi, lo = uhl[b // 2]
                    e = slice(b % 2 * P, (b % 2 + 1) * P)
                    if b % 2 == 0:
                        pe.wait_ge(S["u_lo"], g * 2 + (b // 2 + 1))
                    if not (first and b < 2):
                        pe.wait_ge(S["e_gel"], g * EB + (b - 1))
                    for c in range(DC):
                        mm(psum[:, b % 2, :], hi[:, c, e], h2hi[:, c, :], start=c == 0, stop=False)
                        mm(psum[:, b % 2, :], hi[:, c, e], h2lo[:, c, :], start=False, stop=False)
                        last = mm(psum[:, b % 2, :], lo[:, c, e], h2hi[:, c, :], start=False, stop=c == DC - 1)
                    last.then_inc(S["e_a"], 1)

            def down2(g, par):
                pe.wait_ge(S["e_w"], g * (3 * EB) + (3 * EB + 6))
                pe.wait_ge(S["v_lo"], g * EB + EB)
                vh, vl = vhl[par]
                wh, wl = whl[par]
                for f in range(DC):
                    pe.wait_ge(S["e_acc"], g * DC + (f + 1))
                    cols = slice(f * P, (f + 1) * P)
                    for b in range(EB):
                        mm(psum[:, 2 + f % 2, :], vh[:, b, cols], wh[:, b, :], start=b == 0, stop=False)
                        mm(psum[:, 2 + f % 2, :], vh[:, b, cols], wl[:, b, :], start=False, stop=False)
                        last = mm(psum[:, 2 + f % 2, :], vl[:, b, cols], wh[:, b, :], start=False, stop=b == EB - 1)
                    last.then_inc(S["e_o"], 1)

            up(0, 0, first=True)
            with pe.Fori(0, GROUPS // 2 - 1) as i:
                up(i * 2 + 1, 1)
                down2(i * 2, 0)
                up(i * 2 + 2, 0)
                down2(i * 2 + 1, 1)
            up(GROUPS - 1, 1)
            down2(GROUPS - 2, 0)
            down2(GROUPS - 1, 1)

        @block.scalar
        def _(act):
            f_ = act.activation

            def squares(k, src, width, before):
                for c in range(DC):
                    before(c)
                    f_(uT[:, c, 0:width], src[:, c, :], ACT.Square).then_inc(S["sq_ready"], 1)

            def std(k, banks, width):
                act.wait_ge(S["ms_ready"], k + 1)
                for j, src in enumerate(banks):
                    f_(rstd[:, 0, j * width:(j + 1) * width], src, ACT.Sqrt, bias=eps[:, 0:1]
                       ).then_inc(S["std_ready"], 1)

            squares(0, hT, T, lambda c: act.wait_ge(S["h_in"], 32 * DC))
            act.wait_ge(S["pool_step"], 7)
            act.wait_ge(S["small_in"], 16 * SMALL)
            std(0, [psum[:, 6, 0:HALF], psum[:, 7, 0:HALF]], HALF)

            f_(cact[:, :], cact[:, :], ACT.Silu).then_inc(S["cact_ready"], 1)

            def silu_conv(f):
                act.wait_ge(S["conv_done"], f + 1)
                f_(qkvT[:, f, 0:T], ctmp[:, f % 2, :], ACT.Silu).then_inc(S["qkv_ready"], 1)

            def take(f):
                act.wait_ge(S["proj_ready"], f + 1)

            for f in range(12):
                if f >= 2:
                    act.wait_ge(S["conv_done"], f - 1)
                take(f)
                o = cin[:, f % 2, CONV_K - 1:]
                f_(o[:, 0:HALF], pair(f)[0], ACT.Copy)
                f_(o[:, HALF:T], pair(f)[1], ACT.Copy).then_inc(S["proj_taken"], 1)
                if f:
                    silu_conv(f - 1)
            silu_conv(11)
            for f in range(12, 30):
                take(f)
                if f < 24:
                    dst, fn = (zT[:, f - 12, :], ACT.Silu) if f < 16 else (fqk[:, f - 16, :], ACT.Copy)
                    f_(dst[:, 0:HALF], pair(f)[0], fn)
                    f_(dst[:, HALF:T], pair(f)[1], fn).then_inc(S["proj_taken"], 1)
                elif f < 29:
                    rows = P if f < 28 else LAST
                    f_(fv[0:rows, f - 24, 0:256], psum[0:rows, 2 * (f % 2), 0:256], ACT.Copy)
                    f_(fv[0:rows, f - 24, 256:512], psum[0:rows, 2 * (f % 2), 256:512], ACT.Copy).then_inc(S["proj_taken"], 1)
                else:
                    f_(graw[0:NG, 0:HALF], pair(f)[0][0:NG, :], ACT.Copy)
                    f_(graw[0:NG, HALF:T], pair(f)[1][0:NG, :], ACT.Copy).then_inc(S["proj_taken"], 1)

            def head_square(f, src, first):
                n = first + f
                if f >= 2:
                    act.wait_ge(S["l2_done"], n - 1)
                f_(rstd[:, f % 2, 0:T], src[:, f, 0:T], ACT.Square).then_inc(S["l2_sq"], 1)

            def head_std(f, first):
                n = first + f
                act.wait_ge(S["l2_ms"], n + 1)
                for j in range(2):
                    ins = f_(rstd[:, f % 2, j * HALF:(j + 1) * HALF], psum[:, 4 + 2 * (f % 2) + j, 0:HALF], ACT.Sqrt,
                             bias=eps[:, 0:1])
                ins.then_inc(S["l2_std"], 1)

            def head_norms(count, src, first):
                head_square(0, src, first)
                for f in range(count):
                    if f + 1 < count:
                        head_square(f + 1, src, first)
                    head_std(f, first)

            act.wait_ge(S["qkv_ready"], 12)
            act.wait_ge(S["u_ready"], DC)
            head_norms(2 * GH, qkvT, 0)

            act.wait_ge(S["gate_y"], 2)
            f_(gabs[0:NG, :], gabs[0:NG, :], ACT.Exp, scale=-1.0).then_inc(S["gate_act"], 1)
            act.wait_ge(S["gate_act"], 1)
            f_(gln[0:NG, :], gabs[0:NG, :], ACT.Ln, bias=1.0).then_inc(S["gate_act"], 1)
            act.wait_ge(S["small_in"], 16 * SMALL)
            f_(col_al[0:NG, :], col_al[0:NG, :], ACT.Exp).then_inc(S["gate_act"], 1)
            act.wait_ge(S["gate_y"], 3)
            f_(gates[ROW_B:ROW_B + GH, 0:T], gabs[ROW_B:ROW_B + GH, :], ACT.Exp).then_inc(S["gate_done"], 1)

            for m in range(NT):
                act.wait_ge(S["gate_T"], m + 1)
                f_(gtok[:, m, :], psum[:, m % 2, 0:NG], ACT.Copy).then_inc(S["gate_tok"], 1)

            flat = lambda a: a.rearrange("p h t -> p (h t)")

            def delta(m, what):
                if what == "pre":
                    act.wait_ge(S["g_pre"], m + 1)
                    f_(flat(ktok), psum[:, 5, :], ACT.Copy).then_inc(S["g_tok"], 1)
                    f_(flat(vtok), psum[:, 6, :], ACT.Copy).then_inc(S["g_tok"], 1)
                    act.wait_ge(S["g_d1"], m + 1)
                    f_(flat(expD), psum[:, 7, :], ACT.Exp).then_inc(S["g_exp"], 1)
                if what == "decay":
                    act.wait_ge(S["g_d2"], m + 1)
                    f_(flat(expT), psum[:, 5, :], ACT.Exp).then_inc(S["g_exp"], 1)
                    f_(flat(egrow), psum[:, 6, :], ACT.Exp).then_inc(S["g_exp"], 1)
                    act.wait_ge(S["g_diff"], m + 1)
                    f_(ecol[:, 0:12], psum[:, 7, 0:12], ACT.Exp).then_inc(S["g_exp"], 1)
                if isinstance(what, int):
                    act.wait_ge(S["g_p"], m * LEVELS + what + 1)
                    f_(flat(Pm), psum[:, 5, :], ACT.Copy).then_inc(S["g_pc"], 1)
                if what == "values":
                    act.wait_ge(S["g_v"], m + 1)
                    f_(flat(vnew), psum[:, 4, :], ACT.Copy).then_inc(S["g_vc"], 1)
                if what == "output":
                    act.wait_ge(S["g_o"], m + 1)
                    f_(qkvT[:, 2 * GH:3 * GH, m * P:(m + 1) * P], psum[:, 5, :].rearrange("p (h t) -> p h t", h=GH),
                       ACT.Copy).then_inc(S["g_oc"], 1)

            def attend_sums(h):
                act.wait_ge(S["x_cb"], h + 1)
                if h >= 2:
                    act.wait_ge(S["x_sc"], (h - 1) * NT)
                f_(cb[:, h % 2, 0:512], psum[:, 0, :], ACT.Copy)
                f_(cb[:, h % 2, 512:T], psum[:, 1, 0:T - 512], ACT.Copy).then_inc(S["x_cbc"], 1)

            def attend_exp(s):
                h, m, rows, keys = fox(s)
                a = sc[0:rows, s % 3, 0:keys]
                act.wait_ge(S["x_max"], s + 1)
                f_(a, a, ACT.Exp, bias=mx[0:rows, s % 3:s % 3 + 1], accum_out=rs[0:rows, s % 3:s % 3 + 1]
                   ).then_inc(S["x_exp"], 1)

            def attend_turned(s):
                h, m, rows, keys = fox(s)
                act.wait_ge(S["x_t"], s + 1)
                if s >= 2:
                    act.wait_ge(S["x_o"], s - 1)
                full = min(m + 1, NT - 1)
                ins = f_(pT[:, s % 2, 0:full * rows], psum[:, 1, 0:full * rows], ACT.Copy)
                if m == NT - 1:
                    ins = f_(pT[0:LAST, s % 2, full * rows:(full + 1) * rows], psum[0:LAST, 1, full * rows:(full + 1) * rows], ACT.Copy)
                ins.then_inc(S["x_tc"], 1)

            for m, what, s in slots():
                if m is not None:
                    delta(m, what)
                if s is not None:
                    if 0 <= s - 3 < STEPS:
                        attend_turned(s - 3)
                    if s < STEPS and s % NT == 0:
                        attend_sums(s // NT)
                    if 0 <= s - 1 < STEPS:
                        attend_exp(s - 1)

            act.wait_ge(S["g_oc"], NT)
            act.wait_ge(S["g_fin"], NT)
            head_norms(GH, qkvT[:, 2 * GH:3 * GH, :], 2 * GH)

            squares(1, hT, T, lambda c: act.wait_ge(S["res_done"], DC))
            std(1, [psum[:, 6, 0:HALF], psum[:, 7, 0:HALF]], HALF)

            def silu_tile(k, ready, free):
                act.wait_ge(S["ffn_ps"], ready)
                act.wait_ge(S["ffn_hid"], free)
                for j in range(2):
                    ins = f_(sil[:, k, j * HALF:(j + 1) * HALF], psum[:, 2 * k + j, 0:HALF], ACT.Silu)
                ins.then_inc(S["ffn_sil"], 1)

            with act.Fori(0, FC // 2) as i:
                for k in range(2):
                    silu_tile(k, i * 2 + k + 1, i * 2 + k + 1)

            def squares2(k, ready, count):
                for c in range(DC):
                    act.wait_ge(S[ready], count(c))
                    f_(u2[:, c, :], xT2[:, c, :], ACT.Square).then_inc(S["sq_ready"], 1)

            def std2(k):
                act.wait_ge(S["ms_ready"], k + 1)
                f_(r2[:, 0, :], psum[:, 6, :], ACT.Sqrt, bias=eps[:, 0:1]).then_inc(S["std_ready"], 1)

            def shift(k, col):
                for c in range(DC):
                    act.wait_ge(S["u_ready"], (2 + k) * DC + c + 1)
                    f_(u2[:, c, :], u2[:, c, :], ACT.Identity, bias=mod[:, col + c:col + c + 1]).then_inc(S["shifted"], 1)

            squares2(2, "res_done", lambda c: 2 * DC)
            std2(2)
            squares2(3, "x2_ready", lambda c: c + 1)
            std2(3)
            shift(0, 0)
            for f in range(5 + SC):
                act.wait_ge(S["p2_ready"], f + 1)
                if f < 5:
                    f_(qkr[:, f, :], psum[:, f % 2, :], ACT.Copy).then_inc(S["p2_taken"], 1)
                else:
                    f_(vt2[:, f - 5, :], psum[:, f % 2, 0:P], ACT.Copy).then_inc(S["p2_taken"], 1)
            act.wait_ge(S["tab"], 1)
            f_(sinT, sinT, ACT.Sin).then_inc(S["tab_sin"], 1)
            f_(cosT, cosT, ACT.Sin).then_inc(S["tab_sin"], 1)
            act.wait_ge(S["p2_taken"], 5)

            def take_c(j, bank):
                f = 5 + SC + j
                act.wait_ge(S["p2_ready"], f + 1)
                if j >= 2:
                    act.wait_ge(S["p2_taken"], f - 1)
                f_(cc[:, j % 2, :], psum[:, bank, :], ACT.Copy).then_inc(S["cv_cc"], 1)

            for j in range(5):
                if j >= 2:
                    act.wait_ge(S["qk_n"], j - 1)
                f_(sq2[:, j % 2, :], qkr[:, j, :], ACT.Square).then_inc(S["qk_sq"], 1)
                act.wait_ge(S["qk_ms"], j + 1)
                f_(sq2[:, j % 2, :], psum[:, 4 + j % 2, :], ACT.Sqrt, bias=eps[:, 0:1]).then_inc(S["qk_std"], 1)
                if j in (1, 3):
                    take_c(j // 2, (5 + SC + j // 2) % 2)

            for s in range(SC * KV):
                n, kv = divmod(s, KV)
                lo, hi = kv * AD, (kv + 1) * AD
                k0 = P if n == 0 else 0
                act.wait_ge(S["a_exp"], 2 * s + 2)
                for i in range(PER):
                    f_(ex[:, i, k0:], ex[:, i, k0:], ACT.Exp, bias=nms[:, i:i + 1], scale=AD ** -0.5,
                       accum_out=rss[:, i:i + 1])
                f_(ess[:, :], ess[:, :], ACT.Exp).then_inc(S["a_e"], 1)
                act.wait_ge(S["a_t"], s + 1)
                if s:
                    act.wait_ge(S["a_o"], s)
                for kb in range(k0 // P, 2):
                    ins = f_(pT2[:, kb, :], psum[:, 2 + kb, :], ACT.Copy)
                ins.then_inc(S["a_tc"], 1)
                if s in (1, 3):
                    take_c(2 + s // 2, 6)

            for c in range(DC):
                act.wait_ge(S["a_oc"], SC * KV)
                act.wait_ge(S["mix_cv"], 4)
                f_(u2[:, c, :], mix[:, c, :], ACT.Square).then_inc(S["m_sq"], 1)
            for g in range(2):
                act.wait_ge(S["m_ms"], g + 1)
                f_(r2[:, g, :], psum[:, 6 + g, :], ACT.Sqrt, bias=eps[:, 0:1]).then_inc(S["m_std"], 1)

            act.wait_ge(S["m_done"], DC)
            squares2(4, "res2_done", lambda c: c + 1)
            std2(4)
            shift(1, 3 * DC)
            for c in range(DC):
                act.wait_ge(S["shifted"], DC + c + 1)
                f_(h2hi[:, c, :], u2[:, c, :], ACT.Copy).then_inc(S["h2_hi"], 1)

            def take_scores(u):
                act.wait_ge(S["sc_done"], u + 1)
                if u >= 2:
                    act.wait_ge(S["tk_free"], u // 2)
                f_(scb[:, u % 2].rearrange("p t k -> p (t k)"), psum[:, 2 + u % 4, :], ACT.Copy).then_inc(S["sc_taken"], 1)

            def gate_exp(h):
                act.wait_ge(S["tk_top"], h + 1)
                f_(ebest[:, :, :], ebest[:, :, :], ACT.Exp).then_inc(S["tk_exp"], 1)

            for u in range(2 * PH):
                act.wait_ge(S["wq_done"], u + 1)
                if u >= 2:
                    act.wait_ge(S["sc_done"], u - 1)
                f_(qf[:, u % 2, :], psum[:, u % 2, :], ACT.Copy).then_inc(S["wq_taken"], 1)
                if u:
                    take_scores(u - 1)
                if u >= 3 and u % 2:
                    gate_exp(u // 2 - 1)
            take_scores(2 * PH - 1)
            gate_exp(PH - 1)
            for a in range(3):
                act.wait_ge(S["gij_T"], a + 1)
                f_(gij[:, a, :], psum[:, 4 + a, :], ACT.Copy).then_inc(S["gij_in"], 1)

            for t in range(SC):
                if t >= 2:
                    act.wait_ge(S[f"dense_out{t % 2}"], 64 * (t // 2))
                with act.Fori(0, 32 // RING) as i:
                    for k in range(RING):
                        act.wait_ge(S["dense_mm"], i * RING + (32 * t + k + 1 + RING))
                        f_(dense[t % 2][:, :, bass.ds(i * (4 * RING) + 4 * k, 4)].rearrange("p i q -> p q i"),
                           psum[:, k, :].rearrange("p (q i) -> p q i", q=4), ACT.Copy).then_inc(S["dense_in"], 1)


            def u_high(k, landed, used=None):
                act.wait_ge(S[f"u_in{k}"], landed)
                if used is not None:
                    act.wait_ge(S["e_a"], used)
                f_(uhl[k][0][:, :, :], ust[k][:, :, :], ACT.Copy).then_inc(S["u_hi"], 1)

            def gelu_group(g, par, more=True):
                for b in range(EB):
                    act.wait_ge(S["e_a"], g * EB + (b + 1))
                    act.wait_ge(S["e_w"], g * (3 * EB) + (3 * b + 1))
                    f_(gel[b % 2], psum[:, b % 2, :], ACT.Gelu_apprx_tanh).then_inc(S["e_gel"], 1)
                    act.wait_ge(S[f"v_in{b}"], g * 16 + 16)
                    act.wait_ge(S["e_o"], g * DC + 1)
                    f_(vhl[par][0][:, b, :], vst[b], ACT.Copy).then_inc(S["v_hi"], 1)
                    if more and b % 2:
                        u_high(b // 2, g * 16 + 32, g * EB + (b + 1))

            act.wait_ge(S["dense_out0"], 64 * SC // 2)
            u_high(0, 16)
            u_high(1, 16)
            act.wait_ge(S["dense_out1"], 64 * SC // 2)
            with act.Fori(0, GROUPS // 2 - 1) as i:
                gelu_group(i * 2, 0)
                gelu_group(i * 2 + 1, 1)
            gelu_group(GROUPS - 2, 0)
            gelu_group(GROUPS - 1, 1, more=False)

        @block.vector
        def _(dve):
            n_step = 0

            def settle(ins):
                nonlocal n_step
                n_step += 1
                ins.then_inc(S["dve_step"], 1)
                dve.wait_ge(S["dve_step"], n_step)

            stt = dve.scalar_tensor_tensor

            def normed(k, width, src, weight, dst=None):
                dve.wait_ge(S["std_ready"], 2 * k + 2)
                settle(dve.reciprocal(rstd[:, 0, 0:width], rstd[:, 0, 0:width]))
                for c in range(DC):
                    stt((dst or uT)[:, c, 0:width], src[:, c, :], weight[:, c:c + 1], rstd[:, 0, 0:width],
                        ALU.mult, ALU.mult).then_inc(S["u_ready"], 1)

            dve.wait_ge(S["small_in"], 16 * SMALL)
            normed(0, T, hT, col_an)

            for f in range(12):
                dve.wait_ge(S["proj_taken"], f + 1)
                if f >= 2:
                    dve.wait_ge(S["qkv_ready"], f - 1)
                x, o = cin[:, f % 2, :], ctmp[:, f % 2, :]
                settle(dve.tensor_scalar(o, x[:, 0:T], col_conv[:, f, 0:1], None, ALU.mult))
                for k in range(1, CONV_K):
                    ins = stt(o, x[:, k:k + T], col_conv[:, f, k:k + 1], o, ALU.mult, ALU.add)
                    if k < CONV_K - 1:
                        settle(ins)
                ins.then_inc(S["conv_done"], 1)

            def head_scale(f, src, first, scale):
                dve.wait_ge(S["l2_std"], first + f + 1)
                settle(dve.reciprocal(rstd[:, f % 2, 0:T], rstd[:, f % 2, 0:T]))
                return stt(src[:, f, 0:T], src[:, f, 0:T], scale, rstd[:, f % 2, 0:T], ALU.mult, ALU.mult)

            for f in range(2 * GH):
                head_scale(f, qkvT, 0, GD ** -0.5 if f < GH else 1.0).then_inc(S["l2_done"], 1)

            dve.wait_ge(S["proj_taken"], 30)
            settle(dve.tensor_scalar(graw[0:NG, :], graw[0:NG, :], col_gb[0:NG, 0:1], None, ALU.add))
            stt(gabs[0:NG, :], graw[0:NG, :], -1.0, graw[0:NG, :], ALU.mult, ALU.max).then_inc(S["gate_y"], 2)
            dve.wait_ge(S["gate_act"], 3)
            stt(gabs[0:ROW_A, :], graw[0:ROW_A, :], 0.0, gln[0:ROW_A, :], ALU.min, ALU.subtract).then_inc(S["gate_y"], 1)
            settle(stt(gln[ROW_A:NG, :], graw[ROW_A:NG, :], 0.0, gln[ROW_A:NG, :], ALU.max, ALU.add))
            dve.tensor_scalar(gates[ROW_A:NG, 0:T], gln[ROW_A:NG, :], col_al[ROW_A:NG, 0:1], -1.0,
                              ALU.mult, ALU.mult).then_inc(S["gate_done"], 1)
            settle(dve.tensor_scalar(gln[0:FH, :], gabs[0:FH, :], 0.0, 1.0, ALU.mult, ALU.add))
            dve.wait_ge(S["gate_y"], 3)
            dve.tensor_tensor_scan(csum, gln[0:FH, :], gabs[0:FH, :], 0.0, ALU.mult, ALU.subtract).then_inc(S["x_csum"], 1)

            flat = lambda a: a.rearrange("p h t -> p (h t)")
            wide = lambda a: a.unsqueeze(1).to_broadcast([P, GH, P])
            per_head = lambda a: a.unsqueeze(2).to_broadcast([P, GH, P])
            dve.wait_ge(S["x_csum"], 1)
            dve.wait_ge(S["gate_tok"], NT)

            def delta(m, what):
                beta = gtok[:, m, ROW_B:ROW_B + GH]
                if what == "pre":
                    dve.wait_ge(S["g_pre"], m + 1)
                    dve.tensor_copy(E[:, :, :], wide(const("ident"))).then_inc(S["g_init"], 1)
                    dve.tensor_copy(Dm[:, :, :], wide(const("ident"))).then_inc(S["g_init"], 1)
                    dve.wait_ge(S["g_exp"], m * 4 + 1)
                    for h in range(GH):
                        stt(amat[:, h], psum[:, 3, h * P:(h + 1) * P], beta[:, h:h + 1], expD[:, h], ALU.mult,
                            ALU.mult).then_inc(S["g_amat"], 1)
                if what == "decay":
                    dve.wait_ge(S["g_exp"], m * 4 + 3)
                    dve.tensor_tensor(flat(qkT), psum[:, 4, :], flat(expT), ALU.mult).then_inc(S["g_prep"], 1)
                    dve.tensor_tensor(qs[:, :, :], qkvT[:, 0:GH, m * P:(m + 1) * P], egrow[:, :, :], ALU.mult
                                      ).then_inc(S["g_prep"], 1)
                    dve.wait_ge(S["g_exp"], m * 4 + 4)
                    dve.tensor_tensor(kdec[:, :, :], ktok[:, :, :], per_head(ecol[:, 4:8]), ALU.mult).then_inc(S["g_prep"], 1)
                    dve.wait_ge(S["g_prep"], m * 4 + 1)
                    dve.tensor_tensor(qkT[:, :, :], qkT[:, :, :], wide(const("upto")), ALU.mult).then_inc(S["g_prep"], 1)
                if isinstance(what, int):
                    n = m * LEVELS + what
                    dve.wait_ge(S["g_y"], n + 1)
                    if n:
                        dve.wait_ge(S["g_lv"], 2 * n)
                    dve.wait_ge(S["g_init"], m * 2 + 2)
                    dve.tensor_tensor(flat(E), flat(E), psum[:, 6, :], ALU.add).then_inc(S["g_lv"], 1)
                    dve.tensor_tensor(flat(Dm), flat(Dm), psum[:, 7, :], ALU.add).then_inc(S["g_lv"], 1)
                if what == "recall":
                    dve.wait_ge(S["g_ks"], m + 1)
                    dve.tensor_tensor(res[:, :, :], psum[:, 3, :].rearrange("p (h t) -> p h t", h=GH),
                                      per_head(ecol[:, 0:4]), ALU.mult).then_inc(S["g_res"], 1)
                    dve.wait_ge(S["g_res"], m * 2 + 1)
                    dve.tensor_tensor(flat(res), flat(vtok), flat(res), ALU.subtract).then_inc(S["g_res"], 1)
                    dve.wait_ge(S["g_res"], m * 2 + 2)
                    dve.tensor_tensor(res[:, :, :], res[:, :, :], per_head(beta), ALU.mult).then_inc(S["g_r"], 1)
                if what == "output":
                    dve.wait_ge(S["g_o"], m + 1)
                    for h in range(GH):
                        stt(state[:, h], state[:, h], ecol[:, 8 + h:9 + h], psum[:, 6, h * P:(h + 1) * P], ALU.mult,
                            ALU.add).then_inc(S["g_state"], 1)

            def attend_scores(s):
                h, m, rows, keys = fox(s)
                a = sc[0:rows, s % 3, 0:keys]
                col = mx[0:rows, s % 3:s % 3 + 1]
                dve.wait_ge(S["x_s"], s + 1)
                dve.wait_ge(S["x_cbc"], h + 1)
                if s >= 3:
                    dve.wait_ge(S["x_t"], s - 2)
                first = min(512, keys)
                settle(stt(a[:, 0:first], psum[0:rows, 0, 0:first], FD ** -0.5, cb[0:rows, h % 2, 0:first], ALU.mult, ALU.add))
                if keys > 512:
                    settle(stt(a[:, 512:keys], psum[0:rows, 1, 0:keys - 512], FD ** -0.5, cb[0:rows, h % 2, 512:keys],
                               ALU.mult, ALU.add))
                diag = a[:, m * P:keys]
                dve.tensor_tensor(diag, diag, const("causal")[0:rows, 0:rows], ALU.add).then_inc(S["x_sc"], 1)
                dve.wait_ge(S["x_sc"], s + 1)
                settle(dve.tensor_reduce(col, a, AX, ALU.max))
                dve.tensor_scalar(col, col, -1.0, None, ALU.mult).then_inc(S["x_max"], 1)

            def attend_norm(s):
                h, m, rows, keys = fox(s)
                a = sc[0:rows, s % 3, 0:keys]
                col = rs[0:rows, s % 3:s % 3 + 1]
                dve.wait_ge(S["x_exp"], s + 1)
                settle(dve.reciprocal(col, col))
                dve.tensor_scalar(a, a, col, None, ALU.mult).then_inc(S["x_nrm"], 1)

            def attend_out(s):
                h, m, rows, keys = fox(s)
                lo, hi = (h % 2) * FD, (h % 2) * FD + FD
                dve.wait_ge(S["x_o"], s + 1)
                dve.tensor_copy(mT[lo:hi, GH + h // 2, m * P:m * P + rows], psum[lo:hi, 2, 0:rows]).then_inc(S["x_oc"], 1)

            for m, what, s in slots():
                if s is not None:
                    if 0 <= s - 4 < STEPS:
                        attend_out(s - 4)
                    if s < STEPS:
                        attend_scores(s)
                if m is not None:
                    delta(m, what)
                if s is not None and 0 <= s - 1 < STEPS:
                    attend_norm(s - 1)

            o_all = qkvT[:, 2 * GH:3 * GH, :]
            for f in range(GH):
                settle(head_scale(f, o_all, 2 * GH, col_gn[:, 0:1]))
                dve.tensor_tensor(mT[:, f, :], o_all[:, f, 0:T], zT[:, f, :], ALU.mult).then_inc(S["l2_done"], 1)

            def residual(f, lane, ready, dst):
                dve.wait_ge(S["out_done"], ready)
                for j in range(2):
                    a = dst[:, j * HALF:(j + 1) * HALF]
                    ins = dve.tensor_tensor(a, a, psum[:, 2 * lane + j, 0:HALF], ALU.add)
                ins.then_inc(S["res_done"], 1)

            dve.wait_ge(S["mod_done"], MODS)
            settle(dve.tensor_tensor(mod[:, :], psum[:, 2, 256:256 + MODS], mod_b[:, :], ALU.add))
            dve.engine_nop().then_inc(S["mod_ready"], 1)
            for f in range(DC):
                residual(f, f % 2, f + 1, hT[:, f, :])
            normed(1, T, hT, col_fn)

            dve.engine_nop().then_inc(S["ffn_hid"], 2)
            with dve.Fori(0, FC // 2) as i:
                for k in range(2):
                    dve.wait_ge(S["ffn_sil"], i * 2 + k + 1)
                    for j in range(2):
                        ins = dve.tensor_tensor(hid[:, bass.ds(i * 2 + k, 1), j * HALF:(j + 1) * HALF].rearrange("p o t -> p (o t)"),
                                                sil[:, k, j * HALF:(j + 1) * HALF],
                                                psum[:, 4 + 2 * k + j, 0:HALF], ALU.mult)
                    ins.then_inc(S["ffn_hid"], 1)
            with dve.Fori(0, 4) as i:
                for k in range(2):
                    residual(0, k, i * 2 + DC + k + 1,
                             hT[:, bass.ds(i * 2 + k, 1), :].rearrange("p o t -> p (o t)"))

            dve.wait_ge(S["res_done"], 2 * DC)
            dve.wait_ge(S["std_ready"], 5)
            settle(dve.reciprocal(r2[:, 0, :], r2[:, 0, :]))
            for c in range(DC):
                stt(xT2[:, c, :], xT2[:, c, :], col_ln[:, c:c + 1], r2[:, 0, :], ALU.mult, ALU.mult).then_inc(S["x2_ready"], 1)

            def modulated(k, weight, scale):
                settle(stt(amp[:, k, :], mod[:, scale:scale + DC], 1.0, weight[:, :], ALU.add, ALU.mult))
                dve.wait_ge(S["std_ready"], 6 + k)
                settle(dve.reciprocal(r2[:, 0, :], r2[:, 0, :]))
                for c in range(DC):
                    stt(u2[:, c, :], xT2[:, c, :], amp[:, k, c:c + 1], r2[:, 0, :], ALU.mult, ALU.mult).then_inc(S["u_ready"], 1)

            dve.wait_ge(S["x2_ready"], DC)
            modulated(0, col_n1, DC)

            dve.wait_ge(S["posi_in"], 16)
            settle(dve.tensor_copy(angT, posi.bitcast(I32)))
            settle(dve.tensor_scalar(angT, angT, const("freq"), None, ALU.mult))
            parts, rest = [], TWO_PI
            for _ in range(2):
                m, e = np.frexp(rest)
                parts.append(float(np.round(m * 2048) / 2048 * 2.0 ** e))
                rest -= parts[-1]
            parts.append(rest)
            for dst, lead in ((sinT, 0.0), (cosT, 0.25)):
                settle(dve.tensor_scalar(kf, angT, 1.0 / TWO_PI, lead, ALU.mult, ALU.add))
                settle(dve.tensor_scalar(kf, kf, 1.5 * 2.0 ** 23, None, ALU.add))
                settle(dve.tensor_scalar(kf, kf, -1.5 * 2.0 ** 23, None, ALU.add))
                settle(stt(dst, kf, -parts[0], angT, ALU.mult, ALU.add))
                settle(stt(dst, kf, -parts[1], dst, ALU.mult, ALU.add))
                settle(stt(dst, kf, -parts[2], dst, ALU.mult, ALU.add))
                settle(dve.tensor_scalar(dst, dst, lead * TWO_PI, 3.1415925, ALU.add, ALU.min))
                settle(dve.tensor_scalar(dst, dst, -3.1415925, None, ALU.max))
            settle(dve.memset(prod[:, :, 0:CK2 - 1], 0.0))
            dve.engine_nop().then_inc(S["tab"], 1)

            def convolve(j, bank):
                f = 5 + SC + j
                dve.wait_ge(S["cv_cc"], j + 1)
                x = prod[:, j % 2, :]
                dve.tensor_tensor(x[:, CK2 - 1:], cc[:, j % 2, :], psum[:, bank, :], ALU.mult).then_inc(S["p2_taken"], 1)
                dve.wait_ge(S["p2_taken"], f + 1)
                y = y2[:, j, :]
                settle(dve.tensor_scalar(y, x[:, 0:SEC], col_cv2[:, j, 0:1], None, ALU.mult))
                settle(stt(y, x[:, 1:1 + SEC], col_cv2[:, j, 1:2], y, ALU.mult, ALU.add))
                settle(stt(y, x[:, 2:2 + SEC], col_cv2[:, j, 2:3], y, ALU.mult, ALU.add))

            for j in range(7):
                if j < 5:
                    dve.wait_ge(S["qk_std"], j + 1)
                    settle(dve.reciprocal(sq2[:, j % 2, :], sq2[:, j % 2, :]))
                    g = col_qk[:, 0:1] if j < 4 else col_qk[:, 1:2]
                    stt(qkr[:, j, :], qkr[:, j, :], g, sq2[:, j % 2, :], ALU.mult, ALU.mult).then_inc(S["qk_n"], 1)
                if 2 <= j:
                    r = j - 2
                    dve.wait_ge(S["qk_rot"], r + 1)
                    dve.wait_ge(S["tab_sin"], 2)
                    dve.tensor_tensor(tm2[:, j % 2, :], psum[:, 6 + j % 2, :], sinT, ALU.mult)
                    settle(dve.tensor_tensor(qkr[:, r, :], qkr[:, r, :], cosT, ALU.mult))
                    dve.tensor_tensor(qkr[:, r, :], qkr[:, r, :], tm2[:, j % 2, :], ALU.add).then_inc(S["qk_done"], 1)
                if j in (1, 3):
                    convolve(j // 2, 2 + (5 + SC + j // 2) % 2)

            def window_out(s):
                n, kv = divmod(s, KV)
                lo, hi = kv * AD, (kv + 1) * AD
                dve.wait_ge(S["a_o"], s + 1)
                dve.tensor_copy(mix[lo:hi, 0:PER, n * P:(n + 1) * P],
                                psum[lo:hi, 4 + kv, :].rearrange("p (i q) -> p i q", i=PER)).then_inc(S["a_oc"], 1)

            def conv_step(s):
                if s in (1, 3):
                    convolve(2 + s // 2, 7)
                if s >= 4:
                    f = 5 + SC + s
                    dve.wait_ge(S["p2_ready"], f + 1)
                    dve.tensor_tensor(mix[:, s, :], psum[:, 6 + s % 2, :], y2[:, s - 4, :], ALU.mult).then_inc(S["p2_taken"], 1)

            for s in range(SC * KV):
                n, kv = divmod(s, KV)
                k0 = P if n == 0 else 0
                w = 2 * P - k0
                mine = sink[:, kv * PER:(kv + 1) * PER]
                if s:
                    dve.wait_ge(S["a_t"], s)
                dve.wait_ge(S["a_s"], s + 1)
                two = psum[:, 0:2, :].rearrange("p b (i k) -> p (b i) k", i=2)[:, :, k0:]
                mask = const("window")[:, k0:].unsqueeze(1).to_broadcast([P, PER, w])
                dve.tensor_tensor(ex[:, :, k0:], two, mask, ALU.add).then_inc(S["a_sc"], 1)
                dve.wait_ge(S["a_sc"], s + 1)
                settle(dve.tensor_reduce(mxs[:, :], ex[:, :, k0:], AX, ALU.max))
                settle(stt(mxs[:, :], mxs[:, :], AD ** -0.5, mine, ALU.mult, ALU.max))
                dve.tensor_scalar(nms[:, :], mxs[:, :], -1.0, None, ALU.mult).then_inc(S["a_exp"], 1)
                dve.tensor_tensor(ess[:, :], mine, mxs[:, :], ALU.subtract).then_inc(S["a_exp"], 1)
                if s:
                    window_out(s - 1)
                    conv_step(s - 1)
                dve.wait_ge(S["a_e"], s + 1)
                settle(dve.tensor_tensor(rss[:, :], rss[:, :], ess[:, :], ALU.add))
                settle(dve.reciprocal(rss[:, :], rss[:, :]))
                dve.tensor_tensor(ex[:, :, k0:], ex[:, :, k0:], rss[:, :].unsqueeze(2).to_broadcast([P, PER, w]),
                                  ALU.mult).then_inc(S["a_p"], 1)
            window_out(SC * KV - 1)
            conv_step(SC * KV - 1)
            dve.wait_ge(S["p2_taken"], 5 + SC + 8)
            dve.engine_nop().then_inc(S["mix_cv"], 4)

            for g in range(2):
                dve.wait_ge(S["m_std"], g + 1)
                settle(dve.reciprocal(r2[:, g, :], r2[:, g, :]))
                for c in range(4 * g, 4 * g + 4):
                    stt(mix[:, c, :], mix[:, c, :], col_mix[:, c:c + 1], r2[:, g, :], ALU.mult, ALU.mult).then_inc(S["m_done"], 1)
            for f in range(DC):
                dve.wait_ge(S["out2_done"], f + 1)
                stt(xT2[:, f, :], psum[:, f % 2, :], mod[:, 2 * DC + f:2 * DC + f + 1], xT2[:, f, :], ALU.mult,
                    ALU.add).then_inc(S["res2_done"], 1)
            modulated(1, col_n2, 4 * DC)
            for c in range(DC):
                dve.wait_ge(S["h2_hi"], c + 1)
                dve.tensor_tensor(h2lo[:, c, :], u2[:, c, :], h2hi[:, c, :], ALU.subtract).then_inc(S["h2_split"], 1)

            STAGES = 10
            with dve.Fori(0, PH) as h:
                units = [(p, t) for p in range(2) for t in range(SC)]

                def hold(name, value, k):
                    dve.wait_ge(S[name], value)
                    dve.memset(gate_dve[:, k:k + 1], 0.0)

                done = lambda n: hold("tk", h * STAGES + n, n) if n < 7 else dve.wait_ge(S["tk"], h * STAGES + n)
                hold("sc_taken", h * 2 + 2, 0)
                for p, t in units:
                    ins = dve.max(val[:, p, t, 0:8], scb[:, p, t, :])
                ins.then_inc(S["tk"], 1)
                done(1)
                for p, t in units:
                    dve.max_index(idu[:, p, t, 0:8].bitcast(U32), val[:, p, t, 0:8], scb[:, p, t, :])
                for p, t in units:
                    ins = dve.match_replace(scr[:, p, t, :], val[:, p, t, 0:8], scb[:, p, t, :], LOW)
                ins.then_inc(S["tk_free"], 1)
                hold("tk_free", h + 1, 7)
                for p, t in units:
                    ins = dve.max(val[:, p, t, 8:16], scr[:, p, t, :])
                ins.then_inc(S["tk"], 1)
                done(2)
                for p, t in units:
                    dve.max_index(idu[:, p, t, 8:16].bitcast(U32), val[:, p, t, 8:16], scr[:, p, t, :])
                ins = dve.tensor_tensor(cand[:, :, :].rearrange("p t (a b) -> p t a b", a=TOP),
                                        val[:, 0].unsqueeze(3).to_broadcast([P, SC, TOP, TOP]),
                                        val[:, 1].unsqueeze(2).to_broadcast([P, SC, TOP, TOP]), ALU.add)
                ins.then_inc(S["tk"], 1)
                done(3)
                for t in range(SC):
                    ins = dve.max(best[:, t, 0:8], cand[:, t, :])
                ins.then_inc(S["tk"], 1)
                done(4)
                for t in range(SC):
                    dve.max_index(posu[:, t, 0:8].bitcast(U32), best[:, t, 0:8], cand[:, t, :])
                for t in range(SC):
                    ins = dve.match_replace(cand2[:, t, :], best[:, t, 0:8], cand[:, t, :], LOW)
                ins.then_inc(S["tk"], 1)
                done(5)
                for t in range(SC):
                    ins = dve.max(best[:, t, 8:16], cand2[:, t, :])
                ins.then_inc(S["tk"], 1)
                done(6)
                for t in range(SC):
                    dve.max_index(posu[:, t, 8:16].bitcast(U32), best[:, t, 8:16], cand2[:, t, :])
                dve.tensor_tensor(ebest[:, :, :], best[:, :, :], best[:, :, 0:1].to_broadcast([P, SC, TOP]),
                                  ALU.subtract).then_inc(S["tk_top"], 1)
                dve.wait_ge(S["tk_top"], h + 1)
                pu = posu[:, :, :].rearrange("p a b -> p (a b)").bitcast(U32)
                ph, pl = (a[:, :, :].rearrange("p a b -> p (a b)") for a in (posh, posl))
                dve.tensor_single_scalar(ph.bitcast(U32), pu, 4, ALU.logical_shift_right)
                dve.tensor_single_scalar(pl.bitcast(U32), pu, 15, ALU.bitwise_and).then_inc(S["tk"], 1)
                done(7)
                dve.tensor_copy(ph, ph.bitcast(U32))
                dve.tensor_copy(pl, pl.bitcast(U32))
                dve.tensor_copy(idf[:, :, :, :].rearrange("p a b c -> p (a b c)"),
                                idu[:, :, :, :].rearrange("p a b c -> p (a b c)").bitcast(U32)).then_inc(S["tk"], 1)
                done(8)
                io16 = const("iota")[:, 0:TOP].unsqueeze(1).to_broadcast([P, SC * TOP, TOP])
                for p, pos in enumerate((ph, pl)):
                    dve.tensor_tensor(eq[:, p], io16, pos.unsqueeze(2).to_broadcast([P, SC * TOP, TOP]),
                                      ALU.is_equal).then_inc(S["tk_pos"], 1)
                dve.wait_ge(S["tk_exp"], h + 1)
                dve.tensor_reduce(esum[:, :], ebest[:, :, :], AX, ALU.add).then_inc(S["tk"], 1)
                done(9)
                dve.reciprocal(esum[:, :], esum[:, :]).then_inc(S["tk"], 1)
                done(10)
                dve.tensor_tensor(tok[:, 0, :, bass.ds(h * TOP, TOP)], ebest[:, :, :],
                                  esum[:, :].unsqueeze(2).to_broadcast([P, SC, TOP]), ALU.mult).then_inc(S["tk_gate"], 1)
                for p in range(2):
                    dve.wait_ge(S["tk_eq"], h * 2 + 1 + p)
                    dve.tensor_reduce(tok[:, 1 + p, :, bass.ds(h * TOP, TOP)],
                                      eq[:, p].rearrange("p (a b) k -> p a b k", a=SC), AX, ALU.add).then_inc(S["tk_sel"], 1)

            dve.wait_ge(S["gij_in"], 3)
            for t in range(SC):
                with dve.Fori(0, 32 // RING) as i:
                    for k in range(RING):
                        dve.wait_ge(S["dense_mm"], i * RING + (32 * t + k + 1))
                        for hot, a, sig in ((hotA, 1, "hot_i"), (hotB, 2, "hot_j")):
                            col = gij[:, a, bass.ds(i * (4 * RING) + (P * t + 4 * k), 4)]
                            dve.tensor_tensor(hot[:, k].rearrange("p (q i) -> p q i", q=4),
                                              const("iota").unsqueeze(1).to_broadcast([P, 4, P]),
                                              col.unsqueeze(2).to_broadcast([P, 4, P]), ALU.is_equal).then_inc(S[sig], 1)

            def u_low(k, hi):
                dve.wait_ge(S["u_hi"], hi)
                dve.tensor_tensor(uhl[k][1][:, :, :], ust[k][:, :, :], uhl[k][0][:, :, :], ALU.subtract).then_inc(S["u_lo"], 1)

            def gated(g, par, more=True):
                for b in range(EB):
                    dve.wait_ge(S["e_gel"], g * EB + (b + 1))
                    dve.wait_ge(S[f"g_in{b}"], g * 16 + 16)
                    dve.tensor_tensor(wf[b % 2], gel[b % 2], gst[b], ALU.mult).then_inc(S["e_w"], 1)
                    dve.wait_ge(S["e_o"], g * DC + 1)
                    dve.wait_ge(S["e_w"], g * (3 * EB) + (3 * b + 7))
                    dve.tensor_copy(whl[par][0][:, b, :], wf[b % 2]).then_inc(S["e_w"], 1)
                    dve.wait_ge(S["e_w"], g * (3 * EB) + (3 * b + 8))
                    dve.tensor_tensor(whl[par][1][:, b, :], wf[b % 2], whl[par][0][:, b, :], ALU.subtract).then_inc(S["e_w"], 1)
                    if more and b % 2:
                        u_low(b // 2, g * 2 + (2 + b // 2 + 1))

            def gather(g):
                for f in range(DC):
                    dve.wait_ge(S["e_o"], g * DC + (DC + f + 2))
                    dve.wait_ge(S["e_acc"], g * DC + 2)
                    dve.tensor_tensor(acc[:, f, :], acc[:, f, :], psum[:, 2 + f % 2, :], ALU.add).then_inc(S["e_acc"], 1)

            dve.wait_ge(S["acc_zero"], 1)
            u_low(0, 1)
            u_low(1, 2)
            gated(0, 0)
            with dve.Fori(0, GROUPS // 2 - 1) as i:
                gated(i * 2 + 1, 1)
                gather(i * 2)
                gated(i * 2 + 2, 0)
                gather(i * 2 + 1)
            gated(GROUPS - 1, 1, more=False)
            gather(GROUPS - 2)
            gather(GROUPS - 1)
            dve.wait_ge(S["e_acc"], GROUPS * DC + 2)
            for c in range(DC):
                stt(acc[:, c, :], acc[:, c, :], mod[:, 5 * DC + c:5 * DC + c + 1], xT2[:, c, :], ALU.mult,
                    ALU.add).then_inc(S["stored"], 1)


def kernel(**inputs):
    import numpy as _np
    import concourse.bacc as _bacc
    from concourse import mybir as _mybir
    from concourse.bass_utils import run_bass_kernel_spmd as _run

    a = {k: _np.asarray(v) for k, v in inputs.items()}
    heads = lambda x, axis: _np.moveaxis(
        _np.moveaxis(x, axis, 0).reshape((KV, PER, AD) + _np.moveaxis(x, axis, 0).shape[1:]).swapaxes(0, 1).reshape(
            _np.moveaxis(x, axis, 0).shape), 0, axis)
    w_in2 = a["w_in_2"][0]
    w_out2 = a["w_out_2"][0]
    aw = AH * AD
    packed = {
        "consts": _np.concatenate(list(constants().values()), axis=1).astype(_np.float32),
        "xT": a["x"][0].T, "metaT": a["meta_tokens"].T,
        "attn_norm_w": a["attn_norm_w"][0], "ffn_norm_w": a["ffn_norm_w"][0], "final_norm_w": a["final_norm_w"],
        "conv_w": a["conv_w"][0], "gdn_norm_w": a["gdn_norm_w"][0], "fgate_b": a["fgate_b"][0],
        "dt_bias": a["dt_bias"][0], "a_log": a["a_log"][0], "w_in": a["w_in"][0], "w_out": a["w_out"][0],
        "w_gate": a["w_gate"][0], "w_up": a["w_up"][0], "w_down": a["w_down"][0],
        "c": a["c_2"][0], "positions": a["positions_2"][0], "ada_w": a["ada_w_2"][0], "ada_b": a["ada_b_2"][0],
        "norm1_g": a["norm1_g_2"][0], "norm2_g": a["norm2_g_2"][0],
        "w_in2": _np.concatenate([heads(w_in2[:, :aw], 1), w_in2[:, aw:]], axis=1),
        "q_norm_g": a["q_norm_g_2"][0], "k_norm_g": a["k_norm_g_2"][0], "sinks": a["sinks_2"][0],
        "conv_w2": a["conv_w_2"][0],
        "mix_g": _np.concatenate([heads(a["attn_out_g_2"][0], 0), a["conv_out_g_2"][0]]),
        "w_out2": _np.concatenate([heads(w_out2[:aw], 0), w_out2[aw:]], axis=0),
        "wq": a["peer_wq_2"][0],
        "subk": a["peer_subkeys_2"][0].reshape(2 * PH, PK, P).transpose(0, 2, 1),
        "uT": a["peer_u_2"][0].T, "v": a["peer_v_2"][0],
    }
    nc = _bacc.Bacc("TRN2", target_bir_lowering=False, num_devices=1)
    arrays, io = {}, {}
    for name, x in packed.items():
        x = _np.ascontiguousarray(x)
        arrays[f"in_{name}"] = x
        io[name] = nc.dram_tensor(f"in_{name}", x.shape, _mybir.dt.from_np(x.dtype), kind="ExternalInput").ap()
    io["dense"] = nc.dram_tensor("dense_gates", (PK, P, SEC), F32, kind="Internal").ap()
    io["out"] = nc.dram_tensor("out_dram", (D, SEC), F32, kind="ExternalOutput").ap()
    program(nc, io)
    r = _run(nc, [arrays], core_ids=[0])
    return _np.ascontiguousarray(r.results[0]["out_dram"].T)[None]
```
